# Optimizing a Trainium2 kernel written in Bass

```python
import math
import jax
import jax.numpy as jnp
from jax import lax
import numpy as np

D_MODEL = 1024
BATCH = 1
SEQ = 512
DEPTH = 2
DEC_BATCH = 8
DEC_SEQ = 1
PAST_LEN = 256
PAGE_SIZE = 128

N_SSD_LAYERS = DEPTH // 2
N_ATTN_LAYERS = DEPTH - N_SSD_LAYERS

SSD_EXPAND = 2
SSD_D_INNER = SSD_EXPAND * D_MODEL
SSD_HEAD_DIM = 64
SSD_N_HEADS = SSD_D_INNER // SSD_HEAD_DIM
SSD_N_GROUPS = 4
SSD_HEADS_PER_GROUP = SSD_N_HEADS // SSD_N_GROUPS
SSD_D_STATE = 128
SSD_D_CONV = 4
SSD_CHUNK = 128
SSD_GN = SSD_N_GROUPS * SSD_D_STATE
SSD_CONV_DIM = SSD_D_INNER + 2 * SSD_GN
SSD_IN_DIM = SSD_D_INNER + SSD_CONV_DIM + SSD_N_HEADS

ATTN_N_HEADS = 8
ATTN_HEAD_DIM = D_MODEL // ATTN_N_HEADS // 2
ATTN_V_DIM = 2 * ATTN_HEAD_DIM
ATTN_QK_DIM = ATTN_N_HEADS * 2 * ATTN_HEAD_DIM
ATTN_VO_DIM = ATTN_N_HEADS * ATTN_V_DIM
ROT_DIM = ATTN_HEAD_DIM // 4
ROPE_THETA = 500000.0
Q_BLOCK = 128

D_FF = 4 * D_MODEL
RMS_EPS = 1e-6

kernel_name = 'yoco_mamba2_diffattn_decode_step'

def rmsnorm(x, g):
    xf = x.astype(jnp.float32)
    y = xf * lax.rsqrt(jnp.mean(xf * xf, axis=-1, keepdims=True) + RMS_EPS)
    return (y * g.astype(jnp.float32)).astype(x.dtype)

def squared_relu_mlp(x, w_up, w_down):
    h = jax.nn.relu(x @ w_up)
    return (h * h) @ w_down

def ssd_in_proj(xn, w_in):
    zxbcdt = xn @ w_in
    z = zxbcdt[..., :SSD_D_INNER]
    xbc = zxbcdt[..., SSD_D_INNER:SSD_D_INNER + SSD_CONV_DIM]
    dt_raw = zxbcdt[..., SSD_D_INNER + SSD_CONV_DIM:]
    return z, xbc, dt_raw

def causal_dwconv(xbc, buf, w, b):
    length = xbc.shape[1]
    xpad = jnp.concatenate([buf.astype(xbc.dtype), xbc], axis=1)
    acc = b + xpad[:, 0:length] * w[0]
    for k in range(1, SSD_D_CONV):
        acc = acc + xpad[:, k:k + length] * w[k]
    return jax.nn.silu(acc), xpad[:, -(SSD_D_CONV - 1):]

def split_xbc(xbc):
    bsz, length = xbc.shape[:2]
    x = xbc[..., :SSD_D_INNER].reshape(bsz, length, SSD_N_HEADS, SSD_HEAD_DIM)
    b_in = xbc[..., SSD_D_INNER:SSD_D_INNER + SSD_GN].reshape(bsz, length, SSD_N_GROUPS, SSD_D_STATE)
    c_in = xbc[..., SSD_D_INNER + SSD_GN:].reshape(bsz, length, SSD_N_GROUPS, SSD_D_STATE)
    return x, b_in, c_in

def ssd_chunked(x, dt, a, b_in, c_in):
    bsz, seqlen = x.shape[:2]
    nc = seqlen // SSD_CHUNK
    G, R, P, N, L = SSD_N_GROUPS, SSD_HEADS_PER_GROUP, SSD_HEAD_DIM, SSD_D_STATE, SSD_CHUNK
    xg = (x.astype(jnp.float32) * dt[..., None]).reshape(bsz, nc, L, G, R, P)
    adt = jnp.moveaxis((a * dt).reshape(bsz, nc, L, G, R), 2, -1)
    a_cum = jnp.cumsum(adt, axis=-1)
    bc = b_in.astype(jnp.float32).reshape(bsz, nc, L, G, N)
    cc = c_in.astype(jnp.float32).reshape(bsz, nc, L, G, N)
    causal = jnp.tril(jnp.ones((L, L), dtype=bool))
    seg = a_cum[..., :, None] - a_cum[..., None, :]
    decay = jnp.exp(jnp.where(causal, seg, -jnp.inf))
    cb = jnp.einsum('bclgn,bcsgn->bcgls', cc, bc)
    y_diag = jnp.einsum('bcgls,bcgrls,bcsgrp->bclgrp', cb, decay, xg)
    decay_end = jnp.exp(a_cum[..., -1:] - a_cum)
    states = jnp.einsum('bcsgn,bcgrs,bcsgrp->bcgrpn', bc, decay_end, xg)
    chunk_decay = jnp.exp(a_cum[..., -1])

    def pass_state(h, inp):
        st, dec = inp
        return h * dec[..., None, None] + st, h

    h0 = jnp.zeros((bsz, G, R, P, N), jnp.float32)
    h_final, h_prev = lax.scan(pass_state, h0, (jnp.moveaxis(states, 1, 0), jnp.moveaxis(chunk_decay, 1, 0)))
    h_prev = jnp.moveaxis(h_prev, 0, 1)
    y_off = jnp.einsum('bclgn,bcgrpn,bcgrl->bclgrp', cc, h_prev, jnp.exp(a_cum))
    y = (y_diag + y_off).reshape(bsz, seqlen, SSD_N_HEADS, SSD_HEAD_DIM)
    return y, h_final.reshape(bsz, SSD_N_HEADS, SSD_HEAD_DIM, SSD_D_STATE)

def ssd_scan_tokens(x, dt, a, b_in, c_in, h0):
    bsz = x.shape[0]
    G, R, P, N = SSD_N_GROUPS, SSD_HEADS_PER_GROUP, SSD_HEAD_DIM, SSD_D_STATE
    a_gr = a.reshape(G, R)

    def step(h, inp):
        xt, dtt, bt, ct = inp
        xt = xt.astype(jnp.float32).reshape(bsz, G, R, P)
        dtt = dtt.reshape(bsz, G, R)
        h = h * jnp.exp(a_gr * dtt)[..., None, None] + jnp.einsum('bgrp,bgn->bgrpn', xt * dtt[..., None], bt.astype(jnp.float32))
        yt = jnp.einsum('bgrpn,bgn->bgrp', h, ct.astype(jnp.float32))
        return h, yt.reshape(bsz, SSD_N_HEADS, P)

    h_init = h0.astype(jnp.float32).reshape(bsz, G, R, P, N)
    xs = (jnp.moveaxis(x, 1, 0), jnp.moveaxis(dt, 1, 0), jnp.moveaxis(b_in, 1, 0), jnp.moveaxis(c_in, 1, 0))
    h_last, ys = lax.scan(step, h_init, xs)
    return jnp.moveaxis(ys, 0, 1), h_last.reshape(bsz, SSD_N_HEADS, P, N)

def ssd_out(y, x, z, d, gate_norm, w_out, dtype):
    bsz, length = y.shape[:2]
    y = y + x.astype(jnp.float32) * d.astype(jnp.float32)[:, None]
    g = y.reshape(bsz, length, SSD_D_INNER) * jax.nn.silu(z.astype(jnp.float32))
    g = g.reshape(bsz, length, SSD_N_GROUPS, SSD_D_INNER // SSD_N_GROUPS)
    g = g * lax.rsqrt(jnp.mean(g * g, axis=-1, keepdims=True) + RMS_EPS)
    g = g.reshape(bsz, length, SSD_D_INNER) * gate_norm.astype(jnp.float32)
    return g.astype(dtype) @ w_out

def ssd_dt_a(dt_raw, dt_bias, a_log):
    dt = jax.nn.softplus(dt_raw.astype(jnp.float32) + dt_bias.astype(jnp.float32))
    a = -jnp.exp(a_log.astype(jnp.float32))
    return dt, a

def ssd_mixer_prompt(xn, w_in, conv_w, conv_b, dt_bias, a_log, d, gate_norm, w_out):
    z, xbc, dt_raw = ssd_in_proj(xn, w_in)
    buf0 = jnp.zeros((xn.shape[0], SSD_D_CONV - 1, SSD_CONV_DIM), xn.dtype)
    xbc, conv_state = causal_dwconv(xbc, buf0, conv_w, conv_b)
    x, b_in, c_in = split_xbc(xbc)
    dt, a = ssd_dt_a(dt_raw, dt_bias, a_log)
    y, ssm_state = ssd_chunked(x, dt, a, b_in, c_in)
    return ssd_out(y, x, z, d, gate_norm, w_out, xn.dtype), ssm_state, conv_state

def ssd_mixer_sample(xn, ssm0, conv0, w_in, conv_w, conv_b, dt_bias, a_log, d, gate_norm, w_out):
    z, xbc, dt_raw = ssd_in_proj(xn, w_in)
    xbc, conv_state = causal_dwconv(xbc, conv0, conv_w, conv_b)
    x, b_in, c_in = split_xbc(xbc)
    dt, a = ssd_dt_a(dt_raw, dt_bias, a_log)
    y, ssm_state = ssd_scan_tokens(x, dt, a, b_in, c_in, ssm0)
    out = ssd_out(y, x, z, d, gate_norm, w_out, xn.dtype)
    return out, ssm_state.astype(ssm0.dtype), conv_state.astype(conv0.dtype)

def rope_partial(t, pos):
    half = ROT_DIM // 2
    inv = ROPE_THETA ** (-jnp.arange(0, ROT_DIM, 2, dtype=jnp.float32) / ROT_DIM)
    ang = pos.astype(jnp.float32)[:, None] * inv[None, :]
    cos = jnp.cos(ang)[:, None, None, :]
    sin = jnp.sin(ang)[:, None, None, :]
    rot = t[..., :ROT_DIM].astype(jnp.float32)
    r1, r2 = rot[..., :half], rot[..., half:]
    rot = jnp.concatenate([r1 * cos - r2 * sin, r2 * cos + r1 * sin], axis=-1)
    return jnp.concatenate([rot.astype(t.dtype), t[..., ROT_DIM:]], axis=-1)

def shared_kv(h, kv_norm, w_kv, pos):
    bsz, length = h.shape[:2]
    kv = rmsnorm(h, kv_norm) @ w_kv
    k = kv[..., :ATTN_QK_DIM].reshape(bsz, length, ATTN_N_HEADS, 2, ATTN_HEAD_DIM)
    v = kv[..., ATTN_QK_DIM:].reshape(bsz, length, ATTN_N_HEADS, ATTN_V_DIM)
    return rope_partial(k, pos), v

def diff_query(xn, w_q, pos):
    bsz, length = xn.shape[:2]
    q = (xn @ w_q).reshape(bsz, length, ATTN_N_HEADS, 2, ATTN_HEAD_DIM)
    return rope_partial(q, pos)

def diff_lambda(lq1, lk1, lq2, lk2, lam_init):
    f = jnp.float32
    return (jnp.exp(jnp.sum(lq1.astype(f) * lk1.astype(f))) - jnp.exp(jnp.sum(lq2.astype(f) * lk2.astype(f))) + lam_init)

def diff_attn_prompt(q, k, v, lam):
    bsz, seqlen = q.shape[:2]
    nb = seqlen // Q_BLOCK
    scale = ATTN_HEAD_DIM ** -0.5
    qb = jnp.moveaxis(q.reshape(bsz, nb, Q_BLOCK, ATTN_N_HEADS, 2, ATTN_HEAD_DIM), 1, 0)
    kpos = jnp.arange(seqlen)

    def one_block(args):
        qi, blk = args
        qpos = blk * Q_BLOCK + jnp.arange(Q_BLOCK)
        s = jnp.einsum('bqhjd,bkhjd->bhjqk', qi, k).astype(jnp.float32) * scale
        s = jnp.where((kpos[None, :] <= qpos[:, None]), s, -jnp.inf)
        p = jax.nn.softmax(s, axis=-1)
        att = p[:, :, 0] - lam * p[:, :, 1]
        return jnp.einsum('bhqk,bkhe->bqhe', att.astype(v.dtype), v)

    o = lax.map(one_block, (qb, jnp.arange(nb)))
    return jnp.moveaxis(o, 0, 1).reshape(bsz, seqlen, ATTN_N_HEADS, ATTN_V_DIM)

def diff_attn_sample(q, k_past, v_past, k_new, v_new, lam):
    t_new = q.shape[1]
    past = k_past.shape[1]
    scale = ATTN_HEAD_DIM ** -0.5
    s_past = jnp.einsum('bqhjd,bkhjd->bhjqk', q, k_past).astype(jnp.float32) * scale
    s_new = jnp.einsum('bqhjd,bkhjd->bhjqk', q, k_new).astype(jnp.float32) * scale
    s_new = jnp.where(jnp.tril(jnp.ones((t_new, t_new), dtype=bool)), s_new, -jnp.inf)
    p = jax.nn.softmax(jnp.concatenate([s_past, s_new], axis=-1), axis=-1)
    att = (p[:, :, 0] - lam * p[:, :, 1]).astype(v_new.dtype)
    return (jnp.einsum('bhqk,bkhe->bqhe', att[..., :past], v_past) + jnp.einsum('bhqk,bkhe->bqhe', att[..., past:], v_new))

def diff_out(o, lam_init, subln, w_o):
    bsz, length = o.shape[:2]
    o = rmsnorm(o, subln) * (1.0 - lam_init)
    return o.reshape(bsz, length, ATTN_VO_DIM) @ w_o

def setup_inputs(seed: int = 0) -> dict:
    key = jax.random.key(seed)
    ks = jax.random.split(key, 40)
    f32 = jnp.float32
    n_pages = PAST_LEN // PAGE_SIZE
    n_used = DEC_BATCH * n_pages
    n_phys = n_used + max(1, n_used // 4)

    def nrm(k, shape, scale):
        return jax.random.normal(k, shape, f32) * scale

    def gain(k, shape):
        return 1.0 + 0.02 * jax.random.normal(k, shape, f32)

    dt0 = jnp.exp(jax.random.uniform(ks[10], (N_SSD_LAYERS, SSD_N_HEADS), f32) * (math.log(0.1) - math.log(0.001)) + math.log(0.001))
    dt_bias = dt0 + jnp.log(-jnp.expm1(-dt0))
    a_log = jnp.log(jax.random.uniform(ks[11], (N_SSD_LAYERS, SSD_N_HEADS), f32, 1.0, 16.0))
    page_table = jax.random.permutation(ks[6], n_phys)[:n_used].reshape(DEC_BATCH, n_pages).astype(jnp.int32)
    return {
        'x_prompt': nrm(ks[0], (BATCH, SEQ, D_MODEL), 1.0),
        'x_sample': nrm(ks[1], (DEC_BATCH, DEC_SEQ, D_MODEL), 1.0),
        'state_ssm': nrm(ks[2], (N_SSD_LAYERS, DEC_BATCH, SSD_N_HEADS, SSD_HEAD_DIM, SSD_D_STATE), 0.1),
        'state_conv': nrm(ks[3], (N_SSD_LAYERS, DEC_BATCH, SSD_D_CONV - 1, SSD_CONV_DIM), 1.0),
        'cache_k': nrm(ks[4], (n_phys, PAGE_SIZE, ATTN_N_HEADS, 2 * ATTN_HEAD_DIM), 1.0),
        'cache_v': nrm(ks[5], (n_phys, PAGE_SIZE, ATTN_N_HEADS, ATTN_V_DIM), 1.0),
        'page_table': page_table,
        'ssd_norm_pre': gain(ks[7], (N_SSD_LAYERS, D_MODEL)),
        'ssd_norm_post': gain(ks[8], (N_SSD_LAYERS, D_MODEL)),
        'ssd_w_in': nrm(ks[9], (N_SSD_LAYERS, D_MODEL, SSD_IN_DIM), D_MODEL ** -0.5),
        'ssd_conv_w': nrm(ks[12], (N_SSD_LAYERS, SSD_D_CONV, SSD_CONV_DIM), SSD_D_CONV ** -0.5),
        'ssd_conv_b': nrm(ks[13], (N_SSD_LAYERS, SSD_CONV_DIM), 0.02),
        'ssd_dt_bias': dt_bias,
        'ssd_a_log': a_log,
        'ssd_d': gain(ks[14], (N_SSD_LAYERS, SSD_N_HEADS)),
        'ssd_gate_norm': gain(ks[15], (N_SSD_LAYERS, SSD_D_INNER)),
        'ssd_w_out': nrm(ks[16], (N_SSD_LAYERS, SSD_D_INNER, D_MODEL), SSD_D_INNER ** -0.5),
        'mlp_norm_pre': gain(ks[17], (DEPTH, D_MODEL)),
        'mlp_norm_post': gain(ks[18], (DEPTH, D_MODEL)),
        'mlp_w_up': nrm(ks[19], (DEPTH, D_MODEL, D_FF), D_MODEL ** -0.5),
        'mlp_w_down': nrm(ks[20], (DEPTH, D_FF, D_MODEL), D_FF ** -0.5),
        'kv_norm': gain(ks[21], (D_MODEL,)),
        'w_kv': nrm(ks[22], (D_MODEL, ATTN_QK_DIM + ATTN_VO_DIM), D_MODEL ** -0.5),
        'attn_norm_pre': gain(ks[23], (N_ATTN_LAYERS, D_MODEL)),
        'attn_norm_post': gain(ks[24], (N_ATTN_LAYERS, D_MODEL)),
        'attn_w_q': nrm(ks[25], (N_ATTN_LAYERS, D_MODEL, ATTN_QK_DIM), D_MODEL ** -0.5),
        'attn_lambda_q1': nrm(ks[26], (N_ATTN_LAYERS, ATTN_HEAD_DIM), 0.1),
        'attn_lambda_k1': nrm(ks[27], (N_ATTN_LAYERS, ATTN_HEAD_DIM), 0.1),
        'attn_lambda_q2': nrm(ks[28], (N_ATTN_LAYERS, ATTN_HEAD_DIM), 0.1),
        'attn_lambda_k2': nrm(ks[29], (N_ATTN_LAYERS, ATTN_HEAD_DIM), 0.1),
        'attn_subln': gain(ks[30], (N_ATTN_LAYERS, ATTN_V_DIM)),
        'attn_w_o': nrm(ks[31], (N_ATTN_LAYERS, ATTN_VO_DIM, D_MODEL), ATTN_VO_DIM ** -0.5),
    }

def reference(x_prompt, x_sample, state_ssm, state_conv, cache_k, cache_v, page_table,
              ssd_norm_pre, ssd_norm_post, ssd_w_in, ssd_conv_w, ssd_conv_b, ssd_dt_bias, ssd_a_log,
              ssd_d, ssd_gate_norm, ssd_w_out, mlp_norm_pre, mlp_norm_post, mlp_w_up, mlp_w_down,
              kv_norm, w_kv, attn_norm_pre, attn_norm_post, attn_w_q, attn_lambda_q1, attn_lambda_k1,
              attn_lambda_q2, attn_lambda_k2, attn_subln, attn_w_o):
    pos_p = jnp.arange(x_prompt.shape[1])
    pos_s = PAST_LEN + jnp.arange(x_sample.shape[1])
    hp, hs = x_prompt, x_sample
    ssm_p, conv_p, ssm_s, conv_s = [], [], [], []
    k_p = v_p = k_s = v_s = k_past = v_past = None
    for i in range(DEPTH):
        if i < N_SSD_LAYERS:
            j = i
            w = (ssd_w_in[j], ssd_conv_w[j], ssd_conv_b[j], ssd_dt_bias[j], ssd_a_log[j], ssd_d[j], ssd_gate_norm[j], ssd_w_out[j])
            yp, sp, cp = ssd_mixer_prompt(rmsnorm(hp, ssd_norm_pre[j]), *w)
            ys, ss, cs = ssd_mixer_sample(rmsnorm(hs, ssd_norm_pre[j]), state_ssm[j], state_conv[j], *w)
            hp = hp + rmsnorm(yp, ssd_norm_post[j])
            hs = hs + rmsnorm(ys, ssd_norm_post[j])
            ssm_p.append(sp)
            conv_p.append(cp)
            ssm_s.append(ss)
            conv_s.append(cs)
        else:
            j = i - N_SSD_LAYERS
            if j == 0:
                k_p, v_p = shared_kv(hp, kv_norm, w_kv, pos_p)
                k_s, v_s = shared_kv(hs, kv_norm, w_kv, pos_s)
                n_seq = page_table.shape[0]
                k_past = cache_k[page_table].reshape(n_seq, -1, ATTN_N_HEADS, 2, ATTN_HEAD_DIM)
                v_past = cache_v[page_table].reshape(n_seq, -1, ATTN_N_HEADS, ATTN_V_DIM)
            lam_init = 0.8 - 0.6 * math.exp(-0.3 * i)
            lam = diff_lambda(attn_lambda_q1[j], attn_lambda_k1[j], attn_lambda_q2[j], attn_lambda_k2[j], lam_init)
            qp = diff_query(rmsnorm(hp, attn_norm_pre[j]), attn_w_q[j], pos_p)
            op = diff_attn_prompt(qp, k_p, v_p, lam)
            hp = hp + rmsnorm(diff_out(op, lam_init, attn_subln[j], attn_w_o[j]), attn_norm_post[j])
            qs = diff_query(rmsnorm(hs, attn_norm_pre[j]), attn_w_q[j], pos_s)
            os_ = diff_attn_sample(qs, k_past, v_past, k_s, v_s, lam)
            hs = hs + rmsnorm(diff_out(os_, lam_init, attn_subln[j], attn_w_o[j]), attn_norm_post[j])
        hp = hp + rmsnorm(squared_relu_mlp(rmsnorm(hp, mlp_norm_pre[i]), mlp_w_up[i], mlp_w_down[i]), mlp_norm_post[i])
        hs = hs + rmsnorm(squared_relu_mlp(rmsnorm(hs, mlp_norm_pre[i]), mlp_w_up[i], mlp_w_down[i]), mlp_norm_post[i])
    p_ssm = jnp.stack(ssm_p)
    p_conv = jnp.stack(conv_p)
    s_ssm = jnp.stack(ssm_s)
    s_conv = jnp.stack(conv_s)
    p_k = k_p.reshape(k_p.shape[0], k_p.shape[1], ATTN_N_HEADS, 2 * ATTN_HEAD_DIM)
    s_k = k_s.reshape(k_s.shape[0], k_s.shape[1], ATTN_N_HEADS, 2 * ATTN_HEAD_DIM)
    return (hp, hs, p_ssm, p_conv, p_k, v_p, s_ssm, s_conv, s_k, v_s)


_drawn_inputs = setup_inputs


def setup_inputs(seed=0):
    import zlib

    import numpy as np

    out = dict(_drawn_inputs(seed))
    spreads = {}
    factors = {'ssd_norm_post': 3.644,
     'ssd_d': 6.022,
     'ssd_gate_norm': 3.344,
     'mlp_norm_pre': 3.203,
     'mlp_norm_post': 3.419,
     'kv_norm': 2.747,
     'attn_norm_pre': 5.086,
     'attn_norm_post': 5.405,
     'attn_lambda_q2': 3.141,
     'attn_subln': 5.449}
    for name, (base, spread) in spreads.items():
        noise = np.random.default_rng([zlib.crc32(name.encode()), seed]).standard_normal(out[name].shape)
        drawn = base * np.exp(spread * noise) if base else spread * noise
        out[name] = jnp.asarray(drawn.astype(out[name].dtype))
    for name, factor in factors.items():
        out[name] = (out[name] * factor).astype(out[name].dtype)
    return out
```

```python
import math
from contextlib import ExitStack

import concourse.bass as bass
from concourse import mybir

F32 = mybir.dt.float32
F32R = mybir.dt.float32r
I32 = mybir.dt.int32
ACT = mybir.ActivationFunctionType
ALU = mybir.AluOpType
AXX = mybir.AxisListType.X

P = 128
D = 1024
SEQ = 512
NB = 8
T = SEQ + NB
HALF = T // 2
KT = D // P
NH_SSD, NG, NCH = 32, 4, 4
NPAIR = NH_SSD // 2
HG = NH_SSD // NG
NCONV = 24
AH = 8
PAGES = 2
FF = 4096 // P
EPS = 1e-6
LAM_INIT = 0.8 - 0.6 * math.exp(-0.3)
QK_SCALE = 64.0 ** -0.5

PV = {}
_at = 0
for _n, _w in (("ssd_pre", 8), ("ssd_post", 8), ("conv_w", 96), ("conv_b", 24), ("gate", 16), ("mlp_pre0", 8),
               ("mlp_pre1", 8), ("mlp_post0", 8), ("mlp_post1", 8), ("kv", 8), ("attn_pre", 8), ("attn_post", 8),
               ("subln", 1), ("d", 16), ("jsel", 2), ("pairsel", 64), ("rowj", 2), ("lam", 4), ("dt_bias", 32), ("a_log", 32)):
    PV[_n] = (_at, _at + _w)
    _at += _w
NPV = _at
C_ID, C_ONE, C_UP, C_SL, C_MASK, C_PERM = range(6)

GEMMS = [("xbc", 24, 1), ("z", 16, 1), ("out", 8, 2),
         ("up0a", 16, 1), ("down0a", 8, 2), ("up0b", 16, 1), ("down0b", 8, 2),
         ("k", 8, 1), ("q", 8, 1), ("v", 8, 1), ("o", 8, 1),
         ("up1a", 16, 1), ("down1a", 8, 2), ("up1b", 16, 1), ("down1b", 8, 2)]
BLOCK0, TILE0 = {}, {}
_b = _m = 0
for _n, _mt, _kb in GEMMS:
    BLOCK0[_n], TILE0[_n] = _b, _m
    _b += _mt * _kb
    _m += _mt
NBLK = _b
BLOCKS = {n: k for n, _, k in GEMMS}
RAW, SPL = 4, 2


def build(nc, wblk, wdt, x_t, pvec, consts, rope, ssm_in, conv_in, kcache, vcache, ptab,
          y_t, pssm, pconv, kt_out, vt_out, sssm, sconv):
    ctx = ExitStack()
    base = (nc.sbuf_base + 63) // 64 * 64

    def at(name, shape, offset, dt=F32):
        return nc.alloc_sbuf_tensor_at(name, shape, dt, offset=base + offset)

    def sem(name):
        return ctx.enter_context(nc.semaphore(name))

    O_H, O_A, O_HID, O_Y, O_F = 0, 16640, 49920, 116480, 149760
    O_RAW, O_SPL, O_SM = 166400, 182784, 199168
    hT = at("hT", [P, KT, T], O_H)
    aH = at("aH", [P, KT, T], O_A, F32R)
    aL = at("aL", [P, KT, T], O_A + 16640, F32R)
    hH = at("hidH", [P, 16, T], O_HID, F32R)
    hL = at("hidL", [P, 16, T], O_HID + 33280, F32R)
    yT = at("ssdY", [P, NPAIR, T], O_Y)
    bcT = at("bcT", [P, 8, T], O_F)
    fT = at("fT", [P, KT, T], O_F)
    raw = at("wraw", [P, RAW, 1024], O_RAW)
    wH = at("wH", [P, SPL, 1024], O_SPL, F32R)
    wL = at("wL", [P, SPL, 1024], O_SPL + SPL * 4096, F32R)
    cst = at("cst", [P, 6, P], O_SM)
    pv = at("pv", [P, NPV], O_SM + 3072)
    o = O_SM + 3072 + 4 * NPV + 28
    o -= o % 32
    acc = at("acc", [P, T], o)
    rpre = at("rpre", [P, T], o + 2080)
    rpost = at("rpost", [P, T], o + 4160)
    misc = at("misc", [P, 160], o + 6240)
    ptile = at("ptile", [1, NB * PAGES], o + 6880, I32)
    sqt = at("sqt", [P, 2, T], O_Y)
    rel = at("rel", [P, 2, T], O_Y + 4160)
    rsq = at("rsq", [P, 2, T], O_Y + 8320)
    r2 = at("r2", [P, T], O_Y + 12480)
    sq8 = at("sq8", [P, KT, T], O_Y)
    xr = at("xr", [P, 2, SEQ + 3], O_HID)
    cacc = at("cacc", [P, 2, SEQ], O_HID + 4128)
    q0 = O_HID
    xdt = at("xdt", [P, NCH, 512], q0)
    xde = at("xde", [P, NCH, 512], q0 + 8192)
    hst = at("hst", [P, NCH, 512], q0 + 16384)
    btok = at("btok", [P, NCH, P], q0 + 24576)
    cbm = at("cbm", [P, NCH, P], q0 + 26624)
    uadt = at("uadt", [P, 2, SEQ], q0 + 28672)
    seg = at("seg", [P, 2, SEQ], q0 + 32768)
    mm_ = at("mdec", [P, 2, SEQ], q0 + 36864)
    ebc = at("ebc", [P, 2, SEQ], q0 + 40960)
    yo = at("yoff", [P, SEQ], q0 + 45056)
    zs = at("zs", [P, 2, T], q0)
    hs = at("hs", [P, 2, NB, P], q0 + 4160)
    ht = at("ht", [P, NB, P], q0 + 12352)
    bbc = at("bbc", [P, NB, P], q0 + 16448)
    cbc = at("cbc", [P, NB, P], q0 + 20544)
    gs = at("gs", [P, NG, T], q0 + 24640)
    zq = at("zq", [P, 2, T], q0 + 32960)
    rg = at("rg", [P, NG, T], O_F)
    s0 = O_HID + 49152
    xs4 = at("xs4", [P, NCONV, NB, 4], s0)
    xsm = at("xsm", [P, NCONV, NB, 4], s0 + 3072)
    xsc = at("xsc", [P, NCONV, NB], s0 + 6144)
    pcv = at("pcv", [P, NCONV, 3], s0 + 6912)
    dtu = at("dtu", [P, 160], s0 + 7200)
    dtl = at("dtl", [P, 160], s0 + 7840)
    dtt = at("dtt", [P, 160], s0 + 8480)
    adt = at("adt", [P, 160], s0 + 9120)
    dex = at("dex", [P, 3, P], s0 + 9760)
    dtx = at("dtx", [P, NPAIR, NB], s0 + 11296)
    sdx = at("sdx", [P, NPAIR, NB], s0 + 11808)
    yss = at("yss", [P, NPAIR, NB], s0 + 12320)
    ea = at("ea", [P, 32], s0 + 12832)
    wdr = at("wdr", [P, KT, 32], s0 + 12960)
    wdh = at("wdh", [P, KT, 32], s0 + 13984, F32R)
    wdl = at("wdl", [P, KT, 32], s0 + 15008, F32R)
    kT = at("kT", [P, AH, T], O_Y)
    qT = at("qT", [P, AH, T], O_Y + 16640)
    vT = at("vT", [P, AH, T], O_F)
    vtok = at("vtok", [P, NCH, AH * P], O_HID + 16640)
    oT = at("oT", [P, AH, T], O_HID)
    ropt = at("ropt", [P, 2, T], O_HID + 49920)
    pr = at("probs", [P, 2, 2, SEQ], O_HID + 54080)
    attT = at("attT", [P, 2, SEQ], O_HID + 62272)
    ktile = at("ktile", [P, 2, AH, P], O_HID + 33280)
    vtile = at("vtile", [P, 2, AH, P], O_HID + 41472)
    a0 = O_A
    rt1 = at("rt1", [P, T], O_HID + 54080)
    rt2 = at("rt2", [P, T], O_HID + 56160)
    qz = at("qz", [P, AH, NB, 2], a0)
    kz = at("kz", [P, AH, NB, 2], a0 + 512)
    sT = at("sT", [P, PAGES, P], a0 + 1024)
    sE = at("sE", [P, 257], a0 + 2048)
    satt = at("satt", [P, PAGES, 64], a0 + 3104)
    snb = at("snb", [P, 64], a0 + 3616)
    cmb = at("cmb", [P, 64], a0 + 3872)
    ov = at("ov", [P, 64], a0 + 4128)
    osq = at("osq", [P, 2, T], a0 + 4416)
    orr = at("orr", [P, 2, T], a0 + 8576)
    onm = at("onm", [P, KT, T], O_F)

    G = [ctx.enter_context(nc.psum_tensor(f"G{i}", [P, 512], F32)) for i in range(4)]
    W = [ctx.enter_context(nc.psum_tensor(f"W{i}", [P, 512], F32)) for i in range(4)]

    def cc(i):
        return cst[:, i, :]

    def pc(name, i=0, n=1):
        a = PV[name][0] + i
        return pv[:, a:a + n]

    HV = (slice(0, HALF), slice(HALF, T))

    in_x, in_par = sem("in_x"), sem("in_par")
    raw_in = [sem(f"raw_in{i}") for i in range(RAW)]
    w_hi, w_lo = sem("w_hi"), sem("w_lo")
    blk = sem("blk_used")
    taken = sem("taken")
    mm0 = sem("x_sumsq")
    r0 = sem("r_first")
    dve, act = sem("dve_step"), sem("act_step")
    sq0, alo, ahi, ax = sem("sq0"), sem("a_lo"), sem("a_hi"), sem("a_x")
    wd_s, dt_mm, dt_u, dt_l, adt_s, dex_mm, dex_s = (sem(n) for n in (
        "wdt_split", "dt_mm", "dt_u", "dt_ln", "adt_ready", "decay_mm", "decay_ready"))
    xr_in, cv, sil = sem("xr_in"), sem("conv_done"), sem("silu_done")
    cs_in, scv, pss = sem("convstate_in"), sem("sample_conv"), sem("sample_silu")
    xz = sem("xr_zero")
    tr_mm, tr_x, bt_mm, bt_s, st_mm, h_s, cb_mm, cb_s = (sem(n) for n in (
        "x_transposed", "xdt_ready", "b_transposed", "btok_ready", "state_mm", "state_ready", "cb_mm", "cb_ready"))
    ua_s, sg_mm, sg_s, md_s, yd_mm, eb_s, yo_mm, y_s = (sem(n) for n in (
        "uadt_ready", "seg_mm", "seg_exp", "mdec_ready", "ydiag_mm", "e_ready", "yoff_mm", "y_ready"))
    hs_in = [sem("hs_in0"), sem("hs_in1")]
    hs_new, bc_mm, bc_s, ys_s = sem("hs_new"), sem("bcast_mm"), sem("bcast_ready"), sem("ysample")
    z_g, z_sq, z_gs = sem("z_gated"), sem("z_sq"), sem("z_sum")
    g_mm, g_r, g_n, g_hi, g_lo = sem("gn_mm"), sem("gn_r"), sem("gn_x"), sem("gn_hi"), sem("gn_lo")
    f_s, sqf, accf, ps_mm, rp_s = sem("f_ready"), sem("f_sq"), sem("f_acc"), sem("post_mm"), sem("post_r")
    h_n, sqh, acch, pr_mm, r_s = sem("h_new"), sem("h_sq"), sem("h_acc"), sem("pre_mm"), sem("pre_r")
    u_sq, u_hi, u_lo = sem("up_sq"), sem("up_hi"), sem("up_lo")
    qlo, qhi = sem("q_lo"), sem("q_hi")
    rp_in, rt_mm, kq_s = sem("rope_in"), sem("rot_mm"), sem("kq_ready")
    vt_mm, vk_s = sem("v_transposed"), sem("vtok_ready")
    sc_mm, mx_s, ex_s, att_s, at_mm, at_s, av_mm, o_s = (sem(n) for n in (
        "score_mm", "score_max", "probs_exp", "att_ready", "att_transposed", "attT_ready", "av_mm", "o_ready"))
    lm_s, lm_mm, lm_e, lm_r = sem("lam_prod"), sem("lam_mm"), sem("lam_exp"), sem("lam_ready")
    pt_in = sem("ptab_in")
    kp_in = [sem("kpage_in0"), sem("kpage_in1")]
    vp_in = [sem("vpage_in0"), sem("vpage_in1")]
    qz_s, ss_mm, st_s, s2_mm, s2_s, sx_s, cm_s, sa_mm, sa_s, sv_mm, os_s = (sem(n) for n in (
        "qz_ready", "page_scores", "sT_ready", "score_rows", "row_max", "row_exp", "comb_ready", "satt_mm",
        "satt_ready", "page_av", "o_sample"))
    oq_s, on_mm, or_s, ox_s, ohi, olo = (sem(n) for n in (
        "o_sq", "o_mm", "o_r", "o_normed", "o_hi", "o_lo"))
    st_out, fin_out, kv_out, y_out = sem("conv_rows_out"), sem("final_state_out"), sem("kv_out"), sem("y_out")
    hs_out = [sem("hs_out0"), sem("hs_out1")]
    block = ctx.enter_context(nc.Block())

    class Own:

        def __init__(self, eng, s):
            self.eng, self.s, self.n = eng, s, 0

        def __call__(self, ins):
            self.n += 1
            ins.then_inc(self.s, 1)
            self.eng.wait_ge(self.s, self.n)

    def values(pe, n):
        h, i = divmod(n, NCH)
        pe.wait_ge(att_s, n + 1)
        if n >= 2:
            pe.wait_ge(at_s, n - 1)
        for kb in range(i + 1):
            ins = pe.transpose(W[n % 2][:, kb * P:(kb + 1) * P], pr[:, n % 2, 0, kb * P:(kb + 1) * P], cc(C_ID))
        ins.then_inc(at_mm, 1)
        pe.wait_ge(at_s, n + 1)
        if n >= 2:
            pe.wait_ge(o_s, n - 1)
        for kb in range(i + 1):
            ins = pe.matmul(W[2 + n % 2][:, 0:P], vtok[:, kb, h * P:(h + 1) * P], attT[:, n % 2, kb * P:(kb + 1) * P],
                            start=kb == 0, stop=kb == i)
        ins.then_inc(av_mm, 1)

    def sub_norm(h, rsqrt):
        sc = nc.scalar
        sc.wait_ge(on_mm, h + 1)
        if h >= 2:
            sc.wait_ge(ox_s, h - 1)
        rsqrt(orr[:, h % 2, :], W, P, or_s)

    def gate_sums(m):
        return 3 * (m // 4) + m % 4 if m >= 0 else 0

    def gate_sq(sc, m):
        sc.wait_ge(z_g, m + 1)
        if m % 4 == 0:
            sc.activation(gs[:, m // 4, :], yT[:, m, :], ACT.Square).then_inc(z_sq, 1)
        else:
            if gate_sums(m - 2) > 0:
                sc.wait_ge(z_gs, gate_sums(m - 2))
            sc.activation(zq[:, m % 2, :], yT[:, m, :], ACT.Square).then_inc(z_sq, 1)

    def attT_copy(sc, n):
        i = n % NCH
        sc.wait_ge(at_mm, n + 1)
        if n >= 2:
            sc.wait_ge(av_mm, n - 1)
        sc.activation(attT[:, n % 2, 0:(i + 1) * P], W[n % 2][:, 0:(i + 1) * P], ACT.Copy).then_inc(at_s, 1)

    def gate_sum(v, own, m):
        if m % 4:
            v.wait_ge(z_sq, m + 1)
            if gate_sums(m - 1):
                v.wait_ge(z_gs, gate_sums(m - 1))
            v.tensor_tensor(gs[:, m // 4, :], gs[:, m // 4, :], zq[:, m % 2, :], ALU.add).then_inc(z_gs, 1)

    @block.sync
    def _(sp):
        sp.dma_start(hT[:, :, :], x_t).then_inc(in_x, 16)
        sp.dma_start(pv[:, :], pvec).then_inc(in_par, 16)
        sp.dma_start(cst[:, :, :], consts).then_inc(in_par, 16)
        sp.dma_start(wdr[:, :, :], wdt).then_inc(in_par, 16)
        for s in range(RAW):
            sp.dma_start(raw[:, s, :], wblk[s, :, :]).then_inc(raw_in[s], 16)
        sp.dma_start(xs4[:, :, :, 0:3], conv_in).then_inc(cs_in, 16)
        sp.dma_start(ptile[:, :], ptab).then_inc(pt_in, 16)
        def stream(a, b):
            with sp.Fori(a // RAW, b // RAW) as i:
                for s in range(RAW):
                    sp.wait_ge(w_lo, i * RAW + (s + 1 - RAW))
                    sp.dma_start(raw[:, s, :], wblk[bass.ds(i * RAW + s, 1), :, :].rearrange("o p n -> p (o n)")
                                 ).then_inc(raw_in[s], 16)

        zb, kb, ob = BLOCK0["z"] + RAW, BLOCK0["k"] + RAW, BLOCK0["o"] + RAW
        stream(RAW, zb)
        sp.wait_ge(cv, NCONV)
        sp.dma_start(pconv, pcv[:, :, :]).then_inc(st_out, 16)
        sp.wait_ge(scv, 1)
        sp.dma_start(sconv, xs4[:, :, :, 1:4]).then_inc(st_out, 16)
        for g in range(NG):
            sp.wait_ge(h_s, NCH * (g + 1))
            sp.dma_start(pssm[:, g, :], hst[:, NCH - 1, :]).then_inc(fin_out, 16)
        sp.wait_ge(y_s, NPAIR)
        sp.wait_ge(fin_out, 16 * NG)
        for m in range(2):
            sp.dma_start(hs[:, m, :, :], ssm_in[m, :, :, :]).then_inc(hs_in[m], 16)
        for m in range(NPAIR):
            b = zb + m
            sp.wait_ge(w_lo, b + 1 - RAW)
            sp.dma_start(raw[:, b % RAW, :], wblk[b, :, :]).then_inc(raw_in[b % RAW], 16)
            sp.wait_ge(ys_s, m + 1)
            sp.dma_start(sssm[m, :, :, :], hs[:, m % 2, :, :]).then_inc(hs_out[m % 2], 16)
            if m + 2 < NPAIR:
                sp.wait_ge(hs_out[m % 2], 16 * (m // 2 + 1))
                sp.dma_start(hs[:, m % 2, :, :], ssm_in[m + 2, :, :, :]).then_inc(hs_in[m % 2], 16)
        stream(zb + NPAIR, kb)
        sp.wait_ge(blk, BLOCK0["k"])
        sp.dma_start(ropt[:, :, :], rope).then_inc(rp_in, 16)
        stream(kb, ob)
        sp.wait_ge(pt_in, 16)
        sp.wait_ge(blk, BLOCK0["v"])

        def page(n, cache, dst, s):
            idx = sp.value_load(ptile[0:1, n:n + 1], min_val=0, max_val=cache.shape[0] - 1)
            sp.dma_start(dst[:, n % 2, :, :].rearrange("p h k -> p (h k)"),
                         cache[bass.ds(idx, 1), :, :].rearrange("o p n -> p (o n)")).then_inc(s[n % 2], 16)

        for n in range(2):
            page(n, kcache, ktile, kp_in)
            page(n, vcache, vtile, vp_in)
        sp.wait_ge(kq_s, 16)
        sp.dma_start(kt_out, kT[:, :, :]).then_inc(kv_out, 16)
        sp.wait_ge(taken, TILE0["v"] + AH)
        sp.dma_start(vt_out, vT[:, :, :]).then_inc(kv_out, 16)
        for n in range(2, NB * PAGES):
            sp.wait_ge(ss_mm, n - 1)
            page(n, kcache, ktile, kp_in)
        for n in range(2, NB * PAGES):
            sp.wait_ge(sv_mm, n - 1)
            page(n, vcache, vtile, vp_in)
        stream(ob, NBLK)
        sp.wait_ge(h_n, 32)
        sp.dma_start(y_t, hT[:, :, :]).then_inc(y_out, 16)
        sp.wait_ge(st_out, 32)
        sp.wait_ge(fin_out, 16 * NG)
        for i in range(2):
            sp.wait_ge(hs_out[i], 16 * NPAIR // 2)
        sp.wait_ge(kv_out, 32)
        sp.wait_ge(y_out, 16)

    @block.gpsimd
    def _(pool):
        def split(i, s, first):
            d = s % SPL
            pool.wait_ge(raw_in[s], i * 16 + 16)
            if not (first and s < SPL):
                pool.wait_ge(blk, i * RAW + (s + 1 - SPL))
            pool.tensor_tensor(wH[:, d, :].rearrange("p (k n) -> p k n", k=8),
                               raw[:, s, :].rearrange("p (k n) -> p k n", k=8),
                               cst[:, C_ONE:C_ONE + 1, :].broadcast_to([P, 8, P]), ALU.mult).then_inc(w_hi, 1)
            pool.wait_ge(w_hi, i * RAW + (s + 1))
            pool.tensor_tensor(wL[:, d, :], raw[:, s, :], wH[:, d, :].bitcast(F32), ALU.subtract).then_inc(w_lo, 1)

        pool.wait_ge(in_par, 48)
        for s in range(RAW):
            split(0, s, True)
        with pool.Fori(1, NBLK // RAW) as i:
            for s in range(RAW):
                split(i, s, False)

    @block.tensor
    def _(pe):
        def three(out, lh, ll, rh, rl, first, last):
            pe.matmul(out, lh, rh, start=first, stop=False)
            pe.matmul(out, lh, rl, start=False, stop=False)
            return pe.matmul(out, ll, rh, start=False, stop=last)

        def tile(name, m, b, inH, inL, wait_taken, koff=0):
            nk = BLOCKS[name]
            par = m[1]
            if wait_taken:
                pe.wait_ge(taken, m[0] - 1)
            for kb in range(nk):
                d = (b[1] + kb) % SPL
                pe.wait_ge(w_lo, b[0] + kb + 1)
                for k in range(8):
                    for h in range(2):
                        o_ = G[2 * par + h][:, 0:HALF]
                        lh, ll = wH[:, d, k * P:(k + 1) * P], wL[:, d, k * P:(k + 1) * P]
                        kk = kb * 8 + k
                        ins = three(o_, lh, ll, inH[:, kk, HV[h]], inL[:, kk, HV[h]],
                                    kb == 0 and k == 0, kb == nk - 1 and k == 7)
                ins.then_inc(blk, 1)

        def gemm(name, inH, inL, after=None):
            n = dict((a, b) for a, b, _ in GEMMS)[name]
            nk, m0, b0 = BLOCKS[name], TILE0[name], BLOCK0[name]
            if after is not None:
                for m in range(n):
                    tile(name, (m0 + m, (m0 + m) % 2), (b0 + m * nk, b0 + m * nk), inH, inL, True)
                    after(m)
                return
            first = 0
            if m0 == 0:
                for m in range(2):
                    tile(name, (m, m), (m * nk, m * nk), inH, inL, False)
                first = 1
            with pe.Fori(first, n // 2) as i:
                for u in range(2):
                    tile(name, (i * 2 + (m0 + u), (m0 + u) % 2), (i * (2 * nk) + (b0 + u * nk), b0 + u * nk),
                         inH, inL, True)

        pe.wait_ge(in_par, 48)
        pe.wait_ge(sq0, 1)
        for h in range(2):
            for t in range(KT):
                ins = pe.matmul(W[h][:, 0:HALF], cc(C_ONE), sq8[:, t, HV[h]], start=t == 0, stop=t == KT - 1)
        ins.then_inc(mm0, 1)
        pe.wait_ge(wd_s, 1)
        pe.wait_ge(alo, KT)
        for c in range(NCH + 1):
            n = P if c < NCH else NB
            ts = slice(c * P, c * P + n)
            for k in range(KT):
                ins = three(W[2][0:n, c * 32:c * 32 + 32], aH[:, k, ts], aL[:, k, ts], wdh[:, k, :], wdl[:, k, :],
                            k == 0, k == KT - 1)
        ins.then_inc(dt_mm, 1)
        pe.wait_ge(adt_s, 1)
        pe.matmul(W[3][:, 0:P], cc(C_ONE), adt[:, 0:P], start=True, stop=True)
        pe.matmul(W[3][:, P:2 * P], cc(C_SL), adt[:, 0:P], start=True, stop=True)
        for j, src in ((2, adt), (3, dtt)):
            for h in range(NH_SSD):
                e, q = 64 * (h % 2), h // 2
                ins = pe.matmul(W[3][e:e + 64, j * P + q * NB:j * P + q * NB + NB],
                                src[0:NB, P + h:P + h + 1].broadcast_to([NB, 64]), cst[0:NB, C_ID, 0:NB],
                                start=True, stop=True)
        ins.then_inc(dex_mm, 1)

        gemm("xbc", aH, aL)

        def seg_sum(k):
            pe.wait_ge(ua_s, k + 1)
            if k >= 2:
                pe.wait_ge(sg_s, k - 1)
            pe.matmul(W[k % 2][:, :], cc(C_SL), uadt[:, k % 2, :], start=True, stop=True)
            n, e = k // 2, 64 * (k % 2)
            if n >= 2 and e == 0:
                pe.wait_ge(y_s, n - 1)
            pe.matmul(W[2 + n % 2][e:e + 64, :], cst[:, C_ONE, 0:64], uadt[:, k % 2, :], start=True, stop=True
                      ).then_inc(sg_mm, 1)

        for g in range(NG):
            pe.wait_ge(pss, 1)
            pe.wait_ge(dex_s, 1)
            for c in range(NCH):
                n = g * NCH + c
                if n >= 2:
                    pe.wait_ge(tr_x, n - 1)
                if n < 2:
                    pe.wait_ge(sil, NCONV)
                elif c == 0:
                    pe.wait_ge(y_s, g * 4)
                for q in range(4):
                    ins = pe.transpose(W[c % 2][:, q * P:(q + 1) * P], yT[:, 4 * g + q, c * P:(c + 1) * P], cc(C_ID))
                ins.then_inc(tr_mm, 1)
            for c in range(NCH):
                ins = pe.transpose(W[2][:, c * P:(c + 1) * P], bcT[:, g, c * P:(c + 1) * P], cc(C_ID))
            ins.then_inc(bt_mm, 1)
            for c in range(NCH):
                ins = pe.matmul(W[3][:, c * P:(c + 1) * P], bcT[:, g, c * P:(c + 1) * P],
                                bcT[:, 4 + g, c * P:(c + 1) * P], start=True, stop=True)
            ins.then_inc(cb_mm, 1)
            pe.wait_ge(bt_s, g + 1)
            for c in range(NCH):
                pe.wait_ge(tr_x, g * NCH + NCH)
                if c >= 2:
                    pe.wait_ge(h_s, g * NCH + c - 1)
                pe.matmul(W[c % 2][:, :], btok[:, c, :], xde[:, c, :], start=True, stop=True).then_inc(st_mm, 1)
            pe.wait_ge(h_s, (g + 1) * NCH)
            pe.wait_ge(cb_s, g + 1)
            seg_sum(8 * g)
            for q in range(4):
                n = 4 * g + q
                if n >= 2:
                    pe.wait_ge(y_s, n - 1)
                for c in range(1, NCH):
                    ins = pe.matmul(G[2 + n % 2][:, c * P:(c + 1) * P], hst[:, c - 1, q * P:(q + 1) * P],
                                    bcT[:, 4 + g, c * P:(c + 1) * P], start=True, stop=True)
                ins.then_inc(yo_mm, 1)
                for e in range(2):
                    k = 2 * n + e
                    if k % 8 < 7:
                        seg_sum(k + 1)
                    pe.wait_ge(md_s, k + 1)
                    for c in range(NCH):
                        ins = pe.matmul(G[n % 2][64 * e:64 * e + 64, c * P:(c + 1) * P],
                                        xdt[:, c, (2 * q + e) * 64:(2 * q + e) * 64 + 64],
                                        mm_[:, k % 2, c * P:(c + 1) * P], start=True, stop=True)
                    ins.then_inc(yd_mm, 1)

        def z_after(m):
            if m % 4 == 0:
                g = m // 4
                if g == 0:
                    pe.wait_ge(y_s, NPAIR)
                else:
                    pe.wait_ge(bc_s, 4 * g)
                for j in range(2):
                    for hf in range(2):
                        for b in range(4):
                            ins = pe.matmul(W[2 * j + hf][:, b * P:(b + 1) * P],
                                            bcT[:, 4 * j + g, SEQ + 4 * hf + b:SEQ + 4 * hf + b + 1].broadcast_to([P, P]),
                                            cc(C_ID), start=True, stop=True)
                ins.then_inc(bc_mm, 1)

        z_after(0)
        gemm("z", aH, aL, after=lambda m: z_after(m + 1) if m < 15 else None)
        for g in range(NG):
            pe.wait_ge(z_gs, 3 * NG)
            if g:
                pe.wait_ge(g_r, g)
            for h in range(2):
                ins = pe.matmul(W[h][:, 0:HALF], cc(C_ONE), gs[:, g, HV[h]], start=True, stop=True)
            ins.then_inc(g_mm, 1)
        pe.wait_ge(g_lo, NPAIR)
        gemm("out", hH, hL)

        def boundary(p):
            pe.wait_ge(accf, 8 * p + 8)
            for h in range(2):
                ins = pe.matmul(W[h][:, 0:HALF], cc(C_ONE), acc[:, HV[h]], start=True, stop=True)
            ins.then_inc(ps_mm, 1)
            if p < 3:
                pe.wait_ge(acch, 8 * p + 8)
                for h in range(2):
                    ins = pe.matmul(W[2 + h][:, 0:HALF], cc(C_ONE), acc[:, HV[h]], start=True, stop=True)
                ins.then_inc(pr_mm, 1)
                pe.wait_ge(alo, KT + 8 * (p + 1))

        def mlp(l):
            for v, s in enumerate("ab"):
                gemm(f"up{l}{s}", aH, aL)
                pe.wait_ge(u_lo, 32 * l + 16 * v + 16)
                gemm(f"down{l}{s}", hH, hL)

        boundary(0)
        mlp(0)
        boundary(1)
        gemm("k", aH, aL)
        pe.wait_ge(qlo, KT)
        gemm("q", hH, hL)

        def rotate(n):
            src = kT if n < 8 else qT
            if n == 0:
                pe.wait_ge(taken, TILE0["q"] + 8)
                pe.wait_ge(r_s, 2)
            else:
                pe.wait_ge(kq_s, n)
            for h in range(2):
                ins = pe.matmul(W[h][:, 0:HALF], cc(C_PERM), src[:, n % 8, HV[h]], start=True, stop=True)
            ins.then_inc(rt_mm, 1)

        gemm("v", aH, aL, after=lambda m: (rotate(2 * m), rotate(2 * m + 1)))
        for h in range(AH):
            pe.wait_ge(taken, TILE0["v"] + AH)
            if h >= 2:
                pe.wait_ge(vk_s, h - 1)
            for c in range(NCH):
                ins = pe.transpose(W[2 + h % 2][:, c * P:(c + 1) * P], vT[:, h, c * P:(c + 1) * P], cc(C_ID))
            ins.then_inc(vt_mm, 1)
        pe.wait_ge(lm_s, 1)
        pe.wait_ge(kq_s, 16)
        pe.matmul(W[0][:, 0:2], cc(C_ONE), misc[:, 0:2], start=True, stop=True).then_inc(lm_mm, 1)
        pe.wait_ge(vk_s, AH)
        pe.wait_ge(lm_e, 1)
        n = 0
        for h in range(AH):
            for i in range(NCH):
                w = (i + 1) * P
                if n >= 2:
                    pe.wait_ge(ex_s, 2 * (n - 1))
                for j in range(2):
                    ins = pe.matmul(G[2 * (n % 2) + j][:, 0:w], qT[64 * j:64 * j + 64, h, i * P:(i + 1) * P],
                                    kT[64 * j:64 * j + 64, h, 0:w], start=True, stop=True)
                ins.then_inc(sc_mm, 1)
                if n >= 1:
                    values(pe, n - 1)
                n += 1
        values(pe, n - 1)
        pe.wait_ge(qz_s, 1)
        pe.wait_ge(o_s, 32)
        for b in range(NB):
            for pg in range(PAGES):
                n = 2 * b + pg
                pe.wait_ge(kp_in[n % 2], 16 * (n // 2 + 1))
                for h in range(AH):
                    ins = pe.matmul(G[pg][:, (h * NB + b) * 2:(h * NB + b) * 2 + 2], ktile[:, n % 2, h, :],
                                    qz[:, h, b, :], start=True, stop=True)
                ins.then_inc(ss_mm, 1)
        pe.wait_ge(st_s, 1)
        for pg in range(PAGES):
            pe.transpose(W[0][:, pg * P:(pg + 1) * P], sT[:, pg, :], cc(C_ID))
        pe.matmul(W[0][:, 256:257], kz[:, :, :, :].rearrange("p h b j -> p (h b j)"), cst[:, C_ONE, 0:1],
                  start=True, stop=True).then_inc(s2_mm, 1)
        pe.wait_ge(cm_s, 1)
        for pg in range(PAGES):
            pe.matmul(W[1][:, pg * 64:(pg + 1) * 64], sE[:, pg * P:(pg + 1) * P], cmb[:, :], start=True, stop=True)
        pe.matmul(W[1][:, 128:192], sE[:, 256:257].broadcast_to([P, P]), cmb[:, :], start=True, stop=True
                  ).then_inc(sa_mm, 1)
        pe.wait_ge(sa_s, 1)
        for b in range(NB):
            for pg in range(PAGES):
                n = 2 * b + pg
                pe.wait_ge(vp_in[n % 2], 16 * (n // 2 + 1))
                for h in range(AH):
                    ins = pe.matmul(W[2 + pg][:, h * NB + b:h * NB + b + 1], vtile[:, n % 2, h, :],
                                    satt[:, pg, h * NB + b:h * NB + b + 1], start=True, stop=True)
                ins.then_inc(sv_mm, 1)
        for h in range(AH):
            pe.wait_ge(oq_s, h + 1)
            if h >= 1:
                pe.wait_ge(or_s, h)
            for v in range(2):
                ins = pe.matmul(W[v][:, 0:HALF], cc(C_ONE), osq[:, h % 2, HV[v]], start=True, stop=True)
            ins.then_inc(on_mm, 1)
        pe.wait_ge(olo, AH)
        gemm("o", aH, aL)
        boundary(2)
        mlp(1)
        boundary(3)


    @block.scalar
    def _(sc):
        own = Own(sc, act)
        A = sc.activation

        def rsqrt(dst, banks, n, signal):
            for h in range(2):
                own(A(dst[:, HV[h]], banks[h][:, 0:HALF], ACT.Ln, scale=1.0 / n, bias=misc[:, 8:9]))
            A(dst, dst, ACT.Exp, scale=-0.5).then_inc(signal, 1)

        sc.wait_ge(in_x, 16)
        A(sq8[:, :, :], hT[:, :, :], ACT.Square).then_inc(sq0, 1)
        sc.wait_ge(mm0, 1)
        sc.wait_ge(wd_s, 1)
        rsqrt(rpre[:, :], W, D, r0)
        sc.wait_ge(in_par, 48)
        own(A(ea[:, :], pc("a_log", 0, 32), ACT.Exp))
        for t in range(KT):
            sc.wait_ge(ax, t + 1)
            A(aH[:, t, :], sq8[:, t, :], ACT.Copy).then_inc(ahi, 1)
        sc.wait_ge(dt_u, 1)
        own(A(dtl[:, :], dtu[:, :], ACT.Abs))
        own(A(dtl[:, :], dtl[:, :], ACT.Exp, scale=-1.0))
        A(dtl[:, :], dtl[:, :], ACT.Ln, bias=misc[:, 9:10]).then_inc(dt_l, 1)
        sc.wait_ge(dex_mm, 1)
        own(A(dtx[:, :, :].rearrange("p q b -> p (q b)"), W[3][:, 3 * P:4 * P], ACT.Copy))
        A(dex[:, :, :].rearrange("p q b -> p (q b)"), W[3][:, 0:3 * P], ACT.Exp).then_inc(dex_s, 1)

        def silu_tile(m):
            sc.wait_ge(cv, m + 1)
            dst = bcT[:, m, 0:SEQ] if m < 8 else yT[:, m - 8, 0:SEQ]
            A(dst, cacc[:, m % 2, :], ACT.Silu).then_inc(sil, 1)

        sc.wait_ge(xz, 1)
        for m in range(NCONV):
            sc.wait_ge(blk, m + 1)
            if m >= 2:
                sc.wait_ge(cv, m - 1)
            g = 2 * (m % 2)
            A(xr[:, m % 2, 3:3 + HALF], G[g][:, 0:HALF], ACT.Copy).then_inc(xr_in, 1)
            A(xr[:, m % 2, 3 + HALF:3 + SEQ], G[g + 1][:, 0:SEQ - HALF], ACT.Copy).then_inc(xr_in, 1)
            A(xs4[:, m, :, 3], G[g + 1][:, SEQ - HALF:HALF], ACT.Copy).then_inc(taken, 1)
            if m:
                silu_tile(m - 1)
        silu_tile(NCONV - 1)
        sc.wait_ge(scv, 1)
        own(A(bcT[:, :, SEQ:T], xsc[:, 0:8, :], ACT.Silu))
        A(yT[:, :, SEQ:T], xsc[:, 8:NCONV, :], ACT.Silu).then_inc(pss, 1)

        for g in range(NG):
            sc.wait_ge(bt_mm, g + 1)
            A(btok[:, :, :].rearrange("p c n -> p (c n)"), W[2][:, :], ACT.Copy).then_inc(bt_s, 1)
            for q in range(4):
                n = 4 * g + q
                for k in range(2 * n, 2 * n + 2):
                    sc.wait_ge(sg_mm, k + 1)
                    if k >= 2:
                        sc.wait_ge(md_s, k - 1)
                    A(seg[:, k % 2, :], W[k % 2][:, :], ACT.Exp).then_inc(sg_s, 1)
                if n >= 2:
                    sc.wait_ge(y_s, n - 1)
                A(ebc[:, n % 2, :], W[2 + n % 2][:, :], ACT.Exp).then_inc(eb_s, 1)

        for m in range(NPAIR):
            if m % 4 == 0:
                g = m // 4
                sc.wait_ge(bc_mm, g + 1)
                if g:
                    sc.wait_ge(ys_s, 4 * g)
                else:
                    sc.wait_ge(y_s, NPAIR)
                    sc.wait_ge(fin_out, 16 * NG)
                for j, dst in enumerate((bbc, cbc)):
                    for hf in range(2):
                        A(dst[:, 4 * hf:4 * hf + 4, :].rearrange("p b n -> p (b n)"), W[2 * j + hf][:, :],
                          ACT.Copy).then_inc(bc_s, 1)
            sc.wait_ge(blk, BLOCK0["z"] + m + 1)
            if m >= 2:
                sc.wait_ge(z_g, m - 1)
            gb = 2 * ((TILE0["z"] + m) % 2)
            A(zs[:, m % 2, HV[0]], G[gb][:, 0:HALF], ACT.Silu)
            A(zs[:, m % 2, HV[1]], G[gb + 1][:, 0:HALF], ACT.Silu).then_inc(taken, 1)
            if m:
                gate_sq(sc, m - 1)
        gate_sq(sc, NPAIR - 1)
        for g in range(NG):
            sc.wait_ge(g_mm, g + 1)
            if g == 0:
                sc.wait_ge(z_gs, 3 * NG)
                sc.wait_ge(ys_s, NPAIR)
            rsqrt(rg[:, g, :], W, 512, g_r)
        for q in range(NPAIR):
            sc.wait_ge(g_n, q + 1)
            A(hH[:, q, :], yT[:, q, :], ACT.Copy).then_inc(g_hi, 1)

        def boundary(p, gpre, own_f):
            for m in range(KT):
                if own_f:
                    nm = {0: "out", 2: "o"}[p]
                    gb = 2 * ((TILE0[nm] + m) % 2)
                    sc.wait_ge(blk, BLOCK0[nm] + BLOCKS[nm] * (m + 1))
                    A(fT[:, m, HV[0]], G[gb][:, 0:HALF], ACT.Copy)
                    A(fT[:, m, HV[1]], G[gb + 1][:, 0:HALF], ACT.Copy).then_inc(taken, 1)
                    sc.wait_ge(taken, TILE0[nm] + m + 1)
                else:
                    sc.wait_ge(f_s, 8 * (p // 2) + m + 1)
                if m >= 2:
                    sc.wait_ge(accf, 8 * p + m - 1)
                A(sqt[:, m % 2, :], fT[:, m, :], ACT.Square).then_inc(sqf, 1)
            sc.wait_ge(ps_mm, p + 1)
            rsqrt(rpost[:, :], W, D, rp_s)
            if p == 3:
                return
            for m in range(KT):
                sc.wait_ge(h_n, 8 * p + m + 1)
                if m >= 2:
                    sc.wait_ge(acch, 8 * p + m - 1)
                A(sqt[:, m % 2, :], hT[:, m, :], ACT.Square).then_inc(sqh, 1)
                A(aH[:, m, :], hT[:, m, :], ACT.Copy, scale=pc(gpre, m)).then_inc(ahi, 1)
                if p == 1:
                    A(hH[:, m, :], hT[:, m, :], ACT.Copy, scale=pc("attn_pre", m)).then_inc(qhi, 1)
            sc.wait_ge(pr_mm, p + 1)
            rsqrt(rpre[:, :], W[2:], D, r_s)

        def mlp(l):
            for v, s in enumerate("ab"):
                name = f"up{l}{s}"
                for m in range(16):
                    n = 32 * l + 16 * v + m
                    gb = 2 * ((TILE0[name] + m) % 2)
                    sc.wait_ge(blk, BLOCK0[name] + m + 1)
                    if n >= 2:
                        sc.wait_ge(u_sq, n - 1)
                    sc.wait_ge(taken, TILE0[name] + m)
                    A(rel[:, m % 2, HV[0]], G[gb][:, 0:HALF], ACT.Relu)
                    A(rel[:, m % 2, HV[1]], G[gb + 1][:, 0:HALF], ACT.Relu).then_inc(taken, 1)
                    if m:
                        hidden_hi(n - 1, m - 1)
                hidden_hi(32 * l + 16 * v + 15, 15)

        def hidden_hi(n, m):
            sc.wait_ge(u_sq, n + 1)
            A(hH[:, m, :], rsq[:, m % 2, :], ACT.Copy).then_inc(u_hi, 1)

        boundary(0, "mlp_pre0", True)
        mlp(0)
        boundary(1, "kv", False)
        for n in range(16):
            nm, dst = ("k", kT) if n < 8 else ("q", qT)
            m = n % 8
            gb = 2 * ((TILE0[nm] + m) % 2)
            sc.wait_ge(blk, BLOCK0[nm] + m + 1)
            A(dst[:, m, HV[0]], G[gb][:, 0:HALF], ACT.Copy)
            A(dst[:, m, HV[1]], G[gb + 1][:, 0:HALF], ACT.Copy).then_inc(taken, 1)
        for h in range(AH):
            sc.wait_ge(vt_mm, h + 1)
            A(vtok[:, :, h * P:(h + 1) * P], W[2 + h % 2][:, :].rearrange("p (c n) -> p c n", c=NCH), ACT.Copy
              ).then_inc(vk_s, 1)
        sc.wait_ge(lm_mm, 1)
        A(misc[:, 2:4], W[0][:, 0:2], ACT.Exp).then_inc(lm_e, 1)
        n = 0
        for h in range(AH):
            for i in range(NCH):
                w = (i + 1) * P
                sc.wait_ge(mx_s, n + 1)
                if n >= 2:
                    sc.wait_ge(at_mm, n - 1)
                for j in range(2):
                    A(pr[:, n % 2, j, 0:w], G[2 * (n % 2) + j][:, 0:w], ACT.Exp, scale=QK_SCALE,
                      bias=misc[:, 20 + 4 * (n % 2) + j:21 + 4 * (n % 2) + j],
                      accum_out=misc[:, 30 + 4 * (n % 2) + j:31 + 4 * (n % 2) + j]).then_inc(ex_s, 1)
                if n >= 1:
                    attT_copy(sc, n - 1)
                n += 1
        attT_copy(sc, n - 1)
        sc.wait_ge(ss_mm, 16)
        for pg in range(PAGES):
            ins = A(sT[:, pg, :], G[pg][:, 0:P], ACT.Copy)
            own(ins) if pg == 0 else ins.then_inc(st_s, 1)
        sc.wait_ge(s2_s, 1)
        A(sE[:, :], W[0][:, 0:257], ACT.Exp, scale=QK_SCALE, bias=misc[:, 41:42], accum_out=misc[:, 42:43]
          ).then_inc(sx_s, 1)
        sc.wait_ge(sa_mm, 1)
        own(A(satt[:, :, :].rearrange("p g c -> p (g c)"), W[1][:, 0:128], ACT.Copy))
        A(snb[:, :], W[1][:, 128:192], ACT.Copy).then_inc(sa_s, 1)
        sc.wait_ge(os_s, 1)
        for h in range(AH):
            if h >= 2:
                sc.wait_ge(on_mm, h - 1)
            A(osq[:, h % 2, :], oT[:, h, :], ACT.Square).then_inc(oq_s, 1)
            if h:
                sub_norm(h - 1, rsqrt)
        sub_norm(AH - 1, rsqrt)
        for h in range(AH):
            sc.wait_ge(ox_s, h + 1)
            if h == 0:
                sc.wait_ge(ox_s, AH)
            A(aH[:, h, :], onm[:, h, :], ACT.Copy).then_inc(ohi, 1)
        boundary(2, "mlp_pre1", True)
        mlp(1)
        boundary(3, None, False)






    @block.vector
    def _(v):
        own = Own(v, dve)
        TT, STT, TS = v.tensor_tensor, v.scalar_tensor_tensor, v.tensor_scalar

        own(v.memset(misc[:, 8:9], EPS))
        own(v.memset(misc[:, 9:10], 1.0))
        own(v.memset(dtu[:, :], 0.0))
        v.wait_ge(in_par, 48)
        own(v.tensor_copy(wdh[:, :, :], wdr[:, :, :]))
        TT(wdl[:, :, :], wdr[:, :, :], wdh[:, :, :].bitcast(F32), ALU.subtract).then_inc(wd_s, 1)
        own(v.memset(xr[:, 0, 0:3], 0.0))
        v.memset(xr[:, 1, 0:3], 0.0).then_inc(xz, 1)
        v.wait_ge(r0, 1)

        def first_lo(t):
            v.wait_ge(ahi, t + 1)
            TT(aL[:, t, :], sq8[:, t, :], aH[:, t, :].bitcast(F32), ALU.subtract).then_inc(alo, 1)

        for t in range(KT):
            STT(sq8[:, t, :], hT[:, t, :], pc("ssd_pre", t), rpre[:, :], ALU.mult, ALU.mult).then_inc(ax, 1)
            v.wait_ge(ax, t + 1)
            if t:
                first_lo(t - 1)
        first_lo(KT - 1)
        v.wait_ge(dt_mm, 1)
        own(TT(dtu[:, 0:P].rearrange("p (c h) -> p c h", c=NCH), W[2][:, 0:P].rearrange("p (c h) -> p c h", c=NCH),
               pc("dt_bias", 0, 32).unsqueeze(1).broadcast_to([P, NCH, 32]), ALU.add))
        TT(dtu[0:NB, P:P + 32], W[2][0:NB, P:P + 32], pv[0:NB, PV["dt_bias"][0]:PV["dt_bias"][1]], ALU.add
           ).then_inc(dt_u, 1)
        v.wait_ge(dt_l, 1)
        own(STT(dtt[:, :], dtu[:, :], 0.0, dtl[:, :], ALU.max, ALU.add))
        STT(adt[:, :].rearrange("p (c h) -> p c h", c=5), dtt[:, :].rearrange("p (c h) -> p c h", c=5), -1.0,
            ea[:, :].unsqueeze(1).broadcast_to([P, 5, 32]), ALU.mult, ALU.mult).then_inc(adt_s, 1)

        for m in range(NCONV):
            v.wait_ge(xr_in, 2 * m + 2)
            if m >= 2:
                v.wait_ge(sil, m - 1)
            a = cacc[:, m % 2, :]
            own(v.tensor_copy(pcv[:, m, :], xr[:, m % 2, SEQ:SEQ + 3]))
            own(TS(a, xr[:, m % 2, 0:SEQ], pc("conv_w", m), pc("conv_b", m), ALU.mult, ALU.add))
            for k in (1, 2, 3):
                ins = STT(a, xr[:, m % 2, k:k + SEQ], pc("conv_w", 24 * k + m), a, ALU.mult, ALU.add)
                own(ins) if k < 3 else ins.then_inc(cv, 1)
        v.wait_ge(cs_in, 16)
        v.wait_ge(taken, NCONV)
        for k in range(4):
            ins = TT(xsm[:, :, :, k], xs4[:, :, :, k],
                     pc("conv_w", 24 * k, 24).unsqueeze(2).broadcast_to([P, NCONV, NB]), ALU.mult)
            own(ins)
        own(v.tensor_reduce(xsc[:, :, :], xsm[:, :, :, :], AXX, ALU.add))
        TT(xsc[:, :, :], xsc[:, :, :], pc("conv_b", 0, 24).unsqueeze(2).broadcast_to([P, NCONV, NB]), ALU.add
           ).then_inc(scv, 1)
        v.wait_ge(pss, 1)
        v.wait_ge(dex_s, 1)
        own(TT(sdx[:, :, :], yT[:, :, SEQ:T], dtx[:, :, :], ALU.mult))

        dtb = dtt[:, 0:P].rearrange("p (c h) -> p c h", c=NCH)
        deb = dex[:, 1, :].rearrange("p (c h) -> p c h", c=NCH)
        cdb = dex[:, 0, :].rearrange("p (c h) -> p c h", c=NCH)

        def hb(src, c, g):
            return src[:, c, g * HG:(g + 1) * HG].unsqueeze(2).broadcast_to([P, HG, 64])

        def r8(ap):
            return ap.rearrange("p (h e) -> p h e", h=HG)

        for g in range(NG):
            if g:
                v.wait_ge(yd_mm, 8 * g)
                v.wait_ge(fin_out, 16 * g)
            for c in range(NCH):
                v.wait_ge(tr_mm, g * NCH + c + 1)
                own(TT(r8(xdt[:, c, :]), r8(W[c % 2][:, :]), hb(dtb, c, g), ALU.mult))
                TT(r8(xde[:, c, :]), r8(xdt[:, c, :]), hb(deb, c, g), ALU.mult).then_inc(tr_x, 1)
            v.wait_ge(cb_mm, g + 1)
            TT(cbm[:, :, :], W[3][:, :].rearrange("p (c l) -> p c l", c=NCH),
               cst[:, C_UP:C_UP + 1, :].broadcast_to([P, NCH, P]), ALU.mult).then_inc(cb_s, 1)
            for c in range(NCH):
                v.wait_ge(st_mm, g * NCH + c + 1)
                if c == 0:
                    v.tensor_copy(hst[:, 0, :], W[0][:, :]).then_inc(h_s, 1)
                else:
                    v.wait_ge(h_s, g * NCH + c)
                    own(TT(r8(hst[:, c, :]), r8(hst[:, c - 1, :]), hb(cdb, c, g), ALU.mult))
                    TT(hst[:, c, :], hst[:, c, :], W[c % 2][:, :], ALU.add).then_inc(h_s, 1)
            def make_uadt(k):
                if k >= 2:
                    v.wait_ge(sg_mm, k - 1)
                TT(uadt[:, k % 2, :].rearrange("p (c l) -> p c l", c=NCH),
                   cst[:, C_UP:C_UP + 1, :].broadcast_to([P, NCH, P]),
                   adt[:, 0:P].rearrange("p (c h) -> p c h", c=NCH)[:, :, k:k + 1].broadcast_to([P, NCH, P]),
                   ALU.mult).then_inc(ua_s, 1)

            if g == 0:
                make_uadt(0)
            for q in range(4):
                n = 4 * g + q
                for e in range(2):
                    k = 2 * n + e
                    if k + 1 < NH_SSD:
                        make_uadt(k + 1)
                    v.wait_ge(sg_s, k + 1)
                    if k >= 2:
                        v.wait_ge(yd_mm, k - 1)
                    TT(mm_[:, k % 2, :], seg[:, k % 2, :], cbm[:, :, :].rearrange("p c l -> p (c l)"), ALU.mult
                       ).then_inc(md_s, 1)
                v.wait_ge(eb_s, n + 1)
                v.wait_ge(yo_mm, n + 1)
                own(TT(yo[:, P:SEQ], G[2 + n % 2][:, P:SEQ], ebc[:, n % 2, P:SEQ], ALU.mult))
                v.wait_ge(yd_mm, 2 * n + 2)
                own(STT(yT[:, n, 0:SEQ], yT[:, n, 0:SEQ], pc("d", n), G[n % 2][:, :], ALU.mult, ALU.add))
                TT(yT[:, n, P:SEQ], yT[:, n, P:SEQ], yo[:, P:SEQ], ALU.add).then_inc(y_s, 1)

        for m in range(NPAIR):
            g = m // 4
            v.wait_ge(bc_s, 4 * g + 4)
            v.wait_ge(hs_in[m % 2], 16 * (m // 2 + 1))
            x = hs[:, m % 2, :, :]
            own(TT(x, x, dex[:, 2, m * NB:(m + 1) * NB].unsqueeze(2).broadcast_to([P, NB, P]), ALU.mult))
            own(TT(ht[:, :, :], bbc[:, :, :], sdx[:, m, :].unsqueeze(2).broadcast_to([P, NB, P]), ALU.mult))
            TT(x, x, ht[:, :, :], ALU.add).then_inc(hs_new, 1)
            v.wait_ge(hs_new, m + 1)
            own(TT(ht[:, :, :], x, cbc[:, :, :], ALU.mult))
            v.tensor_reduce(yss[:, m, :], ht[:, :, :], AXX, ALU.add).then_inc(ys_s, 1)
            v.wait_ge(ys_s, m + 1)
            own(STT(yT[:, m, SEQ:T], yT[:, m, SEQ:T], pc("d", m), yss[:, m, :], ALU.mult, ALU.add))
            v.wait_ge(taken, TILE0["z"] + m + 1)
            TT(yT[:, m, :], yT[:, m, :], zs[:, m % 2, :], ALU.mult).then_inc(z_g, 1)
            if m:
                gate_sum(v, own, m - 1)
        gate_sum(v, own, NPAIR - 1)
        def gate_lo(q):
            v.wait_ge(g_hi, q + 1)
            TT(hL[:, q, :], yT[:, q, :], hH[:, q, :].bitcast(F32), ALU.subtract).then_inc(g_lo, 1)

        for q in range(NPAIR):
            v.wait_ge(g_r, max(NG, q // 4 + 1))
            if q == 0:
                for i in range(2):
                    v.wait_ge(hs_out[i], 16 * NPAIR // 2)
                v.wait_ge(st_out, 32)
                v.wait_ge(fin_out, 16 * NG)
            STT(yT[:, q, :], yT[:, q, :], pc("gate", q), rg[:, q // 4, :], ALU.mult, ALU.mult).then_inc(g_n, 1)
            v.wait_ge(g_n, q + 1)
            if q:
                gate_lo(q - 1)
        gate_lo(NPAIR - 1)

        def add_sq(m, first, sem_in, sem_out, base_):
            v.wait_ge(sem_in, base_ + m + 1)
            if m == 0:
                v.tensor_copy(acc[:, :], sqt[:, 0, :]).then_inc(sem_out, 1)
            else:
                v.wait_ge(sem_out, base_ + m)
                TT(acc[:, :], acc[:, :], sqt[:, m % 2, :], ALU.add).then_inc(sem_out, 1)

        def boundary(p, gpost, gpre, own_f):
            if own_f:
                for m in range(KT):
                    add_sq(m, True, sqf, accf, 8 * p)
            v.wait_ge(rp_s, p + 1)

            def lows(m):
                add_sq(m, True, sqh, acch, 8 * p)
                v.wait_ge(ahi, KT + 8 * p + m + 1)
                STT(aL[:, m, :], hT[:, m, :], pc(gpre, m), aH[:, m, :].bitcast(F32), ALU.mult, ALU.subtract
                    ).then_inc(alo, 1)
                if p == 1:
                    v.wait_ge(qhi, m + 1)
                    STT(hL[:, m, :], hT[:, m, :], pc("attn_pre", m), hH[:, m, :].bitcast(F32), ALU.mult,
                        ALU.subtract).then_inc(qlo, 1)

            for m in range(KT):
                own(TT(fT[:, m, :], fT[:, m, :], rpost[:, :], ALU.mult))
                STT(hT[:, m, :], fT[:, m, :], pc(gpost, m), hT[:, m, :], ALU.mult, ALU.add).then_inc(h_n, 1)
                if m and p < 3:
                    v.wait_ge(h_n, 8 * p + m)
                    lows(m - 1)
            if p < 3:
                v.wait_ge(h_n, 8 * p + 8)
                lows(KT - 1)
                v.wait_ge(r_s, p + 1)

        def mlp(l):
            own(TT(r2[:, :], rpre[:, :], rpre[:, :], ALU.mult))

            def hidden_lo(n, m):
                v.wait_ge(u_hi, n + 1)
                TT(hL[:, m, :], rsq[:, m % 2, :], hH[:, m, :].bitcast(F32), ALU.subtract).then_inc(u_lo, 1)

            p = 1 + 2 * l
            for w, s in enumerate("ab"):
                for m in range(16):
                    n = 32 * l + 16 * w + m
                    v.wait_ge(taken, TILE0[f"up{l}{s}"] + m + 1)
                    if n >= 2:
                        v.wait_ge(u_lo, n - 1)
                    TT(rsq[:, m % 2, :], rel[:, m % 2, :], rel[:, m % 2, :], ALU.mult).then_inc(u_sq, 1)
                    v.wait_ge(u_sq, n + 1)
                    if m:
                        hidden_lo(n - 1, m - 1)
                hidden_lo(32 * l + 16 * w + 15, 15)
                name = f"down{l}{s}"
                for m in range(KT):
                    gb = 2 * ((TILE0[name] + m) % 2)
                    v.wait_ge(blk, BLOCK0[name] + 2 * (m + 1))
                    v.wait_ge(taken, TILE0[name] + m)
                    if s == "a":
                        own(v.tensor_copy(fT[:, m, HV[0]], G[gb][:, 0:HALF]))
                        v.tensor_copy(fT[:, m, HV[1]], G[gb + 1][:, 0:HALF]).then_inc(taken, 1)
                        v.wait_ge(taken, TILE0[name] + m + 1)
                    else:
                        own(TT(fT[:, m, HV[0]], fT[:, m, HV[0]], G[gb][:, 0:HALF], ALU.add))
                        TT(fT[:, m, HV[1]], fT[:, m, HV[1]], G[gb + 1][:, 0:HALF], ALU.add).then_inc(taken, 1)
                        v.wait_ge(taken, TILE0[name] + m + 1)
                        TT(fT[:, m, :], fT[:, m, :], r2[:, :], ALU.mult).then_inc(f_s, 1)
                        v.wait_ge(f_s, 8 * (p // 2) + m + 1)
                        if m:
                            add_sq(m - 1, True, sqf, accf, 8 * p)
            add_sq(KT - 1, True, sqf, accf, 8 * p)

        boundary(0, "ssd_post", "mlp_pre0", True)
        mlp(0)
        boundary(1, "mlp_post0", "kv", False)
        v.wait_ge(rp_in, 16)
        for j in range(2):
            own(TT(ropt[:, j, :], ropt[:, j, :], rpre[:, :], ALU.mult))

        def rope_tile(n):
            x = (kT if n < 8 else qT)[:, n % 8, :]
            v.wait_ge(rt_mm, n + 1)
            own(TT(rt1[:, :], x, ropt[:, 0, :], ALU.mult))
            for h in range(2):
                own(TT(rt2[:, HV[h]], W[h][:, 0:HALF], ropt[:, 1, HV[h]], ALU.mult))
            TT(x, rt1[:, :], rt2[:, :], ALU.add).then_inc(kq_s, 1)
            v.wait_ge(kq_s, n + 1)

        for m in range(AH):
            gb = 2 * ((TILE0["v"] + m) % 2)
            v.wait_ge(blk, BLOCK0["v"] + m + 1)
            v.wait_ge(taken, TILE0["v"] + m)
            own(TT(vT[:, m, HV[0]], G[gb][:, 0:HALF], rpre[:, HV[0]], ALU.mult))
            TT(vT[:, m, HV[1]], G[gb + 1][:, 0:HALF], rpre[:, HV[1]], ALU.mult).then_inc(taken, 1)
            rope_tile(2 * m)
            rope_tile(2 * m + 1)
        v.memset(misc[:, 0:2], 0.0).then_inc(lm_r, 1)
        v.wait_ge(lm_r, 1)
        lam = PV["lam"][0]
        for j in range(2):
            ins = TT(misc[:, j:j + 1], pv[:, lam + 2 * j:lam + 2 * j + 1], pv[:, lam + 2 * j + 1:lam + 2 * j + 2],
                     ALU.mult)
            own(ins) if j == 0 else ins.then_inc(lm_s, 1)
        v.wait_ge(lm_e, 1)
        own(TT(misc[:, 4:5], misc[:, 3:4], misc[:, 2:3], ALU.subtract))
        own(TS(misc[:, 4:5], misc[:, 4:5], -LAM_INIT, None, ALU.add))

        def combine(n):
            i = n % NCH
            w = (i + 1) * P
            s_ = 30 + 4 * (n % 2)
            v.wait_ge(ex_s, 2 * n + 2)
            own(v.reciprocal(misc[:, s_ + 2:s_ + 4], misc[:, s_:s_ + 2]))
            own(TT(misc[:, s_ + 3:s_ + 4], misc[:, s_ + 3:s_ + 4], misc[:, 4:5], ALU.mult))
            own(TS(pr[:, n % 2, 1, 0:w], pr[:, n % 2, 1, 0:w], misc[:, s_ + 3:s_ + 4], None, ALU.mult))
            STT(pr[:, n % 2, 0, 0:w], pr[:, n % 2, 0, 0:w], misc[:, s_ + 2:s_ + 3], pr[:, n % 2, 1, 0:w],
                ALU.mult, ALU.add).then_inc(att_s, 1)

        def take_o(n):
            h, i = divmod(n, NCH)
            v.wait_ge(av_mm, n + 1)
            v.tensor_copy(oT[:, h, i * P:(i + 1) * P], W[2 + n % 2][:, 0:P]).then_inc(o_s, 1)

        for n in range(AH * NCH):
            i = n % NCH
            w = (i + 1) * P
            v.wait_ge(sc_mm, n + 1)
            for j in range(2):
                own(TT(G[2 * (n % 2) + j][:, i * P:w], G[2 * (n % 2) + j][:, i * P:w], cc(C_MASK), ALU.add))
            for j in range(2):
                c_ = 20 + 4 * (n % 2) + j
                own(v.tensor_reduce(misc[:, c_ + 2:c_ + 3], G[2 * (n % 2) + j][:, 0:w], AXX, ALU.max))
            TS(misc[:, 20 + 4 * (n % 2):22 + 4 * (n % 2)], misc[:, 22 + 4 * (n % 2):24 + 4 * (n % 2)], -QK_SCALE, None,
               ALU.mult).then_inc(mx_s, 1)
            if n >= 1:
                combine(n - 1)
            if n >= 2:
                take_o(n - 2)
        combine(31)
        take_o(30)
        take_o(31)
        for j in range(2):
            own(TS(qz[:, :, :, j], qT[:, :, SEQ:T], pc("jsel", j), None, ALU.mult))
        for j in range(2):
            ins = TT(kz[:, :, :, j], qz[:, :, :, j], kT[:, :, SEQ:T], ALU.mult)
            own(ins) if j == 0 else ins.then_inc(qz_s, 1)
        v.wait_ge(s2_mm, 1)
        own(v.tensor_reduce(misc[:, 40:41], W[0][:, 0:257], AXX, ALU.max))
        TS(misc[:, 41:42], misc[:, 40:41], -QK_SCALE, None, ALU.mult).then_inc(s2_s, 1)
        v.wait_ge(sx_s, 1)
        own(v.reciprocal(misc[:, 43:44], misc[:, 42:43]))
        own(STT(misc[:, 44:45], pc("rowj", 1), misc[:, 4:5], pc("rowj", 0), ALU.mult, ALU.add))
        TS(cmb[:, :], pc("pairsel", 0, 64), misc[:, 44:45], misc[:, 43:44], ALU.mult, ALU.mult).then_inc(cm_s, 1)
        v.wait_ge(sv_mm, 16)
        v.wait_ge(sa_s, 1)
        own(TT(ov[:, :].rearrange("p (h b) -> p h b", h=AH), snb[:, :].rearrange("p (h b) -> p h b", h=AH),
               vT[:, :, SEQ:T], ALU.mult))
        for pg in range(PAGES):
            own(TT(ov[:, :], ov[:, :], W[2 + pg][:, 0:64], ALU.add))
        v.tensor_copy(oT[:, :, SEQ:T], ov[:, :].rearrange("p (h b) -> p h b", h=AH)).then_inc(os_s, 1)
        v.wait_ge(kv_out, 32)
        for h in range(AH):
            v.wait_ge(or_s, h + 1)
            own(TT(onm[:, h, :], oT[:, h, :], orr[:, h % 2, :], ALU.mult))
            TS(onm[:, h, :], onm[:, h, :], pc("subln"), 1.0 - LAM_INIT, ALU.mult, ALU.mult).then_inc(ox_s, 1)
        for h in range(AH):
            v.wait_ge(ohi, h + 1)
            TT(aL[:, h, :], onm[:, h, :], aH[:, h, :].bitcast(F32), ALU.subtract).then_inc(olo, 1)
        boundary(2, "attn_post", "mlp_pre1", True)
        mlp(1)
        boundary(3, "mlp_post1", None, False)

    ctx.close()


def kernel(**inputs):
    import numpy as np
    import concourse.bacc as bacc
    from concourse.bass_utils import run_bass_kernel_spmd

    f = {k: np.asarray(v) for k, v in inputs.items()}

    def blocks(w):
        k, n = w.shape
        return w.reshape(k // 1024, 8, P, n // P, P).transpose(3, 0, 2, 1, 4).reshape(-1, P, 1024)

    w_in = f["ssd_w_in"][0]
    xbc0 = 2048
    order = [w_in[:, xbc0 + 2048:xbc0 + 3072], w_in[:, xbc0:xbc0 + 2048], w_in[:, 0:2048], f["ssd_w_out"][0]]

    def mlp(l):
        up, down = f["mlp_w_up"][l], f["mlp_w_down"][l]
        return [up[:, :2048], down[:2048], up[:, 2048:], down[2048:]]

    order += mlp(0) + [f["w_kv"][:, :1024], f["attn_w_q"][0], f["w_kv"][:, 1024:], f["attn_w_o"][0]] + mlp(1)
    wblk = np.concatenate([blocks(w) for w in order])
    wdt = w_in[:, 5120:].reshape(8, P, 32).transpose(1, 0, 2)
    x_t = np.concatenate([f["x_prompt"][0], f["x_sample"][:, 0]]).reshape(T, KT, P).transpose(2, 1, 0)

    def cols(v):
        return v.reshape(-1, P).T

    def conv_order(a):
        return np.concatenate([a[16:24], a[0:16]])

    z = np.float32
    jsel = np.zeros((P, 2), z)
    jsel[:64, 0] = 1
    jsel[64:, 1] = 1
    rowj = np.zeros((P, 2), z)
    rowj[0::2, 0] = 1
    rowj[1::2, 1] = 1
    pairsel = np.kron(np.eye(64, dtype=z), np.ones((2, 1), z))
    lam = np.zeros((P, 4), z)
    for i, n in enumerate(("q1", "k1", "q2", "k2")):
        lam[:64, i] = f["attn_lambda_" + n][0]
    cw = np.concatenate([conv_order(f["ssd_conv_w"][0, k].reshape(24, P)).T for k in range(4)], 1)
    parts = {"ssd_pre": cols(f["ssd_norm_pre"][0]), "ssd_post": cols(f["ssd_norm_post"][0]), "conv_w": cw,
             "conv_b": conv_order(f["ssd_conv_b"][0].reshape(24, P)).T, "gate": cols(f["ssd_gate_norm"][0]),
             "mlp_pre0": cols(f["mlp_norm_pre"][0]), "mlp_pre1": cols(f["mlp_norm_pre"][1]),
             "mlp_post0": cols(f["mlp_norm_post"][0]), "mlp_post1": cols(f["mlp_norm_post"][1]),
             "kv": cols(f["kv_norm"]), "attn_pre": cols(f["attn_norm_pre"][0]), "attn_post": cols(f["attn_norm_post"][0]),
             "subln": cols(f["attn_subln"][0]), "d": cols(np.repeat(f["ssd_d"][0], 64)), "jsel": jsel,
             "pairsel": pairsel, "rowj": rowj, "lam": lam,
             "dt_bias": np.broadcast_to(f["ssd_dt_bias"][0], (P, 32)), "a_log": np.broadcast_to(f["ssd_a_log"][0], (P, 32))}
    pvec = np.concatenate([parts[n] for n in PV], 1)
    up = np.triu(np.ones((P, P), z))
    perm = np.zeros((P, P), z)
    for h in (0, 64):
        for i in range(8):
            perm[h + 8 + i, h + i] = -1
            perm[h + i, h + 8 + i] = 1
    consts = np.stack([np.eye(P, dtype=z), np.ones((P, P), z), up, np.tril(np.ones((P, P), z), -1),
                       np.triu(np.full((P, P), -3e38, z), 1), perm], 1)
    pos = np.concatenate([np.arange(SEQ), np.full(NB, 256)]).astype(z)
    inv = (z(500000.0) ** (-np.arange(0, 16, 2, dtype=z) / z(16))).astype(z)
    ang = inv[:, None] * pos[None, :]
    rope = np.zeros((P, 2, T), z)
    rope[:, 0] = 1
    for h in (0, 8, 64, 72):
        rope[h:h + 8, 0] = np.cos(ang)
        rope[h:h + 8, 1] = np.sin(ang)
    ssm_in = f["state_ssm"][0].reshape(NB, NPAIR, P, P).transpose(1, 2, 0, 3)
    conv_in = conv_order(f["state_conv"][0].reshape(NB, 3, 24, P).transpose(2, 3, 0, 1)).transpose(1, 0, 2, 3)
    npg = f["cache_k"].shape[0]
    kcache = f["cache_k"].transpose(0, 3, 2, 1).reshape(npg, P, 1024)
    vcache = f["cache_v"].reshape(npg, P, 1024)
    ins = {"wblk": wblk, "wdt": wdt, "x_t": x_t, "pvec": pvec, "consts": consts, "rope": rope, "ssm_in": ssm_in,
           "conv_in": conv_in, "kcache": kcache, "vcache": vcache, "ptab": f["page_table"].reshape(1, -1)}
    outs = {"y_t": (P, KT, T), "pssm": (P, NG, 512), "pconv": (P, NCONV, 3), "kt_out": (P, AH, T), "vt_out": (P, AH, T),
            "sssm": (NPAIR, P, NB, P), "sconv": (P, NCONV, NB, 3)}
    nc = bacc.Bacc("TRN2", target_bir_lowering=False, num_devices=1)
    ins = {k: np.ascontiguousarray(a) for k, a in ins.items()}
    args = [nc.dram_tensor(k, a.shape, mybir.dt.from_np(a.dtype), kind="ExternalInput").ap() for k, a in ins.items()]
    args += [nc.dram_tensor(k, sh, F32, kind="ExternalOutput").ap() for k, sh in outs.items()]
    build(nc, *args)
    o = run_bass_kernel_spmd(nc, [ins], core_ids=[0]).results[0]

    def tokens(a):
        a = a.transpose(2, 1, 0)
        return a[:SEQ].reshape(1, SEQ, -1), a[SEQ:].reshape(NB, 1, -1)

    def unconv(a):
        return np.concatenate([a[8:24], a[0:8]])

    y_p, y_s = tokens(o["y_t"])
    k_p, k_s = (a.reshape(*a.shape[:2], AH, P) for a in tokens(o["kt_out"]))
    v_p, v_s = (a.reshape(*a.shape[:2], AH, P) for a in tokens(o["vt_out"]))
    p_ssm = o["pssm"].reshape(P, NH_SSD, 64).transpose(1, 2, 0)[None, None]
    p_conv = unconv(o["pconv"].transpose(1, 0, 2)).reshape(3072, 3).T[None, None]
    s_ssm = o["sssm"].transpose(2, 0, 1, 3).reshape(1, NB, NH_SSD, 64, P)
    s_conv = unconv(o["sconv"].transpose(1, 0, 2, 3)).reshape(3072, NB, 3).transpose(1, 2, 0)[None]
    return tuple(np.ascontiguousarray(a) for a in (y_p, y_s, p_ssm, p_conv, k_p, v_p, s_ssm, s_conv, k_s, v_s))
```

```python
import math
from contextlib import ExitStack

import concourse.bass as bass
from concourse import mybir

F32 = mybir.dt.float32
F32R = mybir.dt.float32r
I32 = mybir.dt.int32
ACT = mybir.ActivationFunctionType
ALU = mybir.AluOpType
AXX = mybir.AxisListType.X

P = 128
D = 1024
SEQ = 512
NB = 8
T = SEQ + NB
HALF = T // 2
KT = D // P
NH_SSD, NG, NCH = 32, 4, 4
NPAIR = NH_SSD // 2
HG = NH_SSD // NG
NCONV = 24
AH = 8
PAGES = 2
FF = 4096 // P
EPS = 1e-6
LAM_INIT = 0.8 - 0.6 * math.exp(-0.3)
QK_SCALE = 64.0 ** -0.5

PV = {}
_at = 0
for _n, _w in (("ssd_pre", 8), ("ssd_post", 8), ("conv_w", 96), ("conv_b", 24), ("gate", 16), ("mlp_pre0", 8),
               ("mlp_pre1", 8), ("mlp_post0", 8), ("mlp_post1", 8), ("kv", 8), ("attn_pre", 8), ("attn_post", 8),
               ("subln", 1), ("d", 16), ("jsel", 2), ("pairsel", 64), ("rowj", 2), ("lam", 4), ("dt_bias", 32), ("a_log", 32)):
    PV[_n] = (_at, _at + _w)
    _at += _w
NPV = _at
C_ID, C_ONE, C_UP, C_SL, C_MASK, C_PERM = range(6)

GEMMS = [("xbc", 24, 1), ("z", 16, 1), ("out", 8, 2),
         ("up0a", 16, 1), ("down0a", 8, 2), ("up0b", 16, 1), ("down0b", 8, 2),
         ("q", 8, 1), ("k", 8, 1), ("v", 8, 1), ("o", 8, 1),
         ("up1a", 16, 1), ("down1a", 8, 2), ("up1b", 16, 1), ("down1b", 8, 2)]
BLOCK0, TILE0 = {}, {}
_b = _m = 0
for _n, _mt, _kb in GEMMS:
    BLOCK0[_n], TILE0[_n] = _b, _m
    _b += _mt * _kb
    _m += _mt
NBLK = _b
BLOCKS = {n: k for n, _, k in GEMMS}
RAW, SPL = 4, 2


def build(nc, wblk, wdt, x_t, pvec, consts, rope, ssm_in, conv_in, kcache, vcache, ptab,
          y_t, pssm, pconv, kt_out, vt_out, sssm, sconv):
    ctx = ExitStack()
    base = (nc.sbuf_base + 63) // 64 * 64

    def at(name, shape, offset, dt=F32):
        return nc.alloc_sbuf_tensor_at(name, shape, dt, offset=base + offset)

    def sem(name):
        return ctx.enter_context(nc.semaphore(name))

    O_H, O_A, O_HID, O_Y, O_F = 0, 16640, 49920, 116480, 149760
    O_RAW, O_SPL, O_SM = 166400, 182784, 199168
    hT = at("hT", [P, KT, T], O_H)
    aH = at("aH", [P, KT, T], O_A, F32R)
    aL = at("aL", [P, KT, T], O_A + 16640, F32R)
    hH = at("hidH", [P, 16, T], O_HID, F32R)
    hL = at("hidL", [P, 16, T], O_HID + 33280, F32R)
    yT = at("ssdY", [P, NPAIR, T], O_Y)
    bcT = at("bcT", [P, 8, T], O_F)
    fT = at("fT", [P, KT, T], O_F)
    raw = at("wraw", [P, RAW, 1024], O_RAW)
    wH = at("wH", [P, SPL, 1024], O_SPL, F32R)
    wL = at("wL", [P, SPL, 1024], O_SPL + SPL * 4096, F32R)
    cst = at("cst", [P, 6, P], O_SM)
    pv = at("pv", [P, NPV], O_SM + 3072)
    o = O_SM + 3072 + 4 * NPV + 28
    o -= o % 32
    acc = at("acc", [P, T], o)
    rpre = at("rpre", [P, T], o + 2080)
    rpost = at("rpost", [P, T], o + 4160)
    misc = at("misc", [P, 160], o + 6240)
    ptile = at("ptile", [1, NB * PAGES], o + 6880, I32)
    sqt = at("sqt", [P, 2, T], O_Y)
    rel = at("rel", [P, 2, T], O_Y + 4160)
    rsq = at("rsq", [P, 2, T], O_Y + 8320)
    r2 = at("r2", [P, T], O_Y + 12480)
    sq8 = at("sq8", [P, KT, T], O_Y)
    xr = at("xr", [P, 2, SEQ + 3], O_HID)
    cacc = at("cacc", [P, 2, SEQ], O_HID + 4128)
    q0 = O_HID
    xdt = at("xdt", [P, NCH, 512], q0)
    xde = at("xde", [P, NCH, 512], q0 + 8192)
    hst = at("hst", [P, NCH, 512], q0 + 16384)
    btok = at("btok", [P, NCH, P], q0 + 24576)
    cbm = at("cbm", [P, NCH, P], q0 + 26624)
    uadt = at("uadt", [P, 2, SEQ], q0 + 28672)
    seg = at("seg", [P, 2, SEQ], q0 + 32768)
    mm_ = at("mdec", [P, 2, SEQ], q0 + 36864)
    ebc = at("ebc", [P, 2, SEQ], q0 + 40960)
    yo = at("yoff", [P, SEQ], q0 + 45056)
    zs = at("zs", [P, 2, T], q0)
    hs = at("hs", [P, 2, NB, P], q0 + 4160)
    ht = at("ht", [P, NB, P], q0 + 12352)
    bbc = at("bbc", [P, NB, P], q0 + 16448)
    cbc = at("cbc", [P, NB, P], q0 + 20544)
    gs = at("gs", [P, NG, T], q0 + 24640)
    zq = at("zq", [P, 2, T], q0 + 32960)
    rg = at("rg", [P, NG, T], O_F)
    s0 = O_HID + 49152
    xs4 = at("xs4", [P, NCONV, NB, 4], s0)
    xsm = at("xsm", [P, NCONV, NB, 4], s0 + 3072)
    xsc = at("xsc", [P, NCONV, NB], s0 + 6144)
    pcv = at("pcv", [P, NCONV, 3], s0 + 6912)
    dtu = at("dtu", [P, 160], s0 + 7200)
    dtl = at("dtl", [P, 160], s0 + 7840)
    dtt = at("dtt", [P, 160], s0 + 8480)
    adt = at("adt", [P, 160], s0 + 9120)
    dex = at("dex", [P, 3, P], s0 + 9760)
    dtx = at("dtx", [P, NPAIR, NB], s0 + 11296)
    sdx = at("sdx", [P, NPAIR, NB], s0 + 11808)
    yss = at("yss", [P, NPAIR, NB], s0 + 12320)
    ea = at("ea", [P, 32], s0 + 12832)
    wdr = at("wdr", [P, KT, 32], s0 + 12960)
    wdh = at("wdh", [P, KT, 32], s0 + 13984, F32R)
    wdl = at("wdl", [P, KT, 32], s0 + 15008, F32R)
    kT = at("kT", [P, AH, T], O_Y)
    qT = at("qT", [P, AH, T], O_Y + 16640)
    vT = at("vT", [P, AH, T], O_F)
    vtok = at("vtok", [P, NCH, AH * P], O_HID + 16640)
    oT = at("oT", [P, AH, T], O_HID)
    ropt = at("ropt", [P, 2, T], O_HID + 49920)
    pr = at("probs", [P, 4, 2, SEQ], O_A + 16640)
    attT = at("attT", [P, 4, SEQ], O_HID + 54080)
    ktile = at("ktile", [P, 4, AH, P], O_A + 16640)
    vtile = at("vtile", [P, 4, AH, P], O_HID + 33280)
    a0 = O_A
    rt1 = at("rt1", [P, T], O_HID + 54080)
    rt2 = at("rt2", [P, T], O_HID + 56160)
    qz = at("qz", [P, AH, NB, 2], a0)
    kz = at("kz", [P, AH, NB, 2], a0 + 512)
    sT = at("sT", [P, PAGES, P], a0 + 1024)
    sE = at("sE", [P, 257], a0 + 2048)
    satt = at("satt", [P, PAGES, 64], a0 + 3104)
    snb = at("snb", [P, 64], a0 + 3616)
    cmb = at("cmb", [P, 64], a0 + 3872)
    ov = at("ov", [P, 64], a0 + 4128)
    osq = at("osq", [P, 2, T], a0 + 4416)
    orr = at("orr", [P, 2, T], a0 + 8576)
    onm = at("onm", [P, KT, T], O_F)

    GP = [ctx.enter_context(nc.psum_tensor(f"GP{i}", [P, 2, 512], F32)) for i in range(2)]
    WP = [ctx.enter_context(nc.psum_tensor(f"WP{i}", [P, 2, 512], F32)) for i in range(2)]
    G = [GP[i // 2][:, i % 2, :] for i in range(4)]
    W = [WP[i // 2][:, i % 2, :] for i in range(4)]

    def cc(i):
        return cst[:, i, :]

    def pc(name, i=0, n=1):
        a = PV[name][0] + i
        return pv[:, a:a + n]

    HV = (slice(0, HALF), slice(HALF, T))

    in_x, in_par = sem("in_x"), sem("in_par")
    raw_in = [sem(f"raw_in{i}") for i in range(RAW)]
    w_hi, w_lo = sem("w_hi"), sem("w_lo")
    blk = sem("blk_used")
    taken = sem("taken")
    mm0 = sem("x_sumsq")
    r0 = sem("r_first")
    dve, act = sem("dve_step"), sem("act_step")
    sq0, alo, ahi, ax = sem("sq0"), sem("a_lo"), sem("a_hi"), sem("a_x")
    wd_s, dt_mm, dt_u, dt_l, adt_s, dex_mm, dex_s = (sem(n) for n in (
        "wdt_split", "dt_mm", "dt_u", "dt_ln", "adt_ready", "decay_mm", "decay_ready"))
    xr_in, cv, sil = sem("xr_in"), sem("conv_done"), sem("silu_done")
    cs_in, scv, pss = sem("convstate_in"), sem("sample_conv"), sem("sample_silu")
    xz = sem("xr_zero")
    tr_mm, tr_x, bt_mm, bt_s, st_mm, h_s, cb_mm, cb_s = (sem(n) for n in (
        "x_transposed", "xdt_ready", "b_transposed", "btok_ready", "state_mm", "state_ready", "cb_mm", "cb_ready"))
    ua_s, sg_mm, sg_s, md_s, yd_mm, eb_s, yo_mm, y_s = (sem(n) for n in (
        "uadt_ready", "seg_mm", "seg_exp", "mdec_ready", "ydiag_mm", "e_ready", "yoff_mm", "y_ready"))
    hs_in = [sem("hs_in0"), sem("hs_in1")]
    hs_new, bc_mm, bc_s, ys_s = sem("hs_new"), sem("bcast_mm"), sem("bcast_ready"), sem("ysample")
    z_g, z_sq, z_gs = sem("z_gated"), sem("z_sq"), sem("z_sum")
    g_mm, g_r, g_n, g_hi, g_lo = sem("gn_mm"), sem("gn_r"), sem("gn_x"), sem("gn_hi"), sem("gn_lo")
    f_s, sqf, accf, ps_mm, rp_s = sem("f_ready"), sem("f_sq"), sem("f_acc"), sem("post_mm"), sem("post_r")
    h_n, sqh, pr_mm, r_s = sem("h_new"), sem("h_sq"), sem("pre_mm"), sem("pre_r")
    fr_s = sem("f_scaled")
    u_sq, u_hi, u_lo = sem("up_sq"), sem("up_hi"), sem("up_lo")
    qlo, qhi = sem("q_lo"), sem("q_hi")
    rp_in, rt_mm, kq_s = sem("rope_in"), sem("rot_mm"), sem("kq_ready")
    vt_mm, vk_s = sem("v_transposed"), sem("vtok_ready")
    sc_mm, mx_s, ex_s, att_s, at_mm, at_s, av_mm, o_s = (sem(n) for n in (
        "score_mm", "score_max", "probs_exp", "att_ready", "att_transposed", "attT_ready", "av_mm", "o_ready"))
    lm_s, lm_mm, lm_e, lm_r = sem("lam_prod"), sem("lam_mm"), sem("lam_exp"), sem("lam_ready")
    pt_in = sem("ptab_in")
    kp_in = [sem(f"kpage_in{i}") for i in range(4)]
    vp_in = [sem(f"vpage_in{i}") for i in range(4)]
    kz_s = sem("kz_ready")
    qz_s, ss_mm, st_s, s2_mm, s2_s, sx_s, cm_s, sa_mm, sa_s, sv_mm, os_s = (sem(n) for n in (
        "qz_ready", "page_scores", "sT_ready", "score_rows", "row_max", "row_exp", "comb_ready", "satt_mm",
        "satt_ready", "page_av", "o_sample"))
    oq_s, on_mm, or_s, ox_s, ohi, olo = (sem(n) for n in (
        "o_sq", "o_mm", "o_r", "o_normed", "o_hi", "o_lo"))
    st_out, fin_out, kv_out, y_out = sem("conv_rows_out"), sem("final_state_out"), sem("kv_out"), sem("y_out")
    hs_out = [sem("hs_out0"), sem("hs_out1")]
    block = ctx.enter_context(nc.Block())

    class Own:

        def __init__(self, eng, s):
            self.eng, self.s, self.n = eng, s, 0

        def __call__(self, ins):
            self.n += 1
            ins.then_inc(self.s, 1)
            self.eng.wait_ge(self.s, self.n)

    def sub_norm(h, rsqrt):
        sc = nc.scalar
        sc.wait_ge(on_mm, h + 1)
        if h >= 2:
            sc.wait_ge(ox_s, h - 1)
        rsqrt(orr[:, h % 2, :], GP[h % 2], P, or_s)

    def gate_sums(m):
        return 3 * (m // 4) + m % 4 if m >= 0 else 0

    def gate_sq(sc, m):
        sc.wait_ge(z_g, m + 1)
        if m % 4 == 0:
            sc.activation(gs[:, m // 4, :], yT[:, m, :], ACT.Square).then_inc(z_sq, 1)
        else:
            if gate_sums(m - 2) > 0:
                sc.wait_ge(z_gs, gate_sums(m - 2))
            sc.activation(zq[:, m % 2, :], yT[:, m, :], ACT.Square).then_inc(z_sq, 1)

    def gate_sum(v, own, m):
        if m % 4:
            v.wait_ge(z_sq, m + 1)
            if gate_sums(m - 1):
                v.wait_ge(z_gs, gate_sums(m - 1))
            v.tensor_tensor(gs[:, m // 4, :], gs[:, m // 4, :], zq[:, m % 2, :], ALU.add).then_inc(z_gs, 1)

    @block.sync
    def _(sp):
        sp.dma_start(hT[:, :, :], x_t).then_inc(in_x, 16)
        sp.dma_start(pv[:, :], pvec).then_inc(in_par, 16)
        sp.dma_start(cst[:, :, :], consts).then_inc(in_par, 16)
        sp.dma_start(wdr[:, :, :], wdt).then_inc(in_par, 16)
        for s in range(RAW):
            sp.dma_start(raw[:, s, :], wblk[s, :, :]).then_inc(raw_in[s], 16)
        sp.dma_start(xs4[:, :, :, 0:3], conv_in).then_inc(cs_in, 16)
        sp.dma_start(ptile[:, :], ptab).then_inc(pt_in, 16)
        def stream(a, b):
            with sp.Fori(a // RAW, b // RAW) as i:
                for s in range(RAW):
                    sp.wait_ge(w_lo, i * RAW + (s + 1 - RAW))
                    sp.dma_start(raw[:, s, :], wblk[bass.ds(i * RAW + s, 1), :, :].rearrange("o p n -> p (o n)")
                                 ).then_inc(raw_in[s], 16)

        zb, kb, ob = BLOCK0["z"] + RAW, BLOCK0["q"] + RAW, BLOCK0["o"] + RAW
        stream(RAW, zb)
        sp.wait_ge(cv, NCONV)
        sp.dma_start(pconv, pcv[:, :, :]).then_inc(st_out, 16)
        sp.wait_ge(scv, 1)
        sp.dma_start(sconv, xs4[:, :, :, 1:4]).then_inc(st_out, 16)
        for g in range(NG):
            sp.wait_ge(h_s, NCH * (g + 1))
            sp.dma_start(pssm[:, g, :], hst[:, NCH - 1, :]).then_inc(fin_out, 16)
        sp.wait_ge(y_s, NPAIR)
        sp.wait_ge(fin_out, 16 * NG)
        for m in range(2):
            sp.dma_start(hs[:, m, :, :], ssm_in[m, :, :, :]).then_inc(hs_in[m], 16)
        for m in range(NPAIR):
            b = zb + m
            sp.wait_ge(w_lo, b + 1 - RAW)
            sp.dma_start(raw[:, b % RAW, :], wblk[b, :, :]).then_inc(raw_in[b % RAW], 16)
            sp.wait_ge(ys_s, m + 1)
            sp.dma_start(sssm[m, :, :, :], hs[:, m % 2, :, :]).then_inc(hs_out[m % 2], 16)
            if m + 2 < NPAIR:
                sp.wait_ge(hs_out[m % 2], 16 * (m // 2 + 1))
                sp.dma_start(hs[:, m % 2, :, :], ssm_in[m + 2, :, :, :]).then_inc(hs_in[m % 2], 16)
        stream(zb + NPAIR, kb)
        sp.wait_ge(blk, BLOCK0["q"])
        sp.dma_start(ropt[:, :, :], rope).then_inc(rp_in, 16)
        sp.wait_ge(pt_in, 16)

        def page(n, cache, dst, s):
            idx = sp.value_load(ptile[0:1, n:n + 1], min_val=0, max_val=cache.shape[0] - 1)
            sp.dma_start(dst[:, n % 4, :, :].rearrange("p h k -> p (h k)"),
                         cache[bass.ds(idx, 1), :, :].rearrange("o p n -> p (o n)")).then_inc(s[n % 4], 16)

        vb = BLOCK0["v"]
        stream(kb, vb)
        sp.wait_ge(blk, BLOCK0["k"])
        for n in range(4):
            page(n, kcache, ktile, kp_in)
        for m in range(8 + RAW):
            b = vb + m
            sp.wait_ge(w_lo, b + 1 - RAW)
            sp.dma_start(raw[:, b % RAW, :], wblk[b, :, :]).then_inc(raw_in[b % RAW], 16)
            for n in range(4 + 2 * (m - 3), 6 + 2 * (m - 3)):
                if 4 <= n < NB * PAGES:
                    sp.wait_ge(ss_mm, n - 3)
                    page(n, kcache, ktile, kp_in)
        sp.wait_ge(kq_s, 16)
        sp.dma_start(kt_out, kT[:, :, :]).then_inc(kv_out, 16)
        sp.wait_ge(taken, TILE0["v"] + AH)
        sp.dma_start(vt_out, vT[:, :, :]).then_inc(kv_out, 16)
        for n in range(NB * PAGES):
            if n >= 4:
                sp.wait_ge(sv_mm, n - 3)
            page(n, vcache, vtile, vp_in)
        stream(ob, NBLK)
        for m in range(KT):
            sp.wait_ge(h_n, 24 + m + 1)
            sp.dma_start(y_t[:, m, :], hT[:, m, :]).then_inc(y_out, 16)
        sp.wait_ge(st_out, 32)
        sp.wait_ge(fin_out, 16 * NG)
        for i in range(2):
            sp.wait_ge(hs_out[i], 16 * NPAIR // 2)
        sp.wait_ge(kv_out, 32)
        sp.wait_ge(y_out, 16 * KT)

    @block.gpsimd
    def _(pool):
        def split(i, s, first):
            d = s % SPL
            pool.wait_ge(raw_in[s], i * 16 + 16)
            if not (first and s < SPL):
                pool.wait_ge(blk, i * RAW + (s + 1 - SPL))
            pool.tensor_tensor(wH[:, d, :].rearrange("p (k n) -> p k n", k=8),
                               raw[:, s, :].rearrange("p (k n) -> p k n", k=8),
                               cst[:, C_ONE:C_ONE + 1, :].broadcast_to([P, 8, P]), ALU.mult).then_inc(w_hi, 1)
            pool.wait_ge(w_hi, i * RAW + (s + 1))
            pool.tensor_tensor(wL[:, d, :], raw[:, s, :], wH[:, d, :].bitcast(F32), ALU.subtract).then_inc(w_lo, 1)

        pool.wait_ge(in_par, 48)
        def stream(a, b):
            while a < b and (a % RAW or a == 0 or b - a < RAW):
                n = RAW if a == 0 else 1
                for j in range(n):
                    split((a + j) // RAW, (a + j) % RAW, a == 0)
                a += n
            m = (b - a) // RAW
            if m > 1:
                with pool.Fori(a // RAW, a // RAW + m) as i:
                    for s in range(RAW):
                        split(i, s, False)
                a += m * RAW
            for j in range(a, b):
                split(j // RAW, j % RAW, False)

        def scale_output(p):
            pool.wait_ge(rp_s, p + 1)
            for m in range(KT):
                pool.tensor_tensor(fT[:, m, :], fT[:, m, :], rpost[:, :], ALU.mult).then_inc(fr_s, 1)

        at_ = 0
        for p, nxt in enumerate(("up0a", "q", "up1a")):
            stream(at_, BLOCK0[nxt] + SPL)
            at_ = BLOCK0[nxt] + SPL
            scale_output(p)
        stream(at_, NBLK)
        scale_output(3)

    @block.tensor
    def _(pe):
        def three(out, lh, ll, rh, rl, first, last):
            pe.matmul(out, lh, rh, start=first, stop=False)
            pe.matmul(out, lh, rl, start=False, stop=False)
            return pe.matmul(out, ll, rh, start=False, stop=last)

        def tile(name, m, b, inH, inL, wait_taken, each_k=None):
            nk = BLOCKS[name]
            par = m[1]
            if wait_taken:
                pe.wait_ge(taken, m[0] - 1)
            for kb in range(nk):
                d = (b[1] + kb) % SPL
                pe.wait_ge(w_lo, b[0] + kb + 1)
                for k in range(8):
                    if each_k is not None:
                        each_k(kb * 8 + k)
                    for h in range(2):
                        o_ = G[2 * par + h][:, 0:HALF]
                        lh, ll = wH[:, d, k * P:(k + 1) * P], wL[:, d, k * P:(k + 1) * P]
                        kk = kb * 8 + k
                        ins = three(o_, lh, ll, inH[:, kk, HV[h]], inL[:, kk, HV[h]],
                                    kb == 0 and k == 0, kb == nk - 1 and k == 7)
                ins.then_inc(blk, 1)

        def gemm(name, inH, inL, after=None, each_k=None):
            n = dict((a, b) for a, b, _ in GEMMS)[name]
            nk, m0, b0 = BLOCKS[name], TILE0[name], BLOCK0[name]

            def one(m, hook=None):
                tile(name, (m0 + m, (m0 + m) % 2), (b0 + m * nk, b0 + m * nk), inH, inL, m0 + m >= 2, hook)

            if after is not None:
                for m in range(n):
                    one(m, each_k if m == 0 else None)
                    after(m)
                return
            one(0, each_k)
            one(1)
            with pe.Fori(1, n // 2) as i:
                for u in range(2):
                    tile(name, (i * 2 + (m0 + u), (m0 + u) % 2), (i * (2 * nk) + (b0 + u * nk), b0 + u * nk),
                         inH, inL, True)

        pe.wait_ge(in_par, 48)
        pe.wait_ge(sq0, 1)
        for h in range(2):
            for t in range(KT):
                ins = pe.matmul(W[h][:, 0:HALF], cc(C_ONE), sq8[:, t, HV[h]], start=t == 0, stop=t == KT - 1)
        ins.then_inc(mm0, 1)
        pe.wait_ge(wd_s, 1)
        pe.wait_ge(alo, KT)
        for c in range(NCH + 1):
            n = P if c < NCH else NB
            ts = slice(c * P, c * P + n)
            for k in range(KT):
                ins = three(W[2][0:n, c * 32:c * 32 + 32], aH[:, k, ts], aL[:, k, ts], wdh[:, k, :], wdl[:, k, :],
                            k == 0, k == KT - 1)
        ins.then_inc(dt_mm, 1)
        pe.wait_ge(adt_s, 1)
        pe.matmul(W[3][:, 0:P], cc(C_ONE), adt[:, 0:P], start=True, stop=True)
        pe.matmul(W[3][:, P:2 * P], cc(C_SL), adt[:, 0:P], start=True, stop=True)
        for j, src in ((2, adt), (3, dtt)):
            for h in range(NH_SSD):
                e, q = 64 * (h % 2), h // 2
                ins = pe.matmul(W[3][e:e + 64, j * P + q * NB:j * P + q * NB + NB],
                                src[0:NB, P + h:P + h + 1].broadcast_to([NB, 64]), cst[0:NB, C_ID, 0:NB],
                                start=True, stop=True)
        ins.then_inc(dex_mm, 1)

        gemm("xbc", aH, aL)

        def seg_sum(k):
            pe.wait_ge(ua_s, k + 1)
            if k >= 2:
                pe.wait_ge(sg_s, k - 1)
            pe.matmul(W[k % 2][:, :], cc(C_SL), uadt[:, k % 2, :], start=True, stop=True)
            n, e = k // 2, 64 * (k % 2)
            if n >= 2 and e == 0:
                pe.wait_ge(y_s, n - 1)
            pe.matmul(W[2 + n % 2][e:e + 64, :], cst[:, C_ONE, 0:64], uadt[:, k % 2, :], start=True, stop=True
                      ).then_inc(sg_mm, 1)

        for g in range(NG):
            pe.wait_ge(pss, 1)
            pe.wait_ge(dex_s, 1)
            for c in range(NCH):
                n = g * NCH + c
                if n >= 2:
                    pe.wait_ge(tr_x, n - 1)
                if n < 2:
                    pe.wait_ge(sil, NCONV)
                elif c == 0:
                    pe.wait_ge(y_s, g * 4)
                for q in range(4):
                    ins = pe.transpose(W[c % 2][:, q * P:(q + 1) * P], yT[:, 4 * g + q, c * P:(c + 1) * P], cc(C_ID))
                ins.then_inc(tr_mm, 1)
            for c in range(NCH):
                ins = pe.transpose(W[2][:, c * P:(c + 1) * P], bcT[:, g, c * P:(c + 1) * P], cc(C_ID))
            ins.then_inc(bt_mm, 1)
            for c in range(NCH):
                ins = pe.matmul(W[3][:, c * P:(c + 1) * P], bcT[:, g, c * P:(c + 1) * P],
                                bcT[:, 4 + g, c * P:(c + 1) * P], start=True, stop=True)
            ins.then_inc(cb_mm, 1)
            pe.wait_ge(bt_s, g + 1)
            for c in range(NCH):
                pe.wait_ge(tr_x, g * NCH + NCH)
                if c >= 2:
                    pe.wait_ge(h_s, g * NCH + c - 1)
                pe.matmul(W[c % 2][:, :], btok[:, c, :], xde[:, c, :], start=True, stop=True).then_inc(st_mm, 1)
            pe.wait_ge(h_s, (g + 1) * NCH)
            pe.wait_ge(cb_s, g + 1)
            seg_sum(8 * g)
            for q in range(4):
                n = 4 * g + q
                if n >= 2:
                    pe.wait_ge(y_s, n - 1)
                for c in range(1, NCH):
                    ins = pe.matmul(G[2 + n % 2][:, c * P:(c + 1) * P], hst[:, c - 1, q * P:(q + 1) * P],
                                    bcT[:, 4 + g, c * P:(c + 1) * P], start=True, stop=True)
                ins.then_inc(yo_mm, 1)
                for e in range(2):
                    k = 2 * n + e
                    if k % 8 < 7:
                        seg_sum(k + 1)
                    pe.wait_ge(md_s, k + 1)
                    for c in range(NCH):
                        ins = pe.matmul(G[n % 2][64 * e:64 * e + 64, c * P:(c + 1) * P],
                                        xdt[:, c, (2 * q + e) * 64:(2 * q + e) * 64 + 64],
                                        mm_[:, k % 2, c * P:(c + 1) * P], start=True, stop=True)
                    ins.then_inc(yd_mm, 1)

        def z_after(m):
            if m % 4 == 0:
                g = m // 4
                if g == 0:
                    pe.wait_ge(y_s, NPAIR)
                else:
                    pe.wait_ge(bc_s, 4 * g)
                for j in range(2):
                    for hf in range(2):
                        for b in range(4):
                            ins = pe.matmul(W[2 * j + hf][:, b * P:(b + 1) * P],
                                            bcT[:, 4 * j + g, SEQ + 4 * hf + b:SEQ + 4 * hf + b + 1].broadcast_to([P, P]),
                                            cc(C_ID), start=True, stop=True)
                ins.then_inc(bc_mm, 1)

        z_after(0)
        gemm("z", aH, aL, after=lambda m: z_after(m + 1) if m < 15 else None)
        for g in range(NG):
            pe.wait_ge(z_gs, 3 * NG)
            if g:
                pe.wait_ge(g_r, g)
            for h in range(2):
                ins = pe.matmul(W[h][:, 0:HALF], cc(C_ONE), gs[:, g, HV[h]], start=True, stop=True)
            ins.then_inc(g_mm, 1)
        gemm("out", hH, hL, each_k=lambda k: pe.wait_ge(g_lo, k + 1))

        def post_sum(p):
            pe.wait_ge(accf, 8 * p + 8)
            for h in range(2):
                ins = pe.matmul(W[h][:, 0:HALF], cc(C_ONE), acc[:, HV[h]], start=True, stop=True)
            ins.then_inc(ps_mm, 1)

        def next_k(p):
            def each(k):
                pe.wait_ge(sqh, 8 * p + k + 1)
                for h in range(2):
                    ins = pe.matmul(W[2 + h][:, 0:HALF], cc(C_ONE), sqt[:, k % 2, HV[h]], start=k == 0, stop=k == 7)
                ins.then_inc(pr_mm, 1)
                pe.wait_ge(alo, KT + 8 * p + k + 1)
            return each

        def mlp(l):
            for v, s in enumerate("ab"):
                gemm(f"up{l}{s}", aH, aL, each_k=next_k(2 * l) if v == 0 else None)
                gemm(f"down{l}{s}", hH, hL, each_k=lambda k: pe.wait_ge(u_lo, 32 * l + 16 * v + k + 1))

        post_sum(0)
        mlp(0)
        post_sum(1)

        def rotate(n):
            src = qT if n < 8 else kT
            pe.wait_ge(taken, TILE0["q"] + (n // 8 + 1) * 8)
            if n:
                pe.wait_ge(kq_s, n)
            for h in range(2):
                ins = pe.matmul(W[h][:, 0:HALF], cc(C_PERM), src[:, n % 8, HV[h]], start=True, stop=True)
            ins.then_inc(rt_mm, 1)

        def page_scores(b):
            pe.wait_ge(qz_s, 1)
            for pg in range(PAGES):
                n = PAGES * b + pg
                pe.wait_ge(kp_in[n % 4], 16 * (n // 4 + 1))
                for h in range(AH):
                    c = pg * P + (h * NB + b) * 2
                    ins = pe.matmul(W[2][:, c:c + 2], ktile[:, n % 4, h, :], qz[:, h, b, :], start=True, stop=True)
                ins.then_inc(ss_mm, 1)

        gemm("q", aH, aL, each_k=next_k(1))
        pe.wait_ge(r_s, 2)
        pe.wait_ge(lm_s, 1)
        pe.matmul(W[3][:, 0:2], cc(C_ONE), misc[:, 0:2], start=True, stop=True).then_inc(lm_mm, 1)
        gemm("k", hH, hL, after=rotate, each_k=lambda k: pe.wait_ge(qlo, k + 1))

        def v_after(m):
            rotate(8 + m)
            page_scores(m)

        gemm("v", hH, hL, after=v_after)
        pe.wait_ge(st_s, 1)
        pe.wait_ge(lm_e, 1)
        pe.wait_ge(kz_s, 2)
        for pg in range(PAGES):
            pe.transpose(W[3][:, pg * P:(pg + 1) * P], sT[:, pg, :], cc(C_ID))
        pe.matmul(W[3][:, 256:257], kz[:, :, :, :].rearrange("p h b j -> p (h b j)"), cst[:, C_ONE, 0:1],
                  start=True, stop=True).then_inc(s2_mm, 1)
        for h in range(AH):
            pe.wait_ge(taken, TILE0["v"] + AH)
            if h >= 2:
                pe.wait_ge(vk_s, h - 1)
            for c in range(NCH):
                ins = pe.transpose(W[h % 2][:, c * P:(c + 1) * P], vT[:, h, c * P:(c + 1) * P], cc(C_ID))
            ins.then_inc(vt_mm, 1)
        pe.wait_ge(cm_s, 1)
        for pg in range(PAGES):
            pe.matmul(W[2][:, pg * 64:(pg + 1) * 64], sE[:, pg * P:(pg + 1) * P], cmb[:, :], start=True, stop=True)
        pe.matmul(W[2][:, 128:192], sE[:, 256:257].broadcast_to([P, P]), cmb[:, :], start=True, stop=True
                  ).then_inc(sa_mm, 1)

        def scores(n):
            h, i = divmod(n, NCH)
            w = (i + 1) * P
            if n >= 2:
                pe.wait_ge(ex_s, 2 * (n - 1))
            for j in range(2):
                ins = pe.matmul(G[2 * (n % 2) + j][:, 0:w], qT[64 * j:64 * j + 64, h, i * P:(i + 1) * P],
                                kT[64 * j:64 * j + 64, h, 0:w], start=True, stop=True)
            ins.then_inc(sc_mm, 1)

        def turn(n):
            pe.wait_ge(att_s, n + 1)
            if n >= 2:
                pe.wait_ge(at_s, n - 1)
            for kb in range(n % NCH + 1):
                ins = pe.transpose(W[n % 2][:, kb * P:(kb + 1) * P], pr[:, n % 4, 0, kb * P:(kb + 1) * P], cc(C_ID))
            ins.then_inc(at_mm, 1)

        def values(n):
            h, i = divmod(n, NCH)
            pe.wait_ge(at_s, n + 1)
            if n:
                pe.wait_ge(o_s, n)
            for kb in range(i + 1):
                ins = pe.matmul(W[2][:, 0:P], vtok[:, kb, h * P:(h + 1) * P], attT[:, n % 4, kb * P:(kb + 1) * P],
                                start=kb == 0, stop=kb == i)
            ins.then_inc(av_mm, 1)

        def page_values(n):
            b, pg = divmod(n, PAGES)
            pe.wait_ge(vp_in[n % 4], 16 * (n // 4 + 1))
            for h in range(AH):
                c = h * NB + b
                ins = pe.matmul(W[3][:, pg * 64 + c:pg * 64 + c + 1], vtile[:, n % 4, h, :], satt[:, pg, c:c + 1],
                                start=True, stop=True)
            ins.then_inc(sv_mm, 1)

        pe.wait_ge(vk_s, AH)
        pe.wait_ge(sa_s, 1)
        for n in range(AH * NCH + 3):
            if n < AH * NCH:
                scores(n)
            if 2 <= n < AH * NCH + 2:
                turn(n - 2)
            if n >= 3:
                values(n - 3)
            if n % 2 and n // 2 < NB * PAGES:
                page_values(n // 2)
        for h in range(AH):
            pe.wait_ge(oq_s, h + 1)
            if h >= 2:
                pe.wait_ge(or_s, h - 1)
            for v in range(2):
                ins = pe.matmul(GP[h % 2][:, v, 0:HALF], cc(C_ONE), osq[:, h % 2, HV[v]], start=True, stop=True)
            ins.then_inc(on_mm, 1)
        gemm("o", aH, aL, each_k=lambda k: pe.wait_ge(olo, k + 1))
        post_sum(2)
        mlp(1)
        post_sum(3)

    @block.scalar
    def _(sc):
        own = Own(sc, act)
        A = sc.activation

        def rsqrt(dst, banks, n, signal):
            own(A(dst.rearrange("p (v t) -> p v t", v=2), banks[:, :, 0:HALF], ACT.Ln, scale=1.0 / n,
                  bias=misc[:, 8:9]))
            A(dst, dst, ACT.Exp, scale=-0.5).then_inc(signal, 1)

        LN_EXP = "natural_log_exp_and_others"
        sc.preload_act_table_set(LN_EXP)
        sc.wait_ge(in_x, 16)
        A(sq8[:, :, :], hT[:, :, :], ACT.Square).then_inc(sq0, 1)
        sc.wait_ge(mm0, 1)
        sc.wait_ge(wd_s, 1)
        rsqrt(rpre[:, :], WP[0], D, r0)
        sc.wait_ge(in_par, 48)
        own(A(ea[:, :], pc("a_log", 0, 32), ACT.Exp))
        for t in range(KT):
            sc.wait_ge(ax, t + 1)
            A(aH[:, t, :], sq8[:, t, :], ACT.Copy).then_inc(ahi, 1)
        sc.wait_ge(dt_u, 1)
        own(A(dtl[:, :], dtu[:, :], ACT.Abs))
        own(A(dtl[:, :], dtl[:, :], ACT.Exp, scale=-1.0))
        A(dtl[:, :], dtl[:, :], ACT.Ln, bias=misc[:, 9:10]).then_inc(dt_l, 1)
        sc.wait_ge(dex_mm, 1)
        own(A(dtx[:, :, :].rearrange("p q b -> p (q b)"), W[3][:, 3 * P:4 * P], ACT.Copy))
        A(dex[:, :, :].rearrange("p q b -> p (q b)"), W[3][:, 0:3 * P], ACT.Exp).then_inc(dex_s, 1)

        def silu_tile(m):
            sc.wait_ge(cv, m + 1)
            dst = bcT[:, m, 0:SEQ] if m < 8 else yT[:, m - 8, 0:SEQ]
            A(dst, cacc[:, m % 2, :], ACT.Silu).then_inc(sil, 1)

        sc.wait_ge(xz, 1)
        for m in range(NCONV):
            sc.wait_ge(blk, m + 1)
            if m >= 2:
                sc.wait_ge(cv, m - 1)
            g = 2 * (m % 2)
            A(xr[:, m % 2, 3:3 + HALF], G[g][:, 0:HALF], ACT.Copy).then_inc(xr_in, 1)
            A(xr[:, m % 2, 3 + HALF:3 + SEQ], G[g + 1][:, 0:SEQ - HALF], ACT.Copy).then_inc(xr_in, 1)
            A(xs4[:, m, :, 3], G[g + 1][:, SEQ - HALF:HALF], ACT.Copy).then_inc(taken, 1)
            if m:
                silu_tile(m - 1)
        silu_tile(NCONV - 1)
        sc.wait_ge(scv, 1)
        own(A(bcT[:, :, SEQ:T], xsc[:, 0:8, :], ACT.Silu))
        A(yT[:, :, SEQ:T], xsc[:, 8:NCONV, :], ACT.Silu).then_inc(pss, 1)

        sc.preload_act_table_set(LN_EXP)
        for g in range(NG):
            sc.wait_ge(bt_mm, g + 1)
            A(btok[:, :, :].rearrange("p c n -> p (c n)"), W[2][:, :], ACT.Copy).then_inc(bt_s, 1)
            for q in range(4):
                n = 4 * g + q
                for k in range(2 * n, 2 * n + 2):
                    sc.wait_ge(sg_mm, k + 1)
                    if k >= 2:
                        sc.wait_ge(md_s, k - 1)
                    A(seg[:, k % 2, :], W[k % 2][:, :], ACT.Exp).then_inc(sg_s, 1)
                if n >= 2:
                    sc.wait_ge(y_s, n - 1)
                A(ebc[:, n % 2, :], W[2 + n % 2][:, :], ACT.Exp).then_inc(eb_s, 1)

        for m in range(NPAIR):
            if m % 4 == 0:
                g = m // 4
                sc.wait_ge(bc_mm, g + 1)
                if g:
                    sc.wait_ge(ys_s, 4 * g)
                else:
                    sc.wait_ge(y_s, NPAIR)
                    sc.wait_ge(fin_out, 16 * NG)
                for j, dst in enumerate((bbc, cbc)):
                    for hf in range(2):
                        A(dst[:, 4 * hf:4 * hf + 4, :].rearrange("p b n -> p (b n)"), W[2 * j + hf][:, :],
                          ACT.Copy).then_inc(bc_s, 1)
            sc.wait_ge(blk, BLOCK0["z"] + m + 1)
            if m >= 2:
                sc.wait_ge(z_g, m - 1)
            gb = 2 * ((TILE0["z"] + m) % 2)
            A(zs[:, m % 2, HV[0]], G[gb][:, 0:HALF], ACT.Silu)
            A(zs[:, m % 2, HV[1]], G[gb + 1][:, 0:HALF], ACT.Silu).then_inc(taken, 1)
            if m:
                gate_sq(sc, m - 1)
        gate_sq(sc, NPAIR - 1)
        sc.preload_act_table_set(LN_EXP)
        for g in range(NG):
            sc.wait_ge(g_mm, g + 1)
            if g == 0:
                sc.wait_ge(z_gs, 3 * NG)
                sc.wait_ge(ys_s, NPAIR)
            rsqrt(rg[:, g, :], WP[0], 512, g_r)
        for q in range(NPAIR):
            sc.wait_ge(g_n, q + 1)
            A(hH[:, q, :], yT[:, q, :], ACT.Copy).then_inc(g_hi, 1)

        def boundary(p, gpre, own_f):
            for m in range(KT):
                if own_f:
                    nm = {0: "out", 2: "o"}[p]
                    gb = 2 * ((TILE0[nm] + m) % 2)
                    sc.wait_ge(blk, BLOCK0[nm] + BLOCKS[nm] * (m + 1))
                    A(fT[:, m, HV[0]], G[gb][:, 0:HALF], ACT.Copy)
                    A(fT[:, m, HV[1]], G[gb + 1][:, 0:HALF], ACT.Copy).then_inc(taken, 1)
                    sc.wait_ge(taken, TILE0[nm] + m + 1)
                else:
                    sc.wait_ge(f_s, 8 * (p // 2) + m + 1)
                if m >= 2:
                    sc.wait_ge(accf, 8 * p + m - 1)
                A(sqt[:, m % 2, :], fT[:, m, :], ACT.Square).then_inc(sqf, 1)
            sc.wait_ge(ps_mm, p + 1)
            rsqrt(rpost[:, :], WP[0], D, rp_s)
            if p == 3:
                return
            for m in range(KT):
                sc.wait_ge(h_n, 8 * p + m + 1)
                A(aH[:, m, :], hT[:, m, :], ACT.Copy, scale=pc(gpre, m)).then_inc(ahi, 1)
                if m >= 2:
                    sc.wait_ge(pr_mm, 8 * p + m - 1)
                A(sqt[:, m % 2, :], hT[:, m, :], ACT.Square).then_inc(sqh, 1)
            if p == 1:
                for m in range(KT):
                    A(hH[:, m, :], hT[:, m, :], ACT.Copy, scale=pc("kv", m)).then_inc(qhi, 1)
            sc.wait_ge(pr_mm, 8 * p + 8)
            rsqrt(rpre[:, :], WP[1], D, r_s)

        def mlp(l):
            for v, s in enumerate("ab"):
                name = f"up{l}{s}"
                for m in range(16):
                    n = 32 * l + 16 * v + m
                    gb = 2 * ((TILE0[name] + m) % 2)
                    sc.wait_ge(blk, BLOCK0[name] + m + 1)
                    if n >= 2:
                        sc.wait_ge(u_sq, n - 1)
                    sc.wait_ge(taken, TILE0[name] + m)
                    A(rel[:, m % 2, HV[0]], G[gb][:, 0:HALF], ACT.Relu)
                    A(rel[:, m % 2, HV[1]], G[gb + 1][:, 0:HALF], ACT.Relu).then_inc(taken, 1)
                    if m:
                        hidden_hi(n - 1, m - 1)
                hidden_hi(32 * l + 16 * v + 15, 15)

        def hidden_hi(n, m):
            sc.wait_ge(u_sq, n + 1)
            A(hH[:, m, :], rsq[:, m % 2, :], ACT.Copy).then_inc(u_hi, 1)

        boundary(0, "mlp_pre0", True)
        mlp(0)
        boundary(1, "attn_pre", False)
        for n in range(16):
            nm, dst = ("q", qT) if n < 8 else ("k", kT)
            if n == 8:
                sc.wait_ge(lm_mm, 1)
                A(misc[:, 2:4], W[3][:, 0:2], ACT.Exp).then_inc(lm_e, 1)
            m = n % 8
            gb = 2 * ((TILE0[nm] + m) % 2)
            sc.wait_ge(blk, BLOCK0[nm] + m + 1)
            A(dst[:, m, HV[0]], G[gb][:, 0:HALF], ACT.Copy)
            A(dst[:, m, HV[1]], G[gb + 1][:, 0:HALF], ACT.Copy).then_inc(taken, 1)
        sc.wait_ge(ss_mm, NB * PAGES)
        A(sT[:, :, :].rearrange("p g c -> p (g c)"), W[2][:, 0:2 * P], ACT.Copy).then_inc(st_s, 1)

        def vtok_copy(h):
            sc.wait_ge(vt_mm, h + 1)
            A(vtok[:, :, h * P:(h + 1) * P], W[h % 2][:, :].rearrange("p (c n) -> p c n", c=NCH), ACT.Copy
              ).then_inc(vk_s, 1)

        for h in range(2):
            vtok_copy(h)
        sc.wait_ge(s2_s, 1)
        A(sE[:, :], W[3][:, 0:257], ACT.Exp, scale=QK_SCALE, bias=misc[:, 41:42], accum_out=misc[:, 42:43]
          ).then_inc(sx_s, 1)
        for h in range(2, AH):
            vtok_copy(h)
        sc.wait_ge(sa_mm, 1)
        A(satt[:, :, :].rearrange("p g c -> p (g c)"), W[2][:, 0:128], ACT.Copy)
        A(snb[:, :], W[2][:, 128:192], ACT.Copy).then_inc(sa_s, 1)

        def attT_copy(n):
            w = (n % NCH + 1) * P
            sc.wait_ge(at_mm, n + 1)
            if n >= 4:
                sc.wait_ge(av_mm, n - 3)
            A(attT[:, n % 4, 0:w], W[n % 2][:, 0:w], ACT.Copy).then_inc(at_s, 1)

        for n in range(AH * NCH + 2):
            if n < AH * NCH:
                w = (n % NCH + 1) * P
                sc.wait_ge(mx_s, n + 1)
                if n >= 4:
                    sc.wait_ge(at_mm, n - 3)
                for j in range(2):
                    A(pr[:, n % 4, j, 0:w], G[2 * (n % 2) + j][:, 0:w], ACT.Exp, scale=QK_SCALE,
                      bias=misc[:, 20 + 2 * (n % 2) + j:21 + 2 * (n % 2) + j],
                      accum_out=misc[:, 30 + 2 * (n % 2) + j:31 + 2 * (n % 2) + j]).then_inc(ex_s, 1)
            if n >= 2:
                attT_copy(n - 2)
        sc.wait_ge(os_s, 1)
        for h in range(AH):
            if h >= 2:
                sc.wait_ge(on_mm, h - 1)
            A(osq[:, h % 2, :], oT[:, h, :], ACT.Square).then_inc(oq_s, 1)
            if h:
                sub_norm(h - 1, rsqrt)
        sub_norm(AH - 1, rsqrt)
        for h in range(AH):
            sc.wait_ge(ox_s, h + 1)
            if h == 0:
                sc.wait_ge(or_s, AH)
                sc.wait_ge(ox_s, AH)
            A(aH[:, h, :], onm[:, h, :], ACT.Copy).then_inc(ohi, 1)
        boundary(2, "mlp_pre1", True)
        mlp(1)
        boundary(3, None, False)






    @block.vector
    def _(v):
        own = Own(v, dve)
        TT, STT, TS = v.tensor_tensor, v.scalar_tensor_tensor, v.tensor_scalar

        own(v.memset(misc[:, 8:9], EPS))
        own(v.memset(misc[:, 9:10], 1.0))
        own(v.memset(dtu[:, :], 0.0))
        v.wait_ge(in_par, 48)
        own(v.tensor_copy(wdh[:, :, :], wdr[:, :, :]))
        TT(wdl[:, :, :], wdr[:, :, :], wdh[:, :, :].bitcast(F32), ALU.subtract).then_inc(wd_s, 1)
        own(v.memset(xr[:, 0, 0:3], 0.0))
        v.memset(xr[:, 1, 0:3], 0.0).then_inc(xz, 1)
        v.wait_ge(r0, 1)

        def first_lo(t):
            v.wait_ge(ahi, t + 1)
            TT(aL[:, t, :], sq8[:, t, :], aH[:, t, :].bitcast(F32), ALU.subtract).then_inc(alo, 1)

        for t in range(KT):
            STT(sq8[:, t, :], hT[:, t, :], pc("ssd_pre", t), rpre[:, :], ALU.mult, ALU.mult).then_inc(ax, 1)
            v.wait_ge(ax, t + 1)
            if t:
                first_lo(t - 1)
        first_lo(KT - 1)
        v.wait_ge(dt_mm, 1)
        own(TT(dtu[:, 0:P].rearrange("p (c h) -> p c h", c=NCH), W[2][:, 0:P].rearrange("p (c h) -> p c h", c=NCH),
               pc("dt_bias", 0, 32).unsqueeze(1).broadcast_to([P, NCH, 32]), ALU.add))
        TT(dtu[0:NB, P:P + 32], W[2][0:NB, P:P + 32], pv[0:NB, PV["dt_bias"][0]:PV["dt_bias"][1]], ALU.add
           ).then_inc(dt_u, 1)
        v.wait_ge(dt_l, 1)
        own(STT(dtt[:, :], dtu[:, :], 0.0, dtl[:, :], ALU.max, ALU.add))
        STT(adt[:, :].rearrange("p (c h) -> p c h", c=5), dtt[:, :].rearrange("p (c h) -> p c h", c=5), -1.0,
            ea[:, :].unsqueeze(1).broadcast_to([P, 5, 32]), ALU.mult, ALU.mult).then_inc(adt_s, 1)

        for m in range(NCONV):
            v.wait_ge(xr_in, 2 * m + 2)
            if m >= 2:
                v.wait_ge(sil, m - 1)
            a = cacc[:, m % 2, :]
            own(v.tensor_copy(pcv[:, m, :], xr[:, m % 2, SEQ:SEQ + 3]))
            own(TS(a, xr[:, m % 2, 0:SEQ], pc("conv_w", m), pc("conv_b", m), ALU.mult, ALU.add))
            for k in (1, 2, 3):
                ins = STT(a, xr[:, m % 2, k:k + SEQ], pc("conv_w", 24 * k + m), a, ALU.mult, ALU.add)
                own(ins) if k < 3 else ins.then_inc(cv, 1)
        v.wait_ge(cs_in, 16)
        v.wait_ge(taken, NCONV)
        for k in range(4):
            ins = TT(xsm[:, :, :, k], xs4[:, :, :, k],
                     pc("conv_w", 24 * k, 24).unsqueeze(2).broadcast_to([P, NCONV, NB]), ALU.mult)
            own(ins)
        own(v.tensor_reduce(xsc[:, :, :], xsm[:, :, :, :], AXX, ALU.add))
        TT(xsc[:, :, :], xsc[:, :, :], pc("conv_b", 0, 24).unsqueeze(2).broadcast_to([P, NCONV, NB]), ALU.add
           ).then_inc(scv, 1)
        v.wait_ge(pss, 1)
        v.wait_ge(dex_s, 1)
        own(TT(sdx[:, :, :], yT[:, :, SEQ:T], dtx[:, :, :], ALU.mult))

        dtb = dtt[:, 0:P].rearrange("p (c h) -> p c h", c=NCH)
        deb = dex[:, 1, :].rearrange("p (c h) -> p c h", c=NCH)
        cdb = dex[:, 0, :].rearrange("p (c h) -> p c h", c=NCH)

        def hb(src, c, g):
            return src[:, c, g * HG:(g + 1) * HG].unsqueeze(2).broadcast_to([P, HG, 64])

        def r8(ap):
            return ap.rearrange("p (h e) -> p h e", h=HG)

        for g in range(NG):
            if g:
                v.wait_ge(yd_mm, 8 * g)
                v.wait_ge(fin_out, 16 * g)
            for c in range(NCH):
                v.wait_ge(tr_mm, g * NCH + c + 1)
                own(TT(r8(xdt[:, c, :]), r8(W[c % 2][:, :]), hb(dtb, c, g), ALU.mult))
                TT(r8(xde[:, c, :]), r8(xdt[:, c, :]), hb(deb, c, g), ALU.mult).then_inc(tr_x, 1)
            v.wait_ge(cb_mm, g + 1)
            TT(cbm[:, :, :], W[3][:, :].rearrange("p (c l) -> p c l", c=NCH),
               cst[:, C_UP:C_UP + 1, :].broadcast_to([P, NCH, P]), ALU.mult).then_inc(cb_s, 1)
            for c in range(NCH):
                v.wait_ge(st_mm, g * NCH + c + 1)
                if c == 0:
                    v.tensor_copy(hst[:, 0, :], W[0][:, :]).then_inc(h_s, 1)
                else:
                    v.wait_ge(h_s, g * NCH + c)
                    own(TT(r8(hst[:, c, :]), r8(hst[:, c - 1, :]), hb(cdb, c, g), ALU.mult))
                    TT(hst[:, c, :], hst[:, c, :], W[c % 2][:, :], ALU.add).then_inc(h_s, 1)
            def make_uadt(k):
                if k >= 2:
                    v.wait_ge(sg_mm, k - 1)
                TT(uadt[:, k % 2, :].rearrange("p (c l) -> p c l", c=NCH),
                   cst[:, C_UP:C_UP + 1, :].broadcast_to([P, NCH, P]),
                   adt[:, 0:P].rearrange("p (c h) -> p c h", c=NCH)[:, :, k:k + 1].broadcast_to([P, NCH, P]),
                   ALU.mult).then_inc(ua_s, 1)

            if g == 0:
                make_uadt(0)
            for q in range(4):
                n = 4 * g + q
                for e in range(2):
                    k = 2 * n + e
                    if k + 1 < NH_SSD:
                        make_uadt(k + 1)
                    v.wait_ge(sg_s, k + 1)
                    if k >= 2:
                        v.wait_ge(yd_mm, k - 1)
                    TT(mm_[:, k % 2, :], seg[:, k % 2, :], cbm[:, :, :].rearrange("p c l -> p (c l)"), ALU.mult
                       ).then_inc(md_s, 1)
                v.wait_ge(eb_s, n + 1)
                v.wait_ge(yo_mm, n + 1)
                own(TT(yo[:, P:SEQ], G[2 + n % 2][:, P:SEQ], ebc[:, n % 2, P:SEQ], ALU.mult))
                v.wait_ge(yd_mm, 2 * n + 2)
                own(STT(yT[:, n, 0:SEQ], yT[:, n, 0:SEQ], pc("d", n), G[n % 2][:, :], ALU.mult, ALU.add))
                TT(yT[:, n, P:SEQ], yT[:, n, P:SEQ], yo[:, P:SEQ], ALU.add).then_inc(y_s, 1)

        for m in range(NPAIR):
            g = m // 4
            v.wait_ge(bc_s, 4 * g + 4)
            v.wait_ge(hs_in[m % 2], 16 * (m // 2 + 1))
            x = hs[:, m % 2, :, :]
            own(TT(x, x, dex[:, 2, m * NB:(m + 1) * NB].unsqueeze(2).broadcast_to([P, NB, P]), ALU.mult))
            own(TT(ht[:, :, :], bbc[:, :, :], sdx[:, m, :].unsqueeze(2).broadcast_to([P, NB, P]), ALU.mult))
            TT(x, x, ht[:, :, :], ALU.add).then_inc(hs_new, 1)
            v.wait_ge(hs_new, m + 1)
            own(TT(ht[:, :, :], x, cbc[:, :, :], ALU.mult))
            v.tensor_reduce(yss[:, m, :], ht[:, :, :], AXX, ALU.add).then_inc(ys_s, 1)
            v.wait_ge(ys_s, m + 1)
            own(STT(yT[:, m, SEQ:T], yT[:, m, SEQ:T], pc("d", m), yss[:, m, :], ALU.mult, ALU.add))
            v.wait_ge(taken, TILE0["z"] + m + 1)
            TT(yT[:, m, :], yT[:, m, :], zs[:, m % 2, :], ALU.mult).then_inc(z_g, 1)
            if m:
                gate_sum(v, own, m - 1)
        gate_sum(v, own, NPAIR - 1)
        def gate_lo(q):
            v.wait_ge(g_hi, q + 1)
            TT(hL[:, q, :], yT[:, q, :], hH[:, q, :].bitcast(F32), ALU.subtract).then_inc(g_lo, 1)

        for q in range(NPAIR):
            v.wait_ge(g_r, max(NG, q // 4 + 1))
            if q == 0:
                for i in range(2):
                    v.wait_ge(hs_out[i], 16 * NPAIR // 2)
                v.wait_ge(st_out, 32)
                v.wait_ge(fin_out, 16 * NG)
            STT(yT[:, q, :], yT[:, q, :], pc("gate", q), rg[:, q // 4, :], ALU.mult, ALU.mult).then_inc(g_n, 1)
            v.wait_ge(g_n, q + 1)
            if q:
                gate_lo(q - 1)
        gate_lo(NPAIR - 1)

        def add_sq(m, first, sem_in, sem_out, base_):
            v.wait_ge(sem_in, base_ + m + 1)
            if m == 0:
                v.tensor_copy(acc[:, :], sqt[:, 0, :]).then_inc(sem_out, 1)
            else:
                v.wait_ge(sem_out, base_ + m)
                TT(acc[:, :], acc[:, :], sqt[:, m % 2, :], ALU.add).then_inc(sem_out, 1)

        def boundary(p, gpost, gpre, own_f):
            if own_f:
                for m in range(KT):
                    add_sq(m, True, sqf, accf, 8 * p)
            def lows(m):
                v.wait_ge(ahi, KT + 8 * p + m + 1)
                STT(aL[:, m, :], hT[:, m, :], pc(gpre, m), aH[:, m, :].bitcast(F32), ALU.mult, ALU.subtract
                    ).then_inc(alo, 1)

            for m in range(KT):
                v.wait_ge(fr_s, 8 * p + m + 1)
                STT(hT[:, m, :], fT[:, m, :], pc(gpost, m), hT[:, m, :], ALU.mult, ALU.add).then_inc(h_n, 1)
                if m and p < 3:
                    lows(m - 1)
            if p < 3:
                lows(KT - 1)
            if p == 1:
                for m in range(KT):
                    v.wait_ge(qhi, m + 1)
                    STT(hL[:, m, :], hT[:, m, :], pc("kv", m), hH[:, m, :].bitcast(F32), ALU.mult,
                        ALU.subtract).then_inc(qlo, 1)

        def mlp(l):
            v.wait_ge(r_s, 2 * l + 1)
            own(TT(r2[:, :], rpre[:, :], rpre[:, :], ALU.mult))

            def hidden_lo(n, m):
                v.wait_ge(u_hi, n + 1)
                TT(hL[:, m, :], rsq[:, m % 2, :], hH[:, m, :].bitcast(F32), ALU.subtract).then_inc(u_lo, 1)

            p = 1 + 2 * l
            for w, s in enumerate("ab"):
                for m in range(16):
                    n = 32 * l + 16 * w + m
                    v.wait_ge(taken, TILE0[f"up{l}{s}"] + m + 1)
                    if n >= 2:
                        v.wait_ge(u_lo, n - 1)
                    TT(rsq[:, m % 2, :], rel[:, m % 2, :], rel[:, m % 2, :], ALU.mult).then_inc(u_sq, 1)
                    v.wait_ge(u_sq, n + 1)
                    if m:
                        hidden_lo(n - 1, m - 1)
                hidden_lo(32 * l + 16 * w + 15, 15)
                name = f"down{l}{s}"
                for m in range(KT):
                    gb = 2 * ((TILE0[name] + m) % 2)
                    v.wait_ge(blk, BLOCK0[name] + 2 * (m + 1))
                    v.wait_ge(taken, TILE0[name] + m)
                    if s == "a":
                        own(v.tensor_copy(fT[:, m, HV[0]], G[gb][:, 0:HALF]))
                        v.tensor_copy(fT[:, m, HV[1]], G[gb + 1][:, 0:HALF]).then_inc(taken, 1)
                        v.wait_ge(taken, TILE0[name] + m + 1)
                    else:
                        own(TT(fT[:, m, HV[0]], fT[:, m, HV[0]], G[gb][:, 0:HALF], ALU.add))
                        TT(fT[:, m, HV[1]], fT[:, m, HV[1]], G[gb + 1][:, 0:HALF], ALU.add).then_inc(taken, 1)
                        v.wait_ge(taken, TILE0[name] + m + 1)
                        TT(fT[:, m, :], fT[:, m, :], r2[:, :], ALU.mult).then_inc(f_s, 1)
                        v.wait_ge(f_s, 8 * (p // 2) + m + 1)
                        if m:
                            add_sq(m - 1, True, sqf, accf, 8 * p)
            add_sq(KT - 1, True, sqf, accf, 8 * p)

        boundary(0, "ssd_post", "mlp_pre0", True)
        mlp(0)
        boundary(1, "mlp_post0", "attn_pre", False)
        v.memset(misc[:, 0:2], 0.0).then_inc(lm_r, 1)
        v.wait_ge(lm_r, 1)
        lam = PV["lam"][0]
        for j in range(2):
            ins = TT(misc[:, j:j + 1], pv[:, lam + 2 * j:lam + 2 * j + 1], pv[:, lam + 2 * j + 1:lam + 2 * j + 2],
                     ALU.mult)
            own(ins) if j == 0 else ins.then_inc(lm_s, 1)
        v.wait_ge(r_s, 2)
        v.wait_ge(rp_in, 16)
        for j in range(2):
            own(TT(ropt[:, j, :], ropt[:, j, :], rpre[:, :], ALU.mult))

        def rope_tile(n):
            x = (qT if n < 8 else kT)[:, n % 8, :]
            v.wait_ge(rt_mm, n + 1)
            own(TT(rt1[:, :], x, ropt[:, 0, :], ALU.mult))
            own(TT(rt2[:, :].rearrange("p (v t) -> p v t", v=2), WP[0][:, :, 0:HALF],
                   ropt[:, 1, :].rearrange("p (v t) -> p v t", v=2), ALU.mult))
            TT(x, rt1[:, :], rt2[:, :], ALU.add).then_inc(kq_s, 1)
            v.wait_ge(kq_s, n + 1)

        for n in range(AH):
            rope_tile(n)
        for j in range(2):
            ins = TS(qz[:, :, :, j], qT[:, :, SEQ:T], pc("jsel", j), None, ALU.mult)
            own(ins) if j == 0 else ins.then_inc(qz_s, 1)
        v.wait_ge(lm_e, 1)
        own(v.memset(misc[:, 4:5], 1.0))
        own(TT(misc[:, 5:6], misc[:, 3:4], misc[:, 2:3], ALU.subtract))
        own(TS(misc[:, 5:6], misc[:, 5:6], -LAM_INIT, None, ALU.add))
        for m in range(AH):
            v.wait_ge(blk, BLOCK0["v"] + m + 1)
            v.wait_ge(taken, TILE0["v"] + m)
            TT(vT[:, m, :].rearrange("p (v t) -> p v t", v=2), GP[(TILE0["v"] + m) % 2][:, :, 0:HALF],
               rpre[:, :].rearrange("p (v t) -> p v t", v=2), ALU.mult).then_inc(taken, 1)
            rope_tile(8 + m)
        v.wait_ge(qz_s, 1)
        for j in range(2):
            TT(kz[:, :, :, j], qz[:, :, :, j], kT[:, :, SEQ:T], ALU.mult).then_inc(kz_s, 1)
        v.wait_ge(s2_mm, 1)
        own(v.tensor_reduce(misc[:, 40:41], W[3][:, 0:257], AXX, ALU.max))
        TS(misc[:, 41:42], misc[:, 40:41], -QK_SCALE, None, ALU.mult).then_inc(s2_s, 1)
        v.wait_ge(sx_s, 1)
        own(v.reciprocal(misc[:, 43:44], misc[:, 42:43]))
        own(STT(misc[:, 44:45], pc("rowj", 1), misc[:, 5:6], pc("rowj", 0), ALU.mult, ALU.add))
        TS(cmb[:, :], pc("pairsel", 0, 64), misc[:, 44:45], misc[:, 43:44], ALU.mult, ALU.mult).then_inc(cm_s, 1)

        def maxima(n):
            i, w, g = n % NCH, (n % NCH + 1) * P, GP[n % 2]
            v.wait_ge(sc_mm, n + 1)
            own(TT(g[:, :, i * P:w], g[:, :, i * P:w], cst[:, C_MASK:C_MASK + 1, :].broadcast_to([P, 2, P]), ALU.add))
            own(v.tensor_reduce(misc[:, 24 + 2 * (n % 2):26 + 2 * (n % 2)], g[:, :, 0:w], AXX, ALU.max))
            TS(misc[:, 20 + 2 * (n % 2):22 + 2 * (n % 2)], misc[:, 24 + 2 * (n % 2):26 + 2 * (n % 2)], -QK_SCALE, None,
               ALU.mult).then_inc(mx_s, 1)

        def combine(n):
            w, c = (n % NCH + 1) * P, 34 + 2 * (n % 2)
            v.wait_ge(ex_s, 2 * n + 2)
            own(v.reciprocal(misc[:, c:c + 2], misc[:, c - 4:c - 2]))
            own(TT(misc[:, c:c + 2], misc[:, c:c + 2], misc[:, 4:6], ALU.mult))
            own(TS(pr[:, n % 4, 1, 0:w], pr[:, n % 4, 1, 0:w], misc[:, c + 1:c + 2], None, ALU.mult))
            STT(pr[:, n % 4, 0, 0:w], pr[:, n % 4, 0, 0:w], misc[:, c:c + 1], pr[:, n % 4, 1, 0:w],
                ALU.mult, ALU.add).then_inc(att_s, 1)

        def take_o(n):
            h, i = divmod(n, NCH)
            v.wait_ge(av_mm, n + 1)
            v.tensor_copy(oT[:, h, i * P:(i + 1) * P], W[2][:, 0:P]).then_inc(o_s, 1)

        for n in range(AH * NCH + 3):
            if n < AH * NCH:
                maxima(n)
            if 1 <= n <= AH * NCH:
                combine(n - 1)
            if n >= 3:
                take_o(n - 3)
        v.wait_ge(sv_mm, NB * PAGES)
        own(TT(ov[:, :].rearrange("p (h b) -> p h b", h=AH), snb[:, :].rearrange("p (h b) -> p h b", h=AH),
               vT[:, :, SEQ:T], ALU.mult))
        own(TT(ov[:, :], ov[:, :], W[3][:, 0:64], ALU.add))
        TT(oT[:, :, SEQ:T], ov[:, :].rearrange("p (h b) -> p h b", h=AH),
           W[3][:, 64:128].rearrange("p (h b) -> p h b", h=AH), ALU.add).then_inc(os_s, 1)
        own(TS(misc[:, 46:47], pc("subln"), 1.0 - LAM_INIT, None, ALU.mult))
        v.wait_ge(kv_out, 32)
        for h in range(AH):
            v.wait_ge(or_s, h + 1)
            STT(onm[:, h, :], oT[:, h, :], misc[:, 46:47], orr[:, h % 2, :], ALU.mult, ALU.mult).then_inc(ox_s, 1)
        for h in range(AH):
            v.wait_ge(ohi, h + 1)
            TT(aL[:, h, :], onm[:, h, :], aH[:, h, :].bitcast(F32), ALU.subtract).then_inc(olo, 1)
        boundary(2, "attn_post", "mlp_pre1", True)
        mlp(1)
        boundary(3, "mlp_post1", None, False)

    ctx.close()


def kernel(**inputs):
    import numpy as np
    import concourse.bacc as bacc
    from concourse.bass_utils import run_bass_kernel_spmd

    f = {k: np.asarray(v) for k, v in inputs.items()}

    def blocks(w):
        k, n = w.shape
        return w.reshape(k // 1024, 8, P, n // P, P).transpose(3, 0, 2, 1, 4).reshape(-1, P, 1024)

    w_in = f["ssd_w_in"][0]
    xbc0 = 2048
    order = [w_in[:, xbc0 + 2048:xbc0 + 3072], w_in[:, xbc0:xbc0 + 2048], w_in[:, 0:2048], f["ssd_w_out"][0]]

    def mlp(l):
        up, down = f["mlp_w_up"][l], f["mlp_w_down"][l]
        return [up[:, :2048], down[:2048], up[:, 2048:], down[2048:]]

    order += mlp(0) + [f["attn_w_q"][0], f["w_kv"][:, :1024], f["w_kv"][:, 1024:], f["attn_w_o"][0]] + mlp(1)
    wblk = np.concatenate([blocks(w) for w in order])
    wdt = w_in[:, 5120:].reshape(8, P, 32).transpose(1, 0, 2)
    x_t = np.concatenate([f["x_prompt"][0], f["x_sample"][:, 0]]).reshape(T, KT, P).transpose(2, 1, 0)

    def cols(v):
        return v.reshape(-1, P).T

    def conv_order(a):
        return np.concatenate([a[16:24], a[0:16]])

    z = np.float32
    jsel = np.zeros((P, 2), z)
    jsel[:64, 0] = 1
    jsel[64:, 1] = 1
    rowj = np.zeros((P, 2), z)
    rowj[0::2, 0] = 1
    rowj[1::2, 1] = 1
    pairsel = np.kron(np.eye(64, dtype=z), np.ones((2, 1), z))
    lam = np.zeros((P, 4), z)
    for i, n in enumerate(("q1", "k1", "q2", "k2")):
        lam[:64, i] = f["attn_lambda_" + n][0]
    cw = np.concatenate([conv_order(f["ssd_conv_w"][0, k].reshape(24, P)).T for k in range(4)], 1)
    parts = {"ssd_pre": cols(f["ssd_norm_pre"][0]), "ssd_post": cols(f["ssd_norm_post"][0]), "conv_w": cw,
             "conv_b": conv_order(f["ssd_conv_b"][0].reshape(24, P)).T, "gate": cols(f["ssd_gate_norm"][0]),
             "mlp_pre0": cols(f["mlp_norm_pre"][0]), "mlp_pre1": cols(f["mlp_norm_pre"][1]),
             "mlp_post0": cols(f["mlp_norm_post"][0]), "mlp_post1": cols(f["mlp_norm_post"][1]),
             "kv": cols(f["kv_norm"]), "attn_pre": cols(f["attn_norm_pre"][0]), "attn_post": cols(f["attn_norm_post"][0]),
             "subln": cols(f["attn_subln"][0]), "d": cols(np.repeat(f["ssd_d"][0], 64)), "jsel": jsel,
             "pairsel": pairsel, "rowj": rowj, "lam": lam,
             "dt_bias": np.broadcast_to(f["ssd_dt_bias"][0], (P, 32)), "a_log": np.broadcast_to(f["ssd_a_log"][0], (P, 32))}
    pvec = np.concatenate([parts[n] for n in PV], 1)
    up = np.triu(np.ones((P, P), z))
    perm = np.zeros((P, P), z)
    for h in (0, 64):
        for i in range(8):
            perm[h + 8 + i, h + i] = -1
            perm[h + i, h + 8 + i] = 1
    consts = np.stack([np.eye(P, dtype=z), np.ones((P, P), z), up, np.tril(np.ones((P, P), z), -1),
                       np.triu(np.full((P, P), -3e38, z), 1), perm], 1)
    pos = np.concatenate([np.arange(SEQ), np.full(NB, 256)]).astype(z)
    inv = (z(500000.0) ** (-np.arange(0, 16, 2, dtype=z) / z(16))).astype(z)
    ang = inv[:, None] * pos[None, :]
    rope = np.zeros((P, 2, T), z)
    rope[:, 0] = 1
    for h in (0, 8, 64, 72):
        rope[h:h + 8, 0] = np.cos(ang)
        rope[h:h + 8, 1] = np.sin(ang)
    ssm_in = f["state_ssm"][0].reshape(NB, NPAIR, P, P).transpose(1, 2, 0, 3)
    conv_in = conv_order(f["state_conv"][0].reshape(NB, 3, 24, P).transpose(2, 3, 0, 1)).transpose(1, 0, 2, 3)
    npg = f["cache_k"].shape[0]
    kcache = f["cache_k"].transpose(0, 3, 2, 1).reshape(npg, P, 1024)
    vcache = f["cache_v"].reshape(npg, P, 1024)
    ins = {"wblk": wblk, "wdt": wdt, "x_t": x_t, "pvec": pvec, "consts": consts, "rope": rope, "ssm_in": ssm_in,
           "conv_in": conv_in, "kcache": kcache, "vcache": vcache, "ptab": f["page_table"].reshape(1, -1)}
    outs = {"y_t": (P, KT, T), "pssm": (P, NG, 512), "pconv": (P, NCONV, 3), "kt_out": (P, AH, T), "vt_out": (P, AH, T),
            "sssm": (NPAIR, P, NB, P), "sconv": (P, NCONV, NB, 3)}
    nc = bacc.Bacc("TRN2", target_bir_lowering=False, num_devices=1)
    ins = {k: np.ascontiguousarray(a) for k, a in ins.items()}
    args = [nc.dram_tensor(k, a.shape, mybir.dt.from_np(a.dtype), kind="ExternalInput").ap() for k, a in ins.items()]
    args += [nc.dram_tensor(k, sh, F32, kind="ExternalOutput").ap() for k, sh in outs.items()]
    build(nc, *args)
    o = run_bass_kernel_spmd(nc, [ins], core_ids=[0]).results[0]

    def tokens(a):
        a = a.transpose(2, 1, 0)
        return a[:SEQ].reshape(1, SEQ, -1), a[SEQ:].reshape(NB, 1, -1)

    def unconv(a):
        return np.concatenate([a[8:24], a[0:8]])

    y_p, y_s = tokens(o["y_t"])
    k_p, k_s = (a.reshape(*a.shape[:2], AH, P) for a in tokens(o["kt_out"]))
    v_p, v_s = (a.reshape(*a.shape[:2], AH, P) for a in tokens(o["vt_out"]))
    p_ssm = o["pssm"].reshape(P, NH_SSD, 64).transpose(1, 2, 0)[None, None]
    p_conv = unconv(o["pconv"].transpose(1, 0, 2)).reshape(3072, 3).T[None, None]
    s_ssm = o["sssm"].transpose(2, 0, 1, 3).reshape(1, NB, NH_SSD, 64, P)
    s_conv = unconv(o["sconv"].transpose(1, 0, 2, 3)).reshape(3072, NB, 3).transpose(1, 2, 0)[None]
    return tuple(np.ascontiguousarray(a) for a in (y_p, y_s, p_ssm, p_conv, k_p, v_p, s_ssm, s_conv, k_s, v_s))
```

```python
import math
from contextlib import ExitStack

import concourse.bass as bass
from concourse import mybir

F32 = mybir.dt.float32
F32R = mybir.dt.float32r
I32 = mybir.dt.int32
ACT = mybir.ActivationFunctionType
ALU = mybir.AluOpType
AXX = mybir.AxisListType.X

P = 128
D = 1024
SEQ = 512
NB = 8
T = SEQ + NB
HALF = T // 2
KT = D // P
NH_SSD, NG, NCH = 32, 4, 4
NPAIR = NH_SSD // 2
HG = NH_SSD // NG
NCONV = 24
AH = 8
PAGES = 2
FF = 4096 // P
EPS = 1e-6
LAM_INIT = 0.8 - 0.6 * math.exp(-0.3)
QK_SCALE = 64.0 ** -0.5

PV = {}
_at = 0
for _n, _w in (("ssd_pre", 8), ("ssd_post", 8), ("conv_w", 96), ("conv_b", 24), ("gate", 16), ("mlp_pre0", 8),
               ("mlp_pre1", 8), ("mlp_post0", 8), ("mlp_post1", 8), ("kv", 8), ("attn_pre", 8), ("attn_post", 8),
               ("subln", 1), ("d", 16), ("jsel", 2), ("pairsel", 64), ("rowj", 2), ("lam", 4), ("dt_bias", 1), ("a_log", 32), ("a_col", 16)):
    PV[_n] = (_at, _at + _w)
    _at += _w
NPV = _at
C_ID, C_ONE, C_UP, C_SL, C_MASK, C_PERM = range(6)

GEMMS = [("xbc", 24, 1), ("z", 16, 1), ("out", 8, 2),
         ("up0a", 16, 1), ("down0a", 8, 2), ("up0b", 16, 1), ("down0b", 8, 2),
         ("q", 8, 1), ("k", 8, 1), ("v", 8, 1), ("o", 8, 1),
         ("up1a", 16, 1), ("down1a", 8, 2), ("up1b", 16, 1), ("down1b", 8, 2)]
BLOCK0, TILE0 = {}, {}
_b = _m = 0
for _n, _mt, _kb in GEMMS:
    BLOCK0[_n], TILE0[_n] = _b, _m
    _b += _mt * _kb
    _m += _mt
NBLK = _b
BLOCKS = {n: k for n, _, k in GEMMS}
QORDER = (0, 3, 1, 2)
NDEC = 5
RAW, SPL = 4, 2


def build(nc, wblk, wdt, x_t, pvec, consts, rope, ssm_in, conv_in, kcache, vcache, ptab,
          y_t, pssm, pconv, kt_out, vt_out, sssm, sconv):
    ctx = ExitStack()
    base = (nc.sbuf_base + 63) // 64 * 64

    def at(name, shape, offset, dt=F32):
        return nc.alloc_sbuf_tensor_at(name, shape, dt, offset=base + offset)

    def sem(name):
        return ctx.enter_context(nc.semaphore(name))

    O_H, O_A, O_HID, O_Y, O_F = 0, 16640, 49920, 116480, 149760
    O_RAW, O_SPL, O_SM = 166400, 182784, 199168
    hT = at("hT", [P, KT, T], O_H)
    aH = at("aH", [P, KT, T], O_A, F32R)
    aL = at("aL", [P, KT, T], O_A + 16640, F32R)
    hH = at("hidH", [P, 16, T], O_HID, F32R)
    hL = at("hidL", [P, 16, T], O_HID + 33280, F32R)
    yT = at("ssdY", [P, NPAIR, T], O_Y)
    bcT = at("bcT", [P, 8, T], O_F)
    fT = at("fT", [P, KT, T], O_F)
    raw = at("wraw", [P, RAW, 1024], O_RAW)
    wH = at("wH", [P, SPL, 1024], O_SPL, F32R)
    wL = at("wL", [P, SPL, 1024], O_SPL + SPL * 4096, F32R)
    cst = at("cst", [P, 6, P], O_SM)
    pv = at("pv", [P, NPV], O_SM + 3072)
    o = O_SM + 3072 + 4 * NPV + 28
    o -= o % 32
    acc = at("acc", [P, T], o)
    rpre = at("rpre", [P, T], o + 2080)
    rpost = at("rpost", [P, T], o + 4160)
    misc = at("misc", [P, 160], o + 6240)
    ptile = at("ptile", [1, NB * PAGES], o + 6880, I32)
    sqt = at("sqt", [P, 2, T], O_Y)
    rel = at("rel", [P, 2, T], O_Y + 4160)
    rsq = at("rsq", [P, 2, T], O_Y + 8320)
    r2 = at("r2", [P, T], O_Y + 12480)
    sq8 = at("sq8", [P, KT, T], O_Y)
    sq8b = at("sq8b", [P, KT, T], O_Y + 16640)
    xr = at("xr", [P, 2, SEQ + 3], O_HID + 36864)
    cacc = at("cacc", [P, 2, SEQ], O_HID + 40992)
    q0 = O_HID
    xdt = at("xdt", [P, NCH, 512], q0)
    xde = at("xde", [P, NCH, 512], q0 + 8192)
    hst = at("hst", [P, NCH, 512], q0 + 16384)
    btok = at("btok", [P, NCH, P], q0 + 24576)
    cbm = at("cbm", [P, NCH, P], q0 + 26624)
    uH = at("uadtH", [P, 2, SEQ], q0 + 28672, F32R)
    uL = at("uadtL", [P, 2, SEQ], q0 + 32768, F32R)
    dec = at("decay", [P, 4, SEQ], q0 + 36864)
    ebc = at("ebc", [P, 2, SEQ], q0 + 45056)
    dtu = at("dtu", [32, T], q0 + 10240)
    dtl = at("dtl", [32, T], q0 + 12320)
    dts = at("dts", [32, T], q0 + 14400)
    zs = at("zs", [P, 2, T], q0)
    hs = at("hs", [P, 2, NB, P], q0 + 4160)
    hc = at("hc", [P, NB, P], q0 + 12352)
    ht = at("ht", [P, 2, NB, P], q0 + 37120)
    bbc = at("bbc", [P, NB, P], q0 + 16448)
    cbc = at("cbc", [P, NB, P], q0 + 20544)
    gs = at("gs", [P, NG, T], q0 + 24640)
    zq = at("zq", [P, 2, T], q0 + 32960)
    rg = at("rg", [P, NG, T], O_F)
    s0 = O_HID + 49152
    xs4 = at("xs4", [P, NCONV, NB, 4], s0)
    xsm = at("xsm", [P, NCONV, NB, 4], s0 + 3072)
    xsc = at("xsc", [P, NCONV, NB], s0 + 6144)
    pcv = at("pcv", [P, NCONV, 3], s0 + 6912)
    slr = at("slr", [P, P], s0 + 7200, F32R)
    hmr = at("hmr", [P, 192], s0 + 7712, F32R)
    dtt = at("dtt", [P, P], s0 + 8480)
    ea = at("ea", [P, 48], s0 + 8992)
    adt = at("adt", [P, P], s0 + 9184)
    dex = at("dex", [P, 3, P], s0 + 9760)
    dtx = at("dtx", [P, NPAIR, NB], s0 + 11296)
    sdx = at("sdx", [P, NPAIR, NB], s0 + 11808)
    yss = at("yss", [P, NPAIR, NB], s0 + 12320)
    wdr = at("wdr", [P, KT, 32], s0 + 12960)
    wdh = at("wdh", [P, KT, 32], s0 + 13984, F32R)
    wdl = at("wdl", [P, KT, 32], s0 + 15008, F32R)
    adH = at("adtH", [P, P], s0 + 12960, F32R)
    adL = at("adtL", [P, P], s0 + 13472, F32R)
    kT = at("kT", [P, AH, T], O_Y)
    qT = at("qT", [P, AH, T], O_Y + 16640)
    vT = at("vT", [P, AH, T], O_F)
    vtok = at("vtok", [P, NCH, AH * P], O_HID + 16640)
    oT = at("oT", [P, AH, T], O_HID)
    ropt = at("ropt", [P, 2, T], O_HID + 49920)
    pr = at("probs", [P, 4, 2, SEQ], O_A + 16640)
    attT = at("attT", [P, 4, SEQ], O_HID + 54080)
    ktile = at("ktile", [P, 4, AH, P], O_A + 16640)
    vtile = at("vtile", [P, 4, AH, P], O_HID + 33280)
    a0 = O_A
    rt1 = at("rt1", [P, T], O_HID + 54080)
    rt2 = at("rt2", [P, T], O_HID + 56160)
    qz = at("qz", [P, AH, NB, 2], a0)
    kz = at("kz", [P, AH, NB, 2], a0 + 512)
    sT = at("sT", [P, PAGES, P], a0 + 1024)
    sE = at("sE", [P, 257], a0 + 2048)
    satt = at("satt", [P, PAGES, 64], a0 + 3104)
    snb = at("snb", [P, 64], a0 + 3616)
    cmb = at("cmb", [P, 64], a0 + 3872)
    ov = at("ov", [P, 64], a0 + 1024)
    kq = at("kq", [P, AH * P], a0 + 4128)
    qb = at("qb", [P, 2, AH * P], a0 + 8224)
    vrow = at("vrow", [P, 4 * P], a0 + 12736)
    osq = at("osq", [P, SEQ], a0 + 4416)
    orr = at("orr", [P, SEQ], a0 + 6464)
    osqs = at("osqs", [P, 64], a0 + 8512)
    orrs = at("orrs", [P, 64], a0 + 8768)

    GP = [ctx.enter_context(nc.psum_tensor(f"GP{i}", [P, 2, 512], F32)) for i in range(2)]
    WP = [ctx.enter_context(nc.psum_tensor(f"WP{i}", [P, 2, 512], F32)) for i in range(2)]
    G = [GP[i // 2][:, i % 2, :] for i in range(4)]
    W = [WP[i // 2][:, i % 2, :] for i in range(4)]

    def cc(i):
        return cst[:, i, :]

    def pc(name, i=0, n=1):
        a = PV[name][0] + i
        return pv[:, a:a + n]

    HV = (slice(0, HALF), slice(HALF, T))

    in_one, in_pv, in_par = sem("in_ones"), sem("in_params"), sem("in_consts")
    in_x = [sem(f"in_x{i}") for i in range(4)]
    raw_in = [sem(f"raw_in{i}") for i in range(RAW)]
    w_hi, w_lo = sem("w_hi"), sem("w_lo")
    blk = sem("blk_used")
    taken = sem("taken")
    mm0 = sem("x_sumsq")
    r0 = sem("r_first")
    dve, act = sem("dve_step"), sem("act_step")
    sq0, alo, ahi, hg_s = sem("sq0"), sem("a_lo"), sem("a_hi"), sem("x_gained")
    ax = [sem("x_even"), sem("x_odd")]
    wd_s, dt_mm, dt_u, dt_l, dt_s, dt_tr, dtx_mm, dtx_s, sda_s, adt_s, dex_mm, dex_s = (sem(n) for n in (
        "wdt_split", "dt_mm", "dt_u", "dt_ln", "dt_ready", "dt_transposed", "dt_spread", "dtx_ready", "sample_adt",
        "adt_ready", "decay_mm", "decay_ready"))
    xr_in, cv, sil = sem("xr_in"), sem("conv_done"), sem("silu_done")
    cs_in, scv, pss = sem("convstate_in"), sem("sample_conv"), sem("sample_silu")
    xz = sem("xr_zero")
    tr_mm, xd_s, xe_s, bt_mm, bt_s, st_mm, h_s, cb_mm, cb_s = (sem(n) for n in (
        "x_transposed", "xdt_ready", "xde_ready", "b_transposed", "btok_ready", "state_mm", "state_ready", "cb_mm", "cb_ready"))
    ua_s, sg_mm, sg_s, md_s, yd_mm, eb_s, yo_mm, y_s = (sem(n) for n in (
        "uadt_ready", "seg_mm", "seg_exp", "mdec_ready", "ydiag_mm", "e_ready", "yoff_mm", "y_ready"))
    hs_in = [sem("hs_in0"), sem("hs_in1")]
    hs_new, hx_s, bc_mm, bc_s, ys_s, sdx_s = sem("hs_new"), sem("hs_terms"), sem("bcast_mm"), sem("bcast_ready"), sem("ysample"), sem("sdx_ready")
    z_g, z_sq, z_gs = sem("z_gated"), sem("z_sq"), sem("z_sum")
    g_mm, g_r, g_hi, g_lo = sem("gn_mm"), sem("gn_r"), sem("gn_hi"), sem("gn_lo")
    g_n = [sem("gn_third_tiles"), sem("gn_other_tiles")]
    f_s, sqf, accf, ps_mm, rp_s = sem("f_ready"), sem("f_sq"), sem("f_acc"), sem("post_mm"), sem("post_r")
    h_n, sqh, acch, pr_mm, r_s = sem("h_new"), sem("h_sq"), sem("h_acc"), sem("pre_mm"), sem("pre_r")
    fr_s = sem("f_scaled")
    u_sq, u_hi, u_lo = sem("up_sq"), sem("up_hi"), sem("up_lo")
    qlo, qhi = sem("q_lo"), sem("q_hi")
    rp_in, rt_mm, kq_s = sem("rope_in"), sem("rot_mm"), sem("kq_ready")
    vt_mm, vk_s = sem("v_transposed"), sem("vtok_ready")
    sc_mm, mx_s, ex_s, att_s, at_mm, at_s, av_mm, o_s = (sem(n) for n in (
        "score_mm", "score_max", "probs_exp", "att_ready", "att_transposed", "attT_ready", "av_mm", "o_ready"))
    lm_s, lm_mm, lm_e, lm_r = sem("lam_prod"), sem("lam_mm"), sem("lam_exp"), sem("lam_ready")
    pt_in = sem("ptab_in")
    kp_in = [sem(f"kpage_in{i}") for i in range(4)]
    vp_in = [sem(f"vpage_in{i}") for i in range(4)]
    kz_s = sem("kz_ready")
    qz_s, ss_s, qb_mm, qb_s, s2_mm, s2_s, sx_s, cm_s, sa_mm, sa_s, sv_mm, pv_s, vr_s, vr_mm, os_s = (sem(n) for n in (
        "qz_ready", "page_scores", "query_mm", "query_spread", "score_rows", "row_max", "row_exp", "comb_ready", "satt_mm",
        "satt_ready", "page_av", "page_weighted", "value_rows", "value_columns", "o_sample"))
    osq_s, on_mm, on_rd, or_s, ox_s, ohi, olo, cf_s, p1_s = (sem(n) for n in (
        "o_sq", "o_mm", "o_sum_read", "o_r", "o_normed", "o_hi", "o_lo", "coefs_ready", "map1_scaled"))
    pw_s = sem("page_products")
    st_out, fin_out, kv_out, y_out = sem("conv_rows_out"), sem("final_state_out"), sem("kv_out"), sem("y_out")
    hs_out = [sem("hs_out0"), sem("hs_out1")]
    block = ctx.enter_context(nc.Block())

    class Own:

        def __init__(self, eng, s):
            self.eng, self.s, self.n = eng, s, 0

        def __call__(self, ins):
            self.n += 1
            ins.then_inc(self.s, 1)
            self.eng.wait_ge(self.s, self.n)

    def q_block(n):
        return n // NCH, QORDER[n % NCH]

    def gate_sums(m):
        return 3 * (m // 4) + m % 4 if m >= 0 else 0

    def gn_place(q):
        return (g_n[0], q // 3 + 1) if q % 3 == 0 else (g_n[1], q - q // 3)

    def gate_sq(sc, m):
        sc.wait_ge(z_g, m + 1)
        if m % 4 == 0:
            sc.activation(gs[:, m // 4, :], yT[:, m, :], ACT.Square).then_inc(z_sq, 1)
        else:
            if gate_sums(m - 2) > 0:
                sc.wait_ge(z_gs, gate_sums(m - 2))
            sc.activation(zq[:, m % 2, :], yT[:, m, :], ACT.Square).then_inc(z_sq, 1)

    def gate_sum(v, own, m):
        if m % 4:
            v.wait_ge(z_sq, m + 1)
            if gate_sums(m - 1):
                v.wait_ge(z_gs, gate_sums(m - 1))
            v.tensor_tensor(gs[:, m // 4, :], gs[:, m // 4, :], zq[:, m % 2, :], ALU.add).then_inc(z_gs, 1)

    dtb = dtt[:, :].rearrange("p (c h) -> p c h", c=NCH)
    deb = dex[:, 1, :].rearrange("p (c h) -> p c h", c=NCH)
    cdb = dex[:, 0, :].rearrange("p (c h) -> p c h", c=NCH)

    def hb(src, c, g):
        return src[:, c, g * HG:(g + 1) * HG].unsqueeze(2).broadcast_to([P, HG, 64])

    def r8(ap):
        return ap.rearrange("p (h e) -> p h e", h=HG)

    @block.sync
    def _(sp):
        sp.dma_start(cst[:, 0:2, :], consts[:, 0:2, :]).then_inc(in_one, 16)
        for i in range(4):
            sp.dma_start(hT[:, 2 * i:2 * i + 2, :], x_t[:, 2 * i:2 * i + 2, :]).then_inc(in_x[i], 16)
        sp.dma_start(raw[:, 0, :], wblk[0, :, :]).then_inc(raw_in[0], 16)
        sp.dma_start(pv[:, :], pvec).then_inc(in_pv, 16)
        sp.dma_start(raw[:, 1, :], wblk[1, :, :]).then_inc(raw_in[1], 16)
        sp.dma_start(cst[:, 2:6, :], consts[:, 2:6, :]).then_inc(in_par, 16)
        sp.dma_start(wdr[:, :, :], wdt).then_inc(in_par, 16)
        for s in range(2, RAW):
            sp.dma_start(raw[:, s, :], wblk[s, :, :]).then_inc(raw_in[s], 16)
        sp.dma_start(xs4[:, :, :, 0:3], conv_in).then_inc(cs_in, 16)
        sp.dma_start(ptile[:, :], ptab).then_inc(pt_in, 16)
        def stream(a, b):
            with sp.Fori(a // RAW, b // RAW) as i:
                for s in range(RAW):
                    sp.wait_ge(w_lo, i * RAW + (s + 1 - RAW))
                    sp.dma_start(raw[:, s, :], wblk[bass.ds(i * RAW + s, 1), :, :].rearrange("o p n -> p (o n)")
                                 ).then_inc(raw_in[s], 16)

        zb, kb, ob = BLOCK0["z"] + RAW, BLOCK0["q"] + RAW, BLOCK0["o"] + RAW
        stream(RAW, zb)
        sp.wait_ge(cv, NCONV)
        sp.dma_start(pconv, pcv[:, :, :]).then_inc(st_out, 16)
        sp.wait_ge(taken, NCONV)
        sp.dma_start(sconv, xs4[:, :, :, 1:4]).then_inc(st_out, 16)
        for g in range(NG):
            sp.wait_ge(h_s, NCH * (g + 1))
            sp.dma_start(pssm[:, g, :], hst[:, NCH - 1, :]).then_inc(fin_out, 16)
        sp.wait_ge(y_s, NPAIR)
        sp.wait_ge(fin_out, 16 * NG)
        for m in range(2):
            sp.dma_start(hs[:, m, :, :], ssm_in[m, :, :, :]).then_inc(hs_in[m], 16)
        for m in range(NPAIR):
            b = zb + m
            sp.wait_ge(w_lo, b + 1 - RAW)
            sp.dma_start(raw[:, b % RAW, :], wblk[b, :, :]).then_inc(raw_in[b % RAW], 16)
            sp.wait_ge(hs_new, m + 1)
            sp.dma_start(sssm[m, :, :, :], hs[:, m % 2, :, :]).then_inc(hs_out[m % 2], 16)
            if m + 2 < NPAIR:
                sp.wait_ge(hs_out[m % 2], 16 * (m // 2 + 1))
                sp.wait_ge(ys_s, m + 1)
                sp.dma_start(hs[:, m % 2, :, :], ssm_in[m + 2, :, :, :]).then_inc(hs_in[m % 2], 16)
        stream(zb + NPAIR, kb)
        sp.wait_ge(blk, BLOCK0["q"])
        sp.dma_start(ropt[:, :, :], rope).then_inc(rp_in, 16)
        sp.wait_ge(pt_in, 16)

        def page(n, cache, dst, s):
            idx = sp.value_load(ptile[0:1, n:n + 1], min_val=0, max_val=cache.shape[0] - 1)
            sp.dma_start(dst[:, n % 4, :, :].rearrange("p h k -> p (h k)"),
                         cache[bass.ds(idx, 1), :, :].rearrange("o p n -> p (o n)")).then_inc(s[n % 4], 16)

        vb = BLOCK0["v"]
        stream(kb, vb)
        sp.wait_ge(blk, BLOCK0["k"])
        for n in range(4):
            page(n, kcache, ktile, kp_in)
        for m in range(8 + RAW):
            b = vb + m
            sp.wait_ge(w_lo, b + 1 - RAW)
            sp.dma_start(raw[:, b % RAW, :], wblk[b, :, :]).then_inc(raw_in[b % RAW], 16)
            for n in range(4 + 2 * (m - 4), 6 + 2 * (m - 4)):
                if 4 <= n < NB * PAGES:
                    sp.wait_ge(ss_s, n - 3)
                    page(n, kcache, ktile, kp_in)
        sp.wait_ge(blk, BLOCK0["o"])
        for n in range(NB * PAGES):
            if n >= 4:
                sp.wait_ge(sv_mm, n // PAGES - 1)
            page(n, vcache, vtile, vp_in)
            if n == 3:
                sp.wait_ge(kq_s, 16)
                sp.dma_start(kt_out, kT[:, :, :]).then_inc(kv_out, 16)
            elif n == 7:
                sp.wait_ge(taken, TILE0["v"] + AH)
                sp.dma_start(vt_out, vT[:, :, :]).then_inc(kv_out, 16)
        stream(ob, NBLK)
        for m in range(KT):
            sp.wait_ge(h_n, 24 + m + 1)
            sp.dma_start(y_t[:, m, :], hT[:, m, :]).then_inc(y_out, 16)
        sp.wait_ge(st_out, 32)
        sp.wait_ge(fin_out, 16 * NG)
        for i in range(2):
            sp.wait_ge(hs_out[i], 16 * NPAIR // 2)
        sp.wait_ge(kv_out, 32)
        sp.wait_ge(y_out, 16 * KT)

    @block.gpsimd
    def _(pool):
        def split(i, s, first):
            d = s % SPL
            pool.wait_ge(raw_in[s], i * 16 + 16)
            if not (first and s < SPL):
                pool.wait_ge(blk, i * RAW + (s + 1 - SPL))
            pool.tensor_tensor(wH[:, d, :].rearrange("p (k n) -> p k n", k=8),
                               raw[:, s, :].rearrange("p (k n) -> p k n", k=8),
                               cst[:, C_ONE:C_ONE + 1, :].broadcast_to([P, 8, P]), ALU.mult).then_inc(w_hi, 1)
            pool.wait_ge(w_hi, i * RAW + (s + 1))
            pool.tensor_tensor(wL[:, d, :], raw[:, s, :], wH[:, d, :].bitcast(F32), ALU.subtract).then_inc(w_lo, 1)

        pool.wait_ge(in_one, 16)
        def stream(a, b):
            while a < b and (a % RAW or a == 0 or b - a < RAW):
                n = min(RAW, b) if a == 0 else 1
                for j in range(n):
                    split((a + j) // RAW, (a + j) % RAW, a == 0)
                a += n
            m = (b - a) // RAW
            if m > 1:
                with pool.Fori(a // RAW, a // RAW + m) as i:
                    for s in range(RAW):
                        split(i, s, False)
                a += m * RAW
            for j in range(a, b):
                split(j // RAW, j % RAW, False)

        def scale_output(p):
            pool.wait_ge(rp_s, p + 1)
            for m in range(KT):
                pool.tensor_tensor(fT[:, m, :], fT[:, m, :], rpost[:, :], ALU.mult).then_inc(fr_s, 1)

        stream(0, SPL)
        pool.wait_ge(r0, 1)
        pool.wait_ge(hg_s, KT)
        for t in range(1, KT, 2):
            pool.tensor_tensor(sq8[:, t, :], fT[:, t, :], rpre[:, :], ALU.mult).then_inc(ax[1], 1)
        stream(SPL, BLOCK0["z"])

        def masked_adt(k):
            if k >= 2:
                pool.wait_ge(sg_mm, k - 1)
            for dst, src in ((uH, adH), (uL, adL)):
                pool.tensor_tensor(dst[:, k % 2, :].rearrange("p (c l) -> p c l", c=NCH),
                                   cst[:, C_UP:C_UP + 1, :].broadcast_to([P, NCH, P]),
                                   src[:, :].bitcast(F32).rearrange("p (c h) -> p c h", c=NCH)[:, :, k:k + 1]
                                   .broadcast_to([P, NCH, P]), ALU.mult).then_inc(ua_s, 1)

        pool.wait_ge(in_par, 32)
        pool.wait_ge(adt_s, 1)
        pool.wait_ge(dex_s, 1)
        for g in range(NG):
            masked_adt(8 * g)
            masked_adt(8 * g + 1)
            for c in range(NCH):
                pool.wait_ge(xd_s, g * NCH + c + 1)
                pool.tensor_tensor(r8(xde[:, c, :]), r8(xdt[:, c, :]), hb(deb, c, g), ALU.mult).then_inc(xe_s, 1)
            for k in range(8 * g + 2, 8 * g + 8):
                masked_adt(k)

        at_ = BLOCK0["z"]
        stream(at_, BLOCK0["out"] + SPL)
        at_ = BLOCK0["out"] + SPL
        for q in range(NPAIR):
            if q % 3:
                pool.wait_ge(g_r, q // 4 + 1)
                pool.tensor_tensor(yT[:, q, :], yT[:, q, :], rg[:, q // 4, :], ALU.mult).then_inc(g_n[1], 1)
        for p, nxt in enumerate(("up0a", "q", "up1a")):
            stream(at_, BLOCK0[nxt] + SPL)
            at_ = BLOCK0[nxt] + SPL
            scale_output(p)
            if p == 1:
                stream(at_, BLOCK0["o"] + SPL)
                at_ = BLOCK0["o"] + SPL
                pool.wait_ge(sa_s, 1)
                for b in range(NB):
                    one, two = vtile[:, 2 * b % 4, :, :], vtile[:, (2 * b + 1) % 4, :, :]
                    for pg, x in enumerate((one, two)):
                        pool.wait_ge(vp_in[(2 * b + pg) % 4], 16 * (b // 2 + 1))
                        pool.tensor_tensor(x, x, satt[:, pg, :].rearrange("p (h b) -> p h b", h=AH)[:, :, b:b + 1]
                                           .broadcast_to([P, AH, P]), ALU.mult).then_inc(pw_s, 1)
                    pool.wait_ge(pw_s, 2 * b + 2)
                    pool.tensor_tensor(one, one, two, ALU.add).then_inc(pv_s, 1)
        stream(at_, NBLK)
        scale_output(3)

    @block.tensor
    def _(pe):
        def three(out, lh, ll, rh, rl, first, last):
            pe.matmul(out, lh, rh, start=first, stop=False)
            pe.matmul(out, lh, rl, start=False, stop=False)
            return pe.matmul(out, ll, rh, start=False, stop=last)

        def tile(name, m, b, inH, inL, wait_taken, each_k=None):
            nk = BLOCKS[name]
            par = m[1]
            if wait_taken:
                pe.wait_ge(taken, m[0] - 1)
            for kb in range(nk):
                d = (b[1] + kb) % SPL
                pe.wait_ge(w_lo, b[0] + kb + 1)
                for k in range(8):
                    if each_k is not None:
                        each_k(kb * 8 + k)
                    for h in range(2):
                        o_ = G[2 * par + h][:, 0:HALF]
                        lh, ll = wH[:, d, k * P:(k + 1) * P], wL[:, d, k * P:(k + 1) * P]
                        kk = kb * 8 + k
                        ins = three(o_, lh, ll, inH[:, kk, HV[h]], inL[:, kk, HV[h]],
                                    kb == 0 and k == 0, kb == nk - 1 and k == 7)
                ins.then_inc(blk, 1)

        def gemm(name, inH, inL, after=None, each_k=None, tiles=None, inside=None):
            n = dict((a, b) for a, b, _ in GEMMS)[name]
            nk, m0, b0 = BLOCKS[name], TILE0[name], BLOCK0[name]

            def one(m, hook=None):
                tile(name, (m0 + m, (m0 + m) % 2), (b0 + m * nk, b0 + m * nk), inH, inL, m0 + m >= 2, hook)

            if after is not None:
                for m in range(n):
                    one(m, each_k if m == 0 else inside and (lambda k, m=m: inside(m, k)))
                    after(m)
                return
            a, e = tiles or (0, n)
            if a == 0:
                one(0, each_k)
                one(1)
                a = 2
            with pe.Fori(a // 2, e // 2) as i:
                for u in range(2):
                    tile(name, (i * 2 + (m0 + u), (m0 + u) % 2), (i * (2 * nk) + (b0 + u * nk), b0 + u * nk),
                         inH, inL, True)

        pe.wait_ge(in_one, 16)
        for t in range(KT):
            pe.wait_ge(sq0, t + 1)
            for h in range(2):
                ins = pe.matmul(W[h][:, 0:HALF], cc(C_ONE), sq8[:, t, HV[h]], start=t == 0, stop=t == KT - 1)
        ins.then_inc(mm0, 1)
        gemm("xbc", aH, aL, each_k=lambda k: pe.wait_ge(alo, k + 1), tiles=(0, 4))
        pe.wait_ge(wd_s, 1)
        for h in range(2):
            for k in range(KT):
                ins = three(W[2 + h][0:32, 0:HALF], wdh[:, k, :], wdl[:, k, :], aH[:, k, HV[h]], aL[:, k, HV[h]],
                            k == 0, k == KT - 1)
        ins.then_inc(dt_mm, 1)
        gemm("xbc", aH, aL, tiles=(4, 10))
        pe.wait_ge(dt_s, 1)
        for c in range(NCH):
            ins = pe.transpose(W[0][:, c * 32:c * 32 + 32], dts[:, c * P:(c + 1) * P], cst[0:32, C_ID, 0:32])
        ins.then_inc(dt_tr, 1)
        for h in range(NH_SSD):
            e, q = 64 * (h % 2), h // 2
            ins = pe.matmul(W[1][e:e + 64, q * NB:q * NB + NB], cst[0:32, C_ID, h:h + 1].broadcast_to([32, 64]),
                            dts[:, SEQ:T], start=True, stop=True)
        ins.then_inc(dtx_mm, 1)
        gemm("xbc", aH, aL, tiles=(10, 14))
        pe.wait_ge(adt_s, 1)
        pe.matmul(W[3][:, 0:P], cc(C_ONE), adt[:, :], start=True, stop=True)
        pe.matmul(W[3][:, P:2 * P], cc(C_SL), adt[:, :], start=True, stop=True).then_inc(dex_mm, 1)
        gemm("xbc", aH, aL, tiles=(14, 22))

        def x_turn(g, c):
            if c == 0:
                pe.wait_ge(sil, 8 + 4 * (g + 1))
                pe.wait_ge(dex_s, 1)
            if c >= 2:
                pe.wait_ge(xd_s, g * NCH + c - 1)
            elif g:
                pe.wait_ge(sg_s, 8 * g)
            for q in range(4):
                ins = pe.transpose(W[c % 2][:, q * P:(q + 1) * P], yT[:, 4 * g + q, c * P:(c + 1) * P], cc(C_ID))
            ins.then_inc(tr_mm, 1)

        def b_turn(g):
            if g:
                pe.wait_ge(eb_s, 4 * g)
            for c in range(NCH):
                ins = pe.transpose(W[2][:, c * P:(c + 1) * P], bcT[:, g, c * P:(c + 1) * P], cc(C_ID))
            ins.then_inc(bt_mm, 1)
            for c in range(NCH):
                ins = pe.matmul(W[3][:, c * P:(c + 1) * P], bcT[:, g, c * P:(c + 1) * P],
                                bcT[:, 4 + g, c * P:(c + 1) * P], start=True, stop=True)
            ins.then_inc(cb_mm, 1)

        x_turn(0, 0)
        x_turn(0, 1)
        b_turn(0)
        gemm("xbc", aH, aL, tiles=(22, 24))

        def seg_sum(k):
            n, e = k // 2, k % 2
            pe.wait_ge(ua_s, 2 * k + 2)
            if k % 8 < 2:
                pe.wait_ge(xd_s, NCH * (k // 8) + 3 + e)
            else:
                pe.wait_ge(sg_s, k - 1)
            pe.matmul(W[e][:, :], slr[:, :], uH[:, e, :], start=True, stop=False)
            pe.matmul(W[e][:, :], slr[:, :], uL[:, e, :], start=False, stop=True)
            if k % 8 == 0:
                pe.wait_ge(bt_s, k // 8 + 1)
            elif k % 8 == 2:
                pe.wait_ge(cb_s, k // 8 + 1)
            elif e == 0:
                pe.wait_ge(eb_s, n - 1)
            half = hmr[:, 64 - 64 * e:192 - 64 * e]
            pe.matmul(W[2 + n % 2][:, :], half, uH[:, e, :], start=e == 0, stop=False)
            pe.matmul(W[2 + n % 2][:, :], half, uL[:, e, :], start=False, stop=e == 1).then_inc(sg_mm, 1)

        for g in range(NG):
            if g:
                x_turn(g, 0)
                x_turn(g, 1)
                b_turn(g)
            x_turn(g, 2)
            x_turn(g, 3)
            seg_sum(8 * g)
            seg_sum(8 * g + 1)
            pe.wait_ge(taken, NCONV)
            if g:
                pe.wait_ge(y_s, 4 * g)
            for c in range(NCH):
                pe.wait_ge(xe_s, g * NCH + c + 1)
                pe.matmul(G[c][:, :], btok[:, c, :], xde[:, c, :], start=True, stop=True).then_inc(st_mm, 1)
            for q in range(4):
                n = 4 * g + q
                if n >= 2:
                    pe.wait_ge(y_s, n - 1)
                for e in range(2):
                    k = 2 * n + e
                    if k % 8 < 6:
                        seg_sum(k + 2)
                    pe.wait_ge(md_s, k + 1)
                    if q < 2 and e == 0:
                        pe.wait_ge(h_s, g * NCH + q + 1)
                    for c in range(NCH):
                        ins = pe.matmul(G[n % 2][64 * e:64 * e + 64, c * P:(c + 1) * P],
                                        xdt[:, c, (2 * q + e) * 64:(2 * q + e) * 64 + 64],
                                        dec[:, k % 4, c * P:(c + 1) * P], start=True, stop=True)
                    ins.then_inc(yd_mm, 1)
                pe.wait_ge(h_s, g * NCH + (3 if q == 0 else 4))
                for c in range(1, NCH):
                    ins = pe.matmul(G[2 + n % 2][:, c * P:(c + 1) * P], hst[:, c - 1, q * P:(q + 1) * P],
                                    bcT[:, 4 + g, c * P:(c + 1) * P], start=True, stop=True)
                ins.then_inc(yo_mm, 1)

        def z_after(m):
            if m % 4 == 0:
                g = m // 4
                if g == 0:
                    pe.wait_ge(eb_s, NPAIR)
                    pe.wait_ge(pss, 1)
                else:
                    pe.wait_ge(bc_s, 4 * g)
                for j in range(2):
                    for hf in range(2):
                        for b in range(4):
                            ins = pe.matmul(W[2 * j + hf][:, b * P:(b + 1) * P],
                                            bcT[:, 4 * j + g, SEQ + 4 * hf + b:SEQ + 4 * hf + b + 1].broadcast_to([P, P]),
                                            cc(C_ID), start=True, stop=True)
                ins.then_inc(bc_mm, 1)

        z_after(0)
        pe.wait_ge(y_s, NPAIR)

        def group_sum(g):
            pe.wait_ge(z_gs, 3 * (g + 1))
            if g == 0:
                pe.wait_ge(bc_s, 16)
            elif g >= 2:
                pe.wait_ge(g_r, g - 1)
            for h in range(2):
                ins = pe.matmul(W[2 * (g % 2) + h][:, 0:HALF], cc(C_ONE), gs[:, g, HV[h]], start=True, stop=True)
            ins.then_inc(g_mm, 1)

        def z_next(m):
            if m < 15:
                z_after(m + 1)
            if m == 14:
                group_sum(0)
                group_sum(1)

        gemm("z", aH, aL, after=z_next)
        for g in range(2, NG):
            group_sum(g)
        gemm("out", hH, hL, each_k=lambda k: pe.wait_ge(g_lo, k + 1))

        def post_sum(p):
            pe.wait_ge(accf, 8 * p + 8)
            for h in range(2):
                ins = pe.matmul(W[h][:, 0:HALF], cc(C_ONE), acc[:, HV[h]], start=True, stop=True)
            ins.then_inc(ps_mm, 1)

        def low_k(p):
            return lambda k: pe.wait_ge(alo, KT + 8 * p + k + 1)

        def first_gemm(name, p):
            gemm(name, aH, aL, each_k=low_k(p), tiles=(0, 4))
            pe.wait_ge(acch, 7 * p + 7)
            for h in range(2):
                ins = pe.matmul(W[2 + h][:, 0:HALF], cc(C_ONE), acc[:, HV[h]], start=True, stop=True)
            ins.then_inc(pr_mm, 1)
            gemm(name, aH, aL, tiles=(4, dict((a, b) for a, b, _ in GEMMS)[name]))

        def mlp(l):
            for v, s in enumerate("ab"):
                if v == 0:
                    first_gemm(f"up{l}{s}", 2 * l)
                else:
                    gemm(f"up{l}{s}", aH, aL)
                gemm(f"down{l}{s}", hH, hL, each_k=lambda k: pe.wait_ge(u_lo, 32 * l + 16 * v + k + 1))

        post_sum(0)
        mlp(0)
        post_sum(1)

        def rotate(n):
            src = qT if n < 8 else kT
            pe.wait_ge(taken, TILE0["q"] + (n // 8 + 1) * 8)
            if n:
                pe.wait_ge(kq_s, n)
            for h in range(2):
                ins = pe.matmul(W[h][:, 0:HALF], cc(C_PERM), src[:, n % 8, HV[h]], start=True, stop=True)
            ins.then_inc(rt_mm, 1)

        def query(b, k):
            if k % 4 < 3:
                return
            hf = k // 4
            if b == hf == 0:
                pe.wait_ge(qz_s, 1)
            else:
                pe.wait_ge(qb_s, 2 * b + hf)
            for h in range(4):
                ins = pe.matmul(W[2][:, h * P:(h + 1) * P],
                                qT[:, 4 * hf + h, SEQ + b:SEQ + b + 1].broadcast_to([P, P]), cc(C_ID),
                                start=True, stop=True)
            ins.then_inc(qb_mm, 1)

        def v_transpose(h):
            pe.wait_ge(taken, TILE0["v"] + h + 1)
            if h:
                pe.wait_ge(vk_s, h)
            else:
                pe.wait_ge(lm_e, 1)
            for c in range(NCH):
                ins = pe.transpose(W[3][:, c * P:(c + 1) * P], vT[:, h, c * P:(c + 1) * P], cc(C_ID))
            ins.then_inc(vt_mm, 1)

        first_gemm("q", 1)
        pe.wait_ge(r_s, 2)
        pe.wait_ge(lm_s, 1)
        pe.matmul(W[3][:, 0:2], cc(C_ONE), misc[:, 0:2], start=True, stop=True).then_inc(lm_mm, 1)
        gemm("k", hH, hL, after=rotate, each_k=lambda k: pe.wait_ge(qlo, k + 1))

        def v_after(m):
            rotate(8 + m)
            if m:
                v_transpose(m - 1)

        gemm("v", hH, hL, after=v_after, each_k=lambda k: query(0, k), inside=query)
        v_transpose(AH - 1)

        def scores(n):
            h, i = q_block(n)
            w = (i + 1) * P
            if n % NCH == 0:
                pe.wait_ge(kq_s, AH + h + 1)
            if n >= 2:
                pe.wait_ge(ex_s, 2 * (n - 1))
            for j in range(2):
                ins = pe.matmul(G[2 * (n % 2) + j][:, 0:w], qT[64 * j:64 * j + 64, h, i * P:(i + 1) * P],
                                kT[64 * j:64 * j + 64, h, 0:w], start=True, stop=True)
            ins.then_inc(sc_mm, 1)

        def turn(n):
            pe.wait_ge(att_s, n + 1)
            if n >= 2:
                pe.wait_ge(at_s, n - 1)
            if n >= 2 * NCH and n % NCH == 0:
                pe.wait_ge(on_rd, n // NCH - 1)
            for kb in range(q_block(n)[1] + 1):
                ins = pe.transpose(W[n % 2][:, kb * P:(kb + 1) * P], pr[:, n % 4, 0, kb * P:(kb + 1) * P], cc(C_ID))
            ins.then_inc(at_mm, 1)

        def values(n):
            h, i = q_block(n)
            pe.wait_ge(at_s, n + 1)
            if n:
                pe.wait_ge(o_s, n)
            for kb in range(i + 1):
                ins = pe.matmul(W[2][:, 0:P], vtok[:, kb, h * P:(h + 1) * P], attT[:, n % 4, kb * P:(kb + 1) * P],
                                start=kb == 0, stop=kb == i)
            ins.then_inc(av_mm, 1)

        def page_values(b):
            pe.wait_ge(pv_s, b + 1)
            for hf in range(2):
                ins = pe.matmul(W[3][64 * hf:64 * hf + NB, :], misc[:, 67 - b:75 - b],
                                vtile[:, 2 * b % 4, 4 * hf:4 * hf + 4, :].rearrange("p h k -> p (h k)"),
                                start=b == 0, stop=b == NB - 1)
            ins.then_inc(sv_mm, 1)

        def head_sum(h):
            pe.wait_ge(osq_s, h + 1)
            pe.wait_ge(at_s, min(NCH * h + 7, AH * NCH))
            pe.matmul(W[0][:, :], cc(C_ONE), osq[:, :], start=True, stop=True).then_inc(on_mm, 1)

        for n in range(AH * NCH + 7):
            if n < AH * NCH:
                scores(n)
            if n == 2:
                pe.wait_ge(ss_s, NB * PAGES)
                pe.wait_ge(kz_s, 2)
                pe.wait_ge(vk_s, AH)
                for pg in range(PAGES):
                    pe.transpose(W[3][:, pg * P:(pg + 1) * P], sT[:, pg, :], cc(C_ID))
                pe.matmul(W[3][:, 256:257], kz[:, :, :, :].rearrange("p h b j -> p (h b j)"), cst[:, C_ONE, 0:1],
                          start=True, stop=True).then_inc(s2_mm, 1)
            elif n == 4:
                pe.wait_ge(cm_s, 1)
                for pg in range(PAGES):
                    pe.matmul(W[3][:, 256 + pg * 64:320 + pg * 64], sE[:, pg * P:(pg + 1) * P], cmb[:, :],
                              start=True, stop=True)
                pe.matmul(W[3][:, 384:448], sE[:, 256:257].broadcast_to([P, P]), cmb[:, :], start=True, stop=True
                          ).then_inc(sa_mm, 1)
            if 3 <= n < AH * NCH + 3:
                turn(n - 3)
            if 4 <= n < AH * NCH + 4:
                values(n - 4)
            if n >= 7 and (n - 7) % 4 == 0 and n < 36:
                page_values((n - 7) // 4)
            if n >= 10 and (n - 10) % 4 == 0:
                head_sum((n - 10) // 4)
        pe.wait_ge(vr_s, 2)
        for h in range(AH):
            a = 64 * (h // 4)
            ins = pe.transpose(W[3][:, h * NB:(h + 1) * NB], vrow[a:a + NB, h % 4 * P:(h % 4 + 1) * P],
                               cst[a:a + NB, C_ID, a:a + NB])
            if h % 4 == 3:
                ins.then_inc(vr_mm, 1)
                pe.wait_ge(vr_mm, h // 4 + 1)
        pe.wait_ge(osq_s, AH + 1)
        pe.matmul(W[2][:, 0:64], cc(C_ONE), osqs[:, :], start=True, stop=True).then_inc(on_mm, 1)
        gemm("o", aH, aL, each_k=lambda k: pe.wait_ge(olo, k + 1))
        post_sum(2)
        mlp(1)
        post_sum(3)

    @block.scalar
    def _(sc):
        own = Own(sc, act)
        A = sc.activation

        def rsqrt(dst, banks, n, signal):
            own(A(dst.rearrange("p (v t) -> p v t", v=2), banks[:, :, 0:HALF], ACT.Ln, scale=1.0 / n,
                  bias=misc[:, 8:9]))
            A(dst, dst, ACT.Exp, scale=-0.5).then_inc(signal, 1)

        LN_EXP = "natural_log_exp_and_others"
        sc.preload_act_table_set(LN_EXP)
        for t in range(KT):
            sc.wait_ge(in_x[t // 2], 16)
            A(sq8[:, t, :], hT[:, t, :], ACT.Square).then_inc(sq0, 1)
        sc.wait_ge(mm0, 1)
        sc.wait_ge(wd_s, 1)
        rsqrt(rpre[:, :], WP[0], D, r0)
        for t in range(KT):
            sc.wait_ge(ax[t % 2], t // 2 + 1)
            A(aH[:, t, :], sq8[:, t, :], ACT.Copy).then_inc(ahi, 1)
        A(ea[:, :], pv[:, PV["a_log"][0]:PV["a_col"][1]], ACT.Exp)

        def silu_tile(m):
            sc.wait_ge(cv, m + 1)
            dst = bcT[:, m, 0:SEQ] if m < 8 else yT[:, m - 8, 0:SEQ]
            A(dst, cacc[:, m % 2, :], ACT.Silu).then_inc(sil, 1)

        sc.wait_ge(xz, 1)
        for m in range(NCONV):
            sc.wait_ge(blk, m + 1)
            if m >= 2:
                sc.wait_ge(cv, m - 1)
            g = 2 * (m % 2)
            A(xr[:, m % 2, 3:3 + HALF], G[g][:, 0:HALF], ACT.Copy).then_inc(xr_in, 1)
            A(xr[:, m % 2, 3 + HALF:3 + SEQ], G[g + 1][:, 0:SEQ - HALF], ACT.Copy).then_inc(xr_in, 1)
            A(xs4[:, m, :, 3], G[g + 1][:, SEQ - HALF:HALF], ACT.Copy).then_inc(taken, 1)
            if m:
                silu_tile(m - 1)
            if m == 6:
                sc.wait_ge(dt_u, 1)
                sc.preload_act_table_set(LN_EXP)
                own(A(dtl[:, :], dtu[:, :], ACT.Abs))
                own(A(dtl[:, :], dtl[:, :], ACT.Exp, scale=-1.0))
                A(dtl[:, :], dtl[:, :], ACT.Ln, bias=misc[0:32, 9:10]).then_inc(dt_l, 1)
            elif m == 12:
                sc.wait_ge(dtx_mm, 1)
                A(dtx[:, :, :].rearrange("p q b -> p (q b)"), W[1][:, 0:P], ACT.Copy).then_inc(dtx_s, 1)
            elif m == 16:
                sc.wait_ge(dex_mm, 1)
                sc.wait_ge(sda_s, 1)
                A(dex[:, 0:2, :].rearrange("p q b -> p (q b)"), W[3][:, 0:2 * P], ACT.Exp)
                A(dex[:, 2, :], dex[:, 2, :], ACT.Exp).then_inc(dex_s, 1)
        silu_tile(NCONV - 1)
        sc.preload_act_table_set(LN_EXP)
        for g in range(NG):
            sc.wait_ge(bt_mm, g + 1)
            A(btok[:, :, :].rearrange("p c n -> p (c n)"), W[2][:, :], ACT.Copy).then_inc(bt_s, 1)
            for q in range(4):
                n = 4 * g + q
                for k in range(2 * n, 2 * n + 2):
                    sc.wait_ge(sg_mm, k + 1)
                    if k >= 4:
                        sc.wait_ge(yd_mm, k - 3)
                    A(dec[:, k % 4, :], W[k % 2][:, :], ACT.Exp).then_inc(sg_s, 1)
                if n >= 2:
                    sc.wait_ge(y_s, n - 1)
                A(ebc[:, n % 2, :], W[2 + n % 2][:, :], ACT.Exp).then_inc(eb_s, 1)

        sc.wait_ge(scv, 3)
        own(A(bcT[:, :, SEQ:T], xsc[:, 0:8, :], ACT.Silu))
        A(yT[:, :, SEQ:T], xsc[:, 8:NCONV, :], ACT.Silu).then_inc(pss, 1)

        def rows(dst, j, g):
            for hf in range(2):
                A(dst[:, 4 * hf:4 * hf + 4, :].rearrange("p b n -> p (b n)"), W[2 * j + hf][:, :],
                  ACT.Copy).then_inc(bc_s, 1)

        for m in range(NPAIR):
            if m % 4 == 0:
                g = m // 4
                sc.wait_ge(bc_mm, g + 1)
                if g:
                    sc.wait_ge(hx_s, m)
                else:
                    sc.wait_ge(y_s, NPAIR)
                    sc.wait_ge(fin_out, 16 * NG)
                    sc.wait_ge(sdx_s, 1)
                rows(bbc, 0, g)
                sc.wait_ge(bc_s, 4 * g + 2)
            if m >= 2:
                sc.wait_ge(hs_new, m - 1)
            sc.wait_ge(hs_in[m % 2], 16 * (m // 2 + 1))
            for b in range(NB):
                A(ht[:, m % 2, b, :], bbc[:, b, :], ACT.Copy, scale=sdx[:, m, b:b + 1])
            for b in range(NDEC):
                ins = A(hs[:, m % 2, b, :], hs[:, m % 2, b, :], ACT.Copy,
                        scale=dex[:, 2, m * NB + b:m * NB + b + 1])
            ins.then_inc(hx_s, 1)
            if m % 4 == 0:
                if g:
                    sc.wait_ge(ys_s, m)
                rows(cbc, 1, g)
            sc.wait_ge(blk, BLOCK0["z"] + m + 1)
            if m >= 2:
                sc.wait_ge(z_g, m - 1)
            gb = 2 * ((TILE0["z"] + m) % 2)
            A(zs[:, m % 2, HV[0]], G[gb][:, 0:HALF], ACT.Silu)
            A(zs[:, m % 2, HV[1]], G[gb + 1][:, 0:HALF], ACT.Silu).then_inc(taken, 1)
            if m:
                gate_sq(sc, m - 1)
        sc.preload_act_table_set(LN_EXP)

        def gated_hi(q):
            s_, n = gn_place(q)
            sc.wait_ge(s_, n)
            A(hH[:, q, :], yT[:, q, :], ACT.Copy, scale=pc("gate", q)).then_inc(g_hi, 1)

        for g in range(NG):
            if g == 2:
                gate_sq(sc, NPAIR - 1)
            if g == 3:
                for i in range(2):
                    sc.wait_ge(hs_out[i], 16 * NPAIR // 2)
                sc.wait_ge(st_out, 32)
                sc.wait_ge(ys_s, NPAIR)
                for q in range(4):
                    gated_hi(q)
            sc.wait_ge(g_mm, g + 1)
            rsqrt(rg[:, g, :], WP[g % 2], 512, g_r)
        for q in range(4, NPAIR):
            gated_hi(q)
        def boundary(p, gpre, own_f):
            for m in range(KT):
                if own_f:
                    nm = {0: "out", 2: "o"}[p]
                    gb = 2 * ((TILE0[nm] + m) % 2)
                    sc.wait_ge(blk, BLOCK0[nm] + BLOCKS[nm] * (m + 1))
                    A(fT[:, m, HV[0]], G[gb][:, 0:HALF], ACT.Copy)
                    A(fT[:, m, HV[1]], G[gb + 1][:, 0:HALF], ACT.Copy).then_inc(taken, 1)
                    sc.wait_ge(taken, TILE0[nm] + m + 1)
                else:
                    sc.wait_ge(f_s, 8 * (p // 2) + m + 1)
                if m >= 2:
                    sc.wait_ge(accf, 8 * p + m - 1)
                A(sqt[:, m % 2, :], fT[:, m, :], ACT.Square).then_inc(sqf, 1)
            sc.wait_ge(ps_mm, p + 1)
            rsqrt(rpost[:, :], WP[0], D, rp_s)
            if p == 3:
                return
            for m in range(KT):
                sc.wait_ge(h_n, 8 * p + m + 1)
                A(aH[:, m, :], hT[:, m, :], ACT.Copy, scale=pc(gpre, m)).then_inc(ahi, 1)
                A((sq8 if p == 1 else sq8b)[:, m, :], hT[:, m, :], ACT.Square).then_inc(sqh, 1)
            if p == 1:
                for m in range(KT):
                    A(hH[:, m, :], hT[:, m, :], ACT.Copy, scale=pc("kv", m)).then_inc(qhi, 1)

        def pre_norm(p):
            sc.wait_ge(pr_mm, p + 1)
            rsqrt(rpre[:, :], WP[1], D, r_s)

        def mlp(l):
            for v, s in enumerate("ab"):
                name = f"up{l}{s}"
                for m in range(16):
                    n = 32 * l + 16 * v + m
                    gb = 2 * ((TILE0[name] + m) % 2)
                    sc.wait_ge(blk, BLOCK0[name] + m + 1)
                    if n >= 2:
                        sc.wait_ge(u_sq, n - 1)
                    sc.wait_ge(taken, TILE0[name] + m)
                    A(rel[:, m % 2, HV[0]], G[gb][:, 0:HALF], ACT.Relu)
                    A(rel[:, m % 2, HV[1]], G[gb + 1][:, 0:HALF], ACT.Relu).then_inc(taken, 1)
                    if m:
                        hidden_hi(n - 1, m - 1)
                    if v == 0 and m == 5:
                        pre_norm(2 * l)
                hidden_hi(32 * l + 16 * v + 15, 15)

        def hidden_hi(n, m):
            sc.wait_ge(u_sq, n + 1)
            A(hH[:, m, :], rsq[:, m % 2, :], ACT.Copy).then_inc(u_hi, 1)

        boundary(0, "mlp_pre0", True)
        mlp(0)
        boundary(1, "attn_pre", False)
        for n in range(16):
            nm, dst = ("q", qT) if n < 8 else ("k", kT)
            if n == 8:
                sc.wait_ge(lm_mm, 1)
                A(misc[:, 2:4], W[3][:, 0:2], ACT.Exp).then_inc(lm_e, 1)
            if n == 5:
                pre_norm(1)
            m = n % 8
            gb = 2 * ((TILE0[nm] + m) % 2)
            sc.wait_ge(blk, BLOCK0[nm] + m + 1)
            A(dst[:, m, HV[0]], G[gb][:, 0:HALF], ACT.Copy)
            A(dst[:, m, HV[1]], G[gb + 1][:, 0:HALF], ACT.Copy).then_inc(taken, 1)

        def vtok_copy(h):
            sc.wait_ge(vt_mm, h + 1)
            A(vtok[:, :, h * P:(h + 1) * P], W[3][:, :].rearrange("p (c n) -> p c n", c=NCH), ACT.Copy
              ).then_inc(vk_s, 1)

        for b in range(NB):
            for hf in range(2):
                sc.wait_ge(qb_mm, 2 * b + hf + 1)
                if b >= 2:
                    sc.wait_ge(ss_s, PAGES * (b - 1))
                A(qb[:, b % 2, 4 * hf * P:4 * (hf + 1) * P], W[2][:, :], ACT.Copy).then_inc(qb_s, 1)
            if b:
                vtok_copy(b - 1)
        vtok_copy(AH - 1)
        def exps(n):
            w = (q_block(n)[1] + 1) * P
            sc.wait_ge(mx_s, n + 1)
            if n >= 4:
                sc.wait_ge(at_mm, n - 3)
            for j in range(2):
                A(pr[:, n % 4, j, 0:w], G[2 * (n % 2) + j][:, 0:w], ACT.Exp, scale=QK_SCALE,
                  bias=misc[:, 20 + 2 * (n % 2) + j:21 + 2 * (n % 2) + j],
                  accum_out=misc[:, 30 + 2 * (n % 2) + j:31 + 2 * (n % 2) + j]).then_inc(ex_s, 1)

        def second_map(n):
            w, c = (q_block(n)[1] + 1) * P, 34 + 2 * (n % 2)
            sc.wait_ge(cf_s, n + 1)
            A(pr[:, n % 4, 1, 0:w], pr[:, n % 4, 1, 0:w], ACT.Copy, scale=misc[:, c + 1:c + 2]).then_inc(p1_s, 1)

        def attT_copy(n):
            w = (q_block(n)[1] + 1) * P
            sc.wait_ge(at_mm, n + 1)
            if n >= 4:
                sc.wait_ge(av_mm, n - 3)
            A(attT[:, n % 4, 0:w], W[n % 2][:, 0:w], ACT.Copy).then_inc(at_s, 1)

        def head_norm(n, sums, r):
            sc.wait_ge(on_mm, n + 1)
            if n:
                sc.wait_ge(ox_s, n)
            A(r, sums, ACT.Ln, scale=1.0 / P, bias=misc[:, 8:9]).then_inc(on_rd, 1)
            sc.wait_ge(on_rd, n + 1)
            A(r, r, ACT.Exp, scale=-0.5).then_inc(or_s, 1)

        for n in range(AH * NCH + 7):
            if n < AH * NCH:
                exps(n)
            if n == 2:
                sc.wait_ge(s2_s, 1)
                A(sE[:, :], W[3][:, 0:257], ACT.Exp, scale=QK_SCALE, bias=misc[:, 41:42], accum_out=misc[:, 42:43]
                  ).then_inc(sx_s, 1)
            elif n == 4:
                sc.wait_ge(sa_mm, 1)
                A(satt[:, :, :].rearrange("p g c -> p (g c)"), W[3][:, 256:384], ACT.Copy)
                A(snb[:, :], W[3][:, 384:448], ACT.Copy).then_inc(sa_s, 1)
            if 1 <= n <= AH * NCH:
                second_map(n - 1)
            if 3 <= n < AH * NCH + 3:
                attT_copy(n - 3)
            if n >= 10 and (n - 10) % 4 == 0:
                head_norm((n - 10) // 4, W[0][:, :], orr[:, :])
        head_norm(AH, W[2][:, 0:64], orrs[:, :])
        sc.wait_ge(ox_s, AH + 1)
        for h in range(AH):
            A(aH[:, h, :], oT[:, h, :], ACT.Copy).then_inc(ohi, 1)
        sc.wait_ge(kv_out, 32)
        boundary(2, "mlp_pre1", True)
        mlp(1)
        boundary(3, None, False)

    @block.vector
    def _(v):
        own = Own(v, dve)
        TT, STT, TS = v.tensor_tensor, v.scalar_tensor_tensor, v.tensor_scalar

        own(v.memset(misc[:, 8:9], EPS))
        own(v.memset(misc[:, 9:10], 1.0))
        own(v.memset(misc[:, 60:75], 0.0))
        own(v.memset(misc[:, 67:68], 1.0))
        v.wait_ge(in_pv, 16)
        for t in range(KT):
            v.wait_ge(in_x[t // 2], 16)
            TS(fT[:, t, :], hT[:, t, :], pc("ssd_pre", t), None, ALU.mult).then_inc(hg_s, 1)
        v.wait_ge(in_par, 32)
        own(v.tensor_copy(wdh[:, :, :], wdr[:, :, :]))
        TT(wdl[:, :, :], wdr[:, :, :], wdh[:, :, :].bitcast(F32), ALU.subtract).then_inc(wd_s, 1)
        own(v.memset(xr[:, 0, 0:3], 0.0))
        v.memset(xr[:, 1, 0:3], 0.0).then_inc(xz, 1)
        v.wait_ge(hg_s, KT)
        v.wait_ge(r0, 1)

        def first_x(t):
            TT(sq8[:, t, :], fT[:, t, :], rpre[:, :], ALU.mult).then_inc(ax[0], 1)

        def first_lo(t):
            v.wait_ge(ahi, t + 1)
            TT(aL[:, t, :], sq8[:, t, :], aH[:, t, :].bitcast(F32), ALU.subtract).then_inc(alo, 1)

        first_x(0)
        for t in range(2, KT, 2):
            first_x(t)
            first_lo(t - 2)
            first_lo(t - 1)
        first_lo(KT - 2)
        first_lo(KT - 1)
        own(v.tensor_copy(slr[:, :], cc(C_SL)))
        own(v.tensor_copy(hmr[:, 64:128], cst[:, C_ONE, 0:64]))
        own(v.tensor_copy(hmr[:, 0:64], cst[:, C_MASK, 0:1].broadcast_to([P, 64])))
        own(v.tensor_copy(hmr[:, 128:192], cst[:, C_MASK, 0:1].broadcast_to([P, 64])))

        def sample_conv(a, b):
            v.wait_ge(taken, b)
            for k in range(4):
                own(TT(xsm[:, a:b, :, k], xs4[:, a:b, :, k],
                       pc("conv_w", 24 * k + a, b - a).unsqueeze(2).broadcast_to([P, b - a, NB]), ALU.mult))
            own(v.tensor_reduce(xsc[:, a:b, :], xsm[:, a:b, :, :], AXX, ALU.add))
            TT(xsc[:, a:b, :], xsc[:, a:b, :], pc("conv_b", a, b - a).unsqueeze(2).broadcast_to([P, b - a, NB]),
               ALU.add).then_inc(scv, 1)

        def x_dt(g, c):
            if g and c == 0:
                v.wait_ge(yd_mm, 8 * g)
            v.wait_ge(tr_mm, g * NCH + c + 1)
            TT(r8(xdt[:, c, :]), r8(W[c % 2][:, :]), hb(dtb, c, g), ALU.mult).then_inc(xd_s, 1)

        def masked_cb(g):
            v.wait_ge(cb_mm, g + 1)
            TT(cbm[:, :, :], W[3][:, :].rearrange("p (c l) -> p c l", c=NCH),
               cst[:, C_UP:C_UP + 1, :].broadcast_to([P, NCH, P]), ALU.mult).then_inc(cb_s, 1)
            v.wait_ge(cb_s, g + 1)

        for m in range(NCONV):
            if m == 5:
                v.wait_ge(dt_mm, 1)
                TT(dtu[:, :].rearrange("p (v t) -> p v t", v=2), WP[1][0:32, :, 0:HALF],
                   pv[0:32, PV["dt_bias"][0]:PV["dt_bias"][1]].unsqueeze(1).broadcast_to([32, 2, HALF]), ALU.add
                   ).then_inc(dt_u, 1)
            elif m == 7:
                v.wait_ge(dt_l, 1)
                STT(dts[:, :], dtu[:, :], 0.0, dtl[:, :], ALU.max, ALU.add).then_inc(dt_s, 1)
            elif m == 11:
                v.wait_ge(dt_tr, 1)
                own(v.tensor_copy(dtt[:, :], W[0][:, 0:P]))
                own(STT(adt[:, :].rearrange("p (c h) -> p c h", c=NCH), dtb, -1.0,
                        ea[:, 0:32].unsqueeze(1).broadcast_to([P, NCH, 32]), ALU.mult, ALU.mult))
                own(v.tensor_copy(adH[:, :], adt[:, :]))
                TT(adL[:, :], adt[:, :], adH[:, :].bitcast(F32), ALU.subtract).then_inc(adt_s, 1)
            elif m == 14:
                v.wait_ge(dtx_s, 1)
                STT(dex[:, 2, :].rearrange("p (q b) -> p q b", q=NPAIR), dtx[:, :, :], -1.0,
                    ea[:, 32:48].unsqueeze(2).broadcast_to([P, NPAIR, NB]), ALU.mult, ALU.mult).then_inc(sda_s, 1)
            elif m == 10:
                v.wait_ge(cs_in, 16)
                sample_conv(0, 9)
            elif m == 18:
                sample_conv(9, 17)
            elif m == 23:
                v.wait_ge(dex_s, 1)
                x_dt(0, 0)
                x_dt(0, 1)
                masked_cb(0)
            v.wait_ge(xr_in, 2 * m + 2)
            if m >= 2:
                v.wait_ge(sil, m - 1)
            a = cacc[:, m % 2, :]
            own(v.tensor_copy(pcv[:, m, :], xr[:, m % 2, SEQ:SEQ + 3]))
            own(TS(a, xr[:, m % 2, 0:SEQ], pc("conv_w", m), pc("conv_b", m), ALU.mult, ALU.add))
            for k in (1, 2, 3):
                ins = STT(a, xr[:, m % 2, k:k + SEQ], pc("conv_w", 24 * k + m), a, ALU.mult, ALU.add)
                own(ins) if k < 3 else ins.then_inc(cv, 1)
        v.wait_ge(dex_s, 1)
        def ssd_out(n):
            v.wait_ge(eb_s, n + 1)
            v.wait_ge(yo_mm, n + 1)
            own(TT(ebc[:, n % 2, P:SEQ], G[2 + n % 2][:, P:SEQ], ebc[:, n % 2, P:SEQ], ALU.mult))
            own(STT(yT[:, n, 0:SEQ], yT[:, n, 0:SEQ], pc("d", n), G[n % 2][:, :], ALU.mult, ALU.add))
            TT(yT[:, n, P:SEQ], yT[:, n, P:SEQ], ebc[:, n % 2, P:SEQ], ALU.add).then_inc(y_s, 1)

        for g in range(NG):
            if g:
                masked_cb(g)
            x_dt(g, 2)
            x_dt(g, 3)

            def decayed_cb(k):
                v.wait_ge(sg_s, k + 1)
                TT(dec[:, k % 4, :], dec[:, k % 4, :], cbm[:, :, :].rearrange("p c l -> p (c l)"), ALU.mult
                   ).then_inc(md_s, 1)

            decayed_cb(8 * g)
            if g:
                v.wait_ge(fin_out, 16 * g)
            for c in range(NCH):
                v.wait_ge(st_mm, g * NCH + c + 1)
                if c == 0:
                    v.tensor_copy(hst[:, 0, :], G[0][:, :]).then_inc(h_s, 1)
                else:
                    v.wait_ge(h_s, g * NCH + c)
                    own(TT(r8(hst[:, c, :]), r8(hst[:, c - 1, :]), hb(cdb, c, g), ALU.mult))
                    TT(hst[:, c, :], hst[:, c, :], G[c][:, :], ALU.add).then_inc(h_s, 1)
                if c < 3:
                    decayed_cb(8 * g + c + 1)
            ssd_out(4 * g)
            for n in range(4 * g + 2, 4 * g + 4):
                decayed_cb(2 * n)
                decayed_cb(2 * n + 1)
                ssd_out(n - 1)
            if g == 0:
                sample_conv(17, NCONV)
            if g + 1 < NG:
                x_dt(g + 1, 0)
                x_dt(g + 1, 1)
            ssd_out(4 * g + 3)

        v.wait_ge(pss, 1)
        TT(sdx[:, :, :], yT[:, :, SEQ:T], dtx[:, :, :], ALU.mult).then_inc(sdx_s, 1)

        for m in range(NPAIR):
            g = m // 4
            x = hs[:, m % 2, :, :]
            v.wait_ge(hs_in[m % 2], 16 * (m // 2 + 1))
            own(TT(x[:, NDEC:, :], x[:, NDEC:, :],
                   dex[:, 2, m * NB + NDEC:(m + 1) * NB].unsqueeze(2).broadcast_to([P, NB - NDEC, P]), ALU.mult))
            v.wait_ge(hx_s, m + 1)
            TT(x, x, ht[:, m % 2, :, :], ALU.add).then_inc(hs_new, 1)
            v.wait_ge(hs_new, m + 1)
            v.wait_ge(bc_s, 4 * g + 4)
            own(TT(hc[:, :, :], x, cbc[:, :, :], ALU.mult))
            v.tensor_reduce(yss[:, m, :], hc[:, :, :], AXX, ALU.add).then_inc(ys_s, 1)
            v.wait_ge(ys_s, m + 1)
            own(STT(yT[:, m, SEQ:T], yT[:, m, SEQ:T], pc("d", m), yss[:, m, :], ALU.mult, ALU.add))
            v.wait_ge(taken, TILE0["z"] + m + 1)
            TT(yT[:, m, :], yT[:, m, :], zs[:, m % 2, :], ALU.mult).then_inc(z_g, 1)
            if m:
                gate_sum(v, own, m - 1)
        gate_sum(v, own, NPAIR - 1)
        def gate_lo(q):
            v.wait_ge(g_hi, q + 1)
            STT(hL[:, q, :], yT[:, q, :], pc("gate", q), hH[:, q, :].bitcast(F32), ALU.mult, ALU.subtract
                ).then_inc(g_lo, 1)

        for q in range(0, NPAIR, 3):
            v.wait_ge(g_r, q // 4 + 1)
            TT(yT[:, q, :], yT[:, q, :], rg[:, q // 4, :], ALU.mult).then_inc(g_n[0], 1)
            for j in range(max(q - 3, 0), q):
                gate_lo(j)
        gate_lo(NPAIR - 1)

        def add_sq(m, sem_in, sem_out, base_):
            v.wait_ge(sem_in, base_ + m + 1)
            if m == 0:
                v.tensor_copy(acc[:, :], sqt[:, 0, :]).then_inc(sem_out, 1)
            else:
                v.wait_ge(sem_out, base_ + m)
                TT(acc[:, :], acc[:, :], sqt[:, m % 2, :], ALU.add).then_inc(sem_out, 1)

        def boundary(p, gpost, gpre, own_f):
            if own_f:
                for m in range(KT):
                    add_sq(m, sqf, accf, 8 * p)
            def lows(m):
                v.wait_ge(ahi, KT + 8 * p + m + 1)
                STT(aL[:, m, :], hT[:, m, :], pc(gpre, m), aH[:, m, :].bitcast(F32), ALU.mult, ALU.subtract
                    ).then_inc(alo, 1)

            for m in range(KT):
                v.wait_ge(fr_s, 8 * p + m + 1)
                STT(hT[:, m, :], fT[:, m, :], pc(gpost, m), hT[:, m, :], ALU.mult, ALU.add).then_inc(h_n, 1)
                if m and p < 3:
                    lows(m - 1)
            if p < 3:
                lows(KT - 1)
            if p == 1:
                for m in range(KT):
                    v.wait_ge(qhi, m + 1)
                    STT(hL[:, m, :], hT[:, m, :], pc("kv", m), hH[:, m, :].bitcast(F32), ALU.mult,
                        ALU.subtract).then_inc(qlo, 1)

        def pre_sum(p):
            sq = sq8 if p == 1 else sq8b
            for m in range(1, KT):
                v.wait_ge(sqh, 8 * p + m + 1)
                if m == 1:
                    v.wait_ge(ps_mm, p + 1)
                else:
                    v.wait_ge(acch, 7 * p + m - 1)
                TT(acc[:, :], sq[:, 0, :] if m == 1 else acc[:, :], sq[:, m, :], ALU.add).then_inc(acch, 1)

        def mlp(l):
            pre_sum(2 * l)

            def hidden_lo(n, m):
                v.wait_ge(u_hi, n + 1)
                TT(hL[:, m, :], rsq[:, m % 2, :], hH[:, m, :].bitcast(F32), ALU.subtract).then_inc(u_lo, 1)

            p = 1 + 2 * l
            for w, s in enumerate("ab"):
                for m in range(16):
                    n = 32 * l + 16 * w + m
                    v.wait_ge(taken, TILE0[f"up{l}{s}"] + m + 1)
                    if n >= 2:
                        v.wait_ge(u_lo, n - 1)
                    TT(rsq[:, m % 2, :], rel[:, m % 2, :], rel[:, m % 2, :], ALU.mult).then_inc(u_sq, 1)
                    v.wait_ge(u_sq, n + 1)
                    if m:
                        hidden_lo(n - 1, m - 1)
                hidden_lo(32 * l + 16 * w + 15, 15)
                name = f"down{l}{s}"
                if s == "a":
                    v.wait_ge(r_s, 2 * l + 1)
                    own(TT(r2[:, :], rpre[:, :], rpre[:, :], ALU.mult))
                for m in range(KT):
                    gb = 2 * ((TILE0[name] + m) % 2)
                    v.wait_ge(blk, BLOCK0[name] + 2 * (m + 1))
                    v.wait_ge(taken, TILE0[name] + m)
                    if s == "a":
                        own(v.tensor_copy(fT[:, m, HV[0]], G[gb][:, 0:HALF]))
                        v.tensor_copy(fT[:, m, HV[1]], G[gb + 1][:, 0:HALF]).then_inc(taken, 1)
                        v.wait_ge(taken, TILE0[name] + m + 1)
                    else:
                        own(TT(fT[:, m, HV[0]], fT[:, m, HV[0]], G[gb][:, 0:HALF], ALU.add))
                        TT(fT[:, m, HV[1]], fT[:, m, HV[1]], G[gb + 1][:, 0:HALF], ALU.add).then_inc(taken, 1)
                        v.wait_ge(taken, TILE0[name] + m + 1)
                        TT(fT[:, m, :], fT[:, m, :], r2[:, :], ALU.mult).then_inc(f_s, 1)
                        v.wait_ge(f_s, 8 * (p // 2) + m + 1)
                        if m:
                            add_sq(m - 1, sqf, accf, 8 * p)
            add_sq(KT - 1, sqf, accf, 8 * p)

        boundary(0, "ssd_post", "mlp_pre0", True)
        mlp(0)
        boundary(1, "mlp_post0", "attn_pre", False)
        pre_sum(1)
        v.memset(misc[:, 0:2], 0.0).then_inc(lm_r, 1)
        v.wait_ge(lm_r, 1)
        lam = PV["lam"][0]
        for j in range(2):
            ins = TT(misc[:, j:j + 1], pv[:, lam + 2 * j:lam + 2 * j + 1], pv[:, lam + 2 * j + 1:lam + 2 * j + 2],
                     ALU.mult)
            own(ins) if j == 0 else ins.then_inc(lm_s, 1)
        v.wait_ge(r_s, 2)
        v.wait_ge(rp_in, 16)
        for j in range(2):
            own(TT(ropt[:, j, :], ropt[:, j, :], rpre[:, :], ALU.mult))

        def rope_tile(n):
            x = (qT if n < 8 else kT)[:, n % 8, :]
            v.wait_ge(rt_mm, n + 1)
            own(TT(rt1[:, :], x, ropt[:, 0, :], ALU.mult))
            own(TT(rt2[:, :].rearrange("p (v t) -> p v t", v=2), WP[0][:, :, 0:HALF],
                   ropt[:, 1, :].rearrange("p (v t) -> p v t", v=2), ALU.mult))
            TT(x, rt1[:, :], rt2[:, :], ALU.add).then_inc(kq_s, 1)
            v.wait_ge(kq_s, n + 1)

        def page_scores(b):
            v.wait_ge(qb_s, 2 * b + 2)
            for pg in range(PAGES):
                n = PAGES * b + pg
                v.wait_ge(kp_in[n % 4], 16 * (n // 4 + 1))
                if n:
                    v.wait_ge(ss_s, n)
                own(TT(kq[:, :], ktile[:, n % 4, :, :].rearrange("p h k -> p (h k)"), qb[:, b % 2, :], ALU.mult))
                v.tensor_reduce(sT[:, pg, :].rearrange("p (h b j) -> p h b j", h=AH, b=NB)[:, :, b, :],
                                kq[:, :].rearrange("p (h j e) -> p h j e", h=AH, j=2), AXX, ALU.add).then_inc(ss_s, 1)

        for n in range(AH):
            rope_tile(n)
        for j in range(2):
            ins = TS(qz[:, :, :, j], qT[:, :, SEQ:T], pc("jsel", j), None, ALU.mult)
            own(ins) if j == 0 else ins.then_inc(qz_s, 1)
        v.wait_ge(lm_e, 1)
        own(v.memset(misc[:, 4:5], 1.0))
        own(TT(misc[:, 5:6], misc[:, 3:4], misc[:, 2:3], ALU.subtract))
        own(TS(misc[:, 5:6], misc[:, 5:6], -LAM_INIT, None, ALU.add))
        for m in range(AH):
            v.wait_ge(blk, BLOCK0["v"] + m + 1)
            v.wait_ge(taken, TILE0["v"] + m)
            TT(vT[:, m, :].rearrange("p (v t) -> p v t", v=2), GP[(TILE0["v"] + m) % 2][:, :, 0:HALF],
               rpre[:, :].rearrange("p (v t) -> p v t", v=2), ALU.mult).then_inc(taken, 1)
            rope_tile(8 + m)
            if m < AH - 1:
                page_scores(m)
        v.wait_ge(qz_s, 1)
        for j in range(2):
            TT(kz[:, :, :, j], qz[:, :, :, j], kT[:, :, SEQ:T], ALU.mult).then_inc(kz_s, 1)

        def sample_max():
            v.wait_ge(s2_mm, 1)
            own(v.tensor_reduce(misc[:, 40:41], W[3][:, 0:257], AXX, ALU.max))
            TS(misc[:, 41:42], misc[:, 40:41], -QK_SCALE, None, ALU.mult).then_inc(s2_s, 1)

        def sample_coefs():
            v.wait_ge(sx_s, 1)
            own(v.reciprocal(misc[:, 43:44], misc[:, 42:43]))
            own(STT(misc[:, 44:45], pc("rowj", 1), misc[:, 5:6], pc("rowj", 0), ALU.mult, ALU.add))
            TS(cmb[:, :], pc("pairsel", 0, 64), misc[:, 44:45], misc[:, 43:44], ALU.mult, ALU.mult).then_inc(cm_s, 1)

        def maxima(n):
            i = q_block(n)[1]
            w, g = (i + 1) * P, GP[n % 2]
            v.wait_ge(sc_mm, n + 1)
            own(TT(g[:, :, i * P:w], g[:, :, i * P:w], cst[:, C_MASK:C_MASK + 1, :].broadcast_to([P, 2, P]), ALU.add))
            own(v.tensor_reduce(misc[:, 24 + 2 * (n % 2):26 + 2 * (n % 2)], g[:, :, 0:w], AXX, ALU.max))
            TS(misc[:, 20 + 2 * (n % 2):22 + 2 * (n % 2)], misc[:, 24 + 2 * (n % 2):26 + 2 * (n % 2)], -QK_SCALE, None,
               ALU.mult).then_inc(mx_s, 1)

        def coefs(n):
            c = 34 + 2 * (n % 2)
            v.wait_ge(ex_s, 2 * n + 2)
            if n >= 2:
                v.wait_ge(att_s, n - 1)
            own(v.reciprocal(misc[:, c:c + 2], misc[:, c - 4:c - 2]))
            TT(misc[:, c:c + 2], misc[:, c:c + 2], misc[:, 4:6], ALU.mult).then_inc(cf_s, 1)

        def combine(n):
            w, c = (q_block(n)[1] + 1) * P, 34 + 2 * (n % 2)
            v.wait_ge(p1_s, n + 1)
            STT(pr[:, n % 4, 0, 0:w], pr[:, n % 4, 0, 0:w], misc[:, c:c + 1], pr[:, n % 4, 1, 0:w],
                ALU.mult, ALU.add).then_inc(att_s, 1)

        def sample_out():
            v.wait_ge(sv_mm, NB)
            for a in (0, 64):
                v.tensor_copy(vrow[a:a + NB, :], W[3][a:a + NB, :]).then_inc(vr_s, 1)
            own(TT(ov[:, :].rearrange("p (h b) -> p h b", h=AH), snb[:, :].rearrange("p (h b) -> p h b", h=AH),
                   vT[:, :, SEQ:T], ALU.mult))

        own(TS(misc[:, 46:47], pc("subln"), 1.0 - LAM_INIT, None, ALU.mult))
        def take_o(n):
            h, i = q_block(n)
            v.wait_ge(av_mm, n + 1)
            v.tensor_copy(oT[:, h, i * P:(i + 1) * P], W[2][:, 0:P]).then_inc(o_s, 1)

        for n in range(AH * NCH + 8):
            if 5 <= n < AH * NCH + 5:
                take_o(n - 5)
            if n < AH * NCH:
                maxima(n)
            if n == 1:
                page_scores(AH - 1)
            elif n == 2:
                sample_max()
            elif n == 3:
                sample_coefs()
            elif n == AH * NCH + 6:
                sample_out()
            if 1 <= n <= AH * NCH:
                coefs(n - 1)
            if 2 <= n < AH * NCH + 2:
                combine(n - 2)
            if n >= 9 and (n - 9) % 4 == 0:
                h = (n - 9) // 4
                v.wait_ge(o_s, NCH * (h + 1))
                if h:
                    v.wait_ge(on_mm, h)
                TT(osq[:, :], oT[:, h, 0:SEQ], oT[:, h, 0:SEQ], ALU.mult).then_inc(osq_s, 1)
            elif n >= 11 and (n - 11) % 4 == 0:
                h = (n - 11) // 4
                v.wait_ge(or_s, h + 1)
                STT(oT[:, h, 0:SEQ], oT[:, h, 0:SEQ], misc[:, 46:47], orr[:, :], ALU.mult, ALU.mult).then_inc(ox_s, 1)
        v.wait_ge(vr_mm, 2)
        TT(oT[:, :, SEQ:T], ov[:, :].rearrange("p (h b) -> p h b", h=AH),
           W[3][:, 0:64].rearrange("p (h b) -> p h b", h=AH), ALU.add).then_inc(os_s, 1)
        v.wait_ge(os_s, 1)
        TT(osqs[:, :].rearrange("p (h b) -> p h b", h=AH), oT[:, :, SEQ:T], oT[:, :, SEQ:T], ALU.mult
           ).then_inc(osq_s, 1)
        v.wait_ge(or_s, AH + 1)
        STT(oT[:, :, SEQ:T], oT[:, :, SEQ:T], misc[:, 46:47], orrs[:, :].rearrange("p (h b) -> p h b", h=AH),
            ALU.mult, ALU.mult).then_inc(ox_s, 1)
        for h in range(AH):
            v.wait_ge(ohi, h + 1)
            TT(aL[:, h, :], oT[:, h, :], aH[:, h, :].bitcast(F32), ALU.subtract).then_inc(olo, 1)
        boundary(2, "attn_post", "mlp_pre1", True)
        mlp(1)
        boundary(3, "mlp_post1", None, False)

    ctx.close()


def kernel(**inputs):
    import numpy as np
    import concourse.bacc as bacc
    from concourse.bass_utils import run_bass_kernel_spmd

    f = {k: np.asarray(v) for k, v in inputs.items()}

    def blocks(w):
        k, n = w.shape
        return w.reshape(k // 1024, 8, P, n // P, P).transpose(3, 0, 2, 1, 4).reshape(-1, P, 1024)

    w_in = f["ssd_w_in"][0]
    xbc0 = 2048
    order = [w_in[:, xbc0 + 2048:xbc0 + 3072], w_in[:, xbc0:xbc0 + 2048], w_in[:, 0:2048], f["ssd_w_out"][0]]

    def mlp(l):
        up, down = f["mlp_w_up"][l], f["mlp_w_down"][l]
        return [up[:, :2048], down[:2048], up[:, 2048:], down[2048:]]

    order += mlp(0) + [f["attn_w_q"][0], f["w_kv"][:, :1024], f["w_kv"][:, 1024:], f["attn_w_o"][0]] + mlp(1)
    wblk = np.concatenate([blocks(w) for w in order])
    wdt = w_in[:, 5120:].reshape(8, P, 32).transpose(1, 0, 2)
    x_t = np.concatenate([f["x_prompt"][0], f["x_sample"][:, 0]]).reshape(T, KT, P).transpose(2, 1, 0)

    def cols(v):
        return v.reshape(-1, P).T

    def conv_order(a):
        return np.concatenate([a[16:24], a[0:16]])

    z = np.float32
    jsel = np.zeros((P, 2), z)
    jsel[:64, 0] = 1
    jsel[64:, 1] = 1
    rowj = np.zeros((P, 2), z)
    rowj[0::2, 0] = 1
    rowj[1::2, 1] = 1
    pairsel = np.kron(np.eye(64, dtype=z), np.ones((2, 1), z))
    lam = np.zeros((P, 4), z)
    for i, n in enumerate(("q1", "k1", "q2", "k2")):
        lam[:64, i] = f["attn_lambda_" + n][0]
    cw = np.concatenate([conv_order(f["ssd_conv_w"][0, k].reshape(24, P)).T for k in range(4)], 1)
    parts = {"ssd_pre": cols(f["ssd_norm_pre"][0]), "ssd_post": cols(f["ssd_norm_post"][0]), "conv_w": cw,
             "conv_b": conv_order(f["ssd_conv_b"][0].reshape(24, P)).T, "gate": cols(f["ssd_gate_norm"][0]),
             "mlp_pre0": cols(f["mlp_norm_pre"][0]), "mlp_pre1": cols(f["mlp_norm_pre"][1]),
             "mlp_post0": cols(f["mlp_norm_post"][0]), "mlp_post1": cols(f["mlp_norm_post"][1]),
             "kv": cols(f["kv_norm"]), "attn_pre": cols(f["attn_norm_pre"][0]), "attn_post": cols(f["attn_norm_post"][0]),
             "subln": cols(f["attn_subln"][0]), "d": cols(np.repeat(f["ssd_d"][0], 64)), "jsel": jsel,
             "pairsel": pairsel, "rowj": rowj, "lam": lam,
             "dt_bias": np.pad(f["ssd_dt_bias"][0], (0, P - NH_SSD))[:, None],
             "a_log": np.broadcast_to(f["ssd_a_log"][0], (P, 32)), "a_col": cols(np.repeat(f["ssd_a_log"][0], 64))}
    pvec = np.concatenate([parts[n] for n in PV], 1)
    up = np.triu(np.ones((P, P), z))
    perm = np.zeros((P, P), z)
    for h in (0, 64):
        for i in range(8):
            perm[h + 8 + i, h + i] = -1
            perm[h + i, h + 8 + i] = 1
    consts = np.stack([np.eye(P, dtype=z), np.ones((P, P), z), up, np.tril(np.ones((P, P), z), -1),
                       np.triu(np.full((P, P), -3e38, z), 1), perm], 1)
    pos = np.concatenate([np.arange(SEQ), np.full(NB, 256)]).astype(z)
    inv = (z(500000.0) ** (-np.arange(0, 16, 2, dtype=z) / z(16))).astype(z)
    ang = inv[:, None] * pos[None, :]
    rope = np.zeros((P, 2, T), z)
    rope[:, 0] = 1
    for h in (0, 8, 64, 72):
        rope[h:h + 8, 0] = np.cos(ang)
        rope[h:h + 8, 1] = np.sin(ang)
    ssm_in = f["state_ssm"][0].reshape(NB, NPAIR, P, P).transpose(1, 2, 0, 3)
    conv_in = conv_order(f["state_conv"][0].reshape(NB, 3, 24, P).transpose(2, 3, 0, 1)).transpose(1, 0, 2, 3)
    npg = f["cache_k"].shape[0]
    kcache = f["cache_k"].reshape(npg, P, 1024)
    vcache = f["cache_v"].reshape(npg, P, 1024)
    ins = {"wblk": wblk, "wdt": wdt, "x_t": x_t, "pvec": pvec, "consts": consts, "rope": rope, "ssm_in": ssm_in,
           "conv_in": conv_in, "kcache": kcache, "vcache": vcache, "ptab": f["page_table"].reshape(1, -1)}
    outs = {"y_t": (P, KT, T), "pssm": (P, NG, 512), "pconv": (P, NCONV, 3), "kt_out": (P, AH, T), "vt_out": (P, AH, T),
            "sssm": (NPAIR, P, NB, P), "sconv": (P, NCONV, NB, 3)}
    nc = bacc.Bacc("TRN2", target_bir_lowering=False, num_devices=1)
    ins = {k: np.ascontiguousarray(a) for k, a in ins.items()}
    args = [nc.dram_tensor(k, a.shape, mybir.dt.from_np(a.dtype), kind="ExternalInput").ap() for k, a in ins.items()]
    args += [nc.dram_tensor(k, sh, F32, kind="ExternalOutput").ap() for k, sh in outs.items()]
    build(nc, *args)
    o = run_bass_kernel_spmd(nc, [ins], core_ids=[0]).results[0]

    def tokens(a):
        a = a.transpose(2, 1, 0)
        return a[:SEQ].reshape(1, SEQ, -1), a[SEQ:].reshape(NB, 1, -1)

    def unconv(a):
        return np.concatenate([a[8:24], a[0:8]])

    y_p, y_s = tokens(o["y_t"])
    k_p, k_s = (a.reshape(*a.shape[:2], AH, P) for a in tokens(o["kt_out"]))
    v_p, v_s = (a.reshape(*a.shape[:2], AH, P) for a in tokens(o["vt_out"]))
    p_ssm = o["pssm"].reshape(P, NH_SSD, 64).transpose(1, 2, 0)[None, None]
    p_conv = unconv(o["pconv"].transpose(1, 0, 2)).reshape(3072, 3).T[None, None]
    s_ssm = o["sssm"].transpose(2, 0, 1, 3).reshape(1, NB, NH_SSD, 64, P)
    s_conv = unconv(o["sconv"].transpose(1, 0, 2, 3)).reshape(3072, NB, 3).transpose(1, 2, 0)[None]
    return tuple(np.ascontiguousarray(a) for a in (y_p, y_s, p_ssm, p_conv, k_p, v_p, s_ssm, s_conv, k_s, v_s))
```
